# Optimizing a Trainium2 kernel written in Bass

```python
import math
import jax, jax.numpy as jnp
from jax import lax
import numpy as np

D_MODEL = 1024
BATCH = 1
SEQ = 256
DEPTH = 1

LA_HEADS = 4
LA_DK = 128
LA_DV = 128
LA_QK = LA_HEADS * LA_DK
LA_V = LA_HEADS * LA_DV
CONV_K = 4
CHUNK = 64
DIFF_HEADS = 4
DIFF_DH = 64
DIFF_DV = 2 * DIFF_DH
DIFF_QK = DIFF_HEADS * 2 * DIFF_DH
DIFF_V = DIFF_HEADS * DIFF_DV
Q_BLOCK = 128
NUM_BUCKETS = 32
MAX_DISTANCE = 128
D_MIX = LA_V + DIFF_V
SPLIT_SIZES = [3 * LA_QK if False else 2 * LA_QK + LA_V, LA_V, LA_HEADS, LA_HEADS, DIFF_QK, DIFF_QK, DIFF_V]
SPLIT_IDX = [int(s) for s in np.cumsum(SPLIT_SIZES)[:-1]]
IN_DIM = int(sum(SPLIT_SIZES))
LA_CONV_DIM = 2 * LA_QK + LA_V
D_FF = -(-(8 * D_MODEL // 3) // 256) * 256
NORM_EPS = 1e-6


def rmsnorm(x, w, eps=NORM_EPS):
    xf = x.astype(jnp.float32)
    y = xf * lax.rsqrt(jnp.mean(xf * xf, axis=-1, keepdims=True) + eps) * w.astype(jnp.float32)
    return y.astype(x.dtype)

def l2norm(x, eps=1e-6):
    return x * lax.rsqrt(jnp.sum(x * x, axis=-1, keepdims=True) + eps)

def causal_conv(x, w):
    T = x.shape[1]
    K = w.shape[0]
    xp = jnp.pad(x, ((0, 0), (K - 1, 0), (0, 0)))
    out = xp[:, 0:T] * w[0]
    for i in range(1, K):
        out = out + xp[:, i:i + T] * w[i]
    return out

def gated_delta_rule(q, k, v, g, beta):
    f32 = jnp.float32
    B, T, H, Dk = q.shape
    Dv = v.shape[-1]
    n = T // CHUNK
    q = l2norm(q.astype(f32)) * (Dk ** -0.5)
    k = l2norm(k.astype(f32))
    v = v.astype(f32)

    def chunk(t):
        return t.reshape(B, n, CHUNK, H, -1).transpose(1, 0, 3, 2, 4)

    q, k, v = chunk(q), chunk(k), chunk(v)
    beta = beta.astype(f32).reshape(B, n, CHUNK, H).transpose(1, 0, 3, 2)
    g = jnp.cumsum(g.astype(f32).reshape(B, n, CHUNK, H).transpose(1, 0, 3, 2), axis=-1)

    causal = jnp.tril(jnp.ones((CHUNK, CHUNK), dtype=bool))
    strict = jnp.tril(jnp.ones((CHUNK, CHUNK), dtype=bool), k=-1)
    gdiff = g[..., :, None] - g[..., None, :]
    decay = jnp.where(causal, jnp.exp(jnp.where(causal, gdiff, 0.0)), 0.0)

    k_beta = k * beta[..., None]
    L = jnp.where(strict, jnp.einsum('nbhcd,nbhsd->nbhcs', k_beta, k) * decay, 0.0)
    A = L + jnp.eye(CHUNK, dtype=f32)
    rhs = jnp.concatenate([v * beta[..., None], k_beta * jnp.exp(g)[..., None]], axis=-1)
    sol = lax.linalg.triangular_solve(A, rhs, left_side=True, lower=True, unit_diagonal=True)
    u, w = sol[..., :Dv], sol[..., Dv:]
    intra = jnp.where(causal, jnp.einsum('nbhcd,nbhsd->nbhcs', q, k) * decay, 0.0)

    def step(S, inp):
        q_i, k_i, u_i, w_i, g_i, a_i = inp
        v_new = u_i - jnp.einsum('bhcd,bhde->bhce', w_i, S)
        o = (jnp.einsum('bhcd,bhde->bhce', q_i * jnp.exp(g_i)[..., None], S)
             + jnp.einsum('bhcs,bhse->bhce', a_i, v_new))
        g_last = g_i[..., -1]
        S = (S * jnp.exp(g_last)[..., None, None]
             + jnp.einsum('bhcd,bhce->bhde', k_i * jnp.exp(g_last[..., None] - g_i)[..., None], v_new))
        return S, o

    S0 = jnp.zeros((B, H, Dk, Dv), dtype=f32)
    _, o = lax.scan(step, S0, (q, k, u, w, g, intra))
    return o.transpose(1, 0, 3, 2, 4).reshape(B, T, H, Dv)

def t5_bucket(rel):
    n = jnp.maximum(rel, 0)
    max_exact = NUM_BUCKETS // 2
    nf = jnp.maximum(n, 1).astype(jnp.float32)
    large = max_exact + (jnp.log(nf / max_exact) / math.log(MAX_DISTANCE / max_exact)
                         * (NUM_BUCKETS - max_exact)).astype(jnp.int32)
    large = jnp.minimum(large, NUM_BUCKETS - 1)
    return jnp.where(n < max_exact, n, large)

def diff_attention(q, k, v, lam, rel_bias):
    B, T, H, _, dh = q.shape
    nb = T // Q_BLOCK
    q = q * (dh ** -0.5)
    qb = q.reshape(B, nb, Q_BLOCK, H, 2, dh).transpose(1, 0, 2, 3, 4, 5)
    kpos = jnp.arange(T)

    def block(args):
        q_blk, i = args
        qpos = i * Q_BLOCK + jnp.arange(Q_BLOCK)
        rel = qpos[:, None] - kpos[None, :]
        bias = rel_bias[t5_bucket(rel)].astype(jnp.float32)
        s = jnp.einsum('bqhmd,bkhmd->bhmqk', q_blk, k).astype(jnp.float32)
        s = s + bias.transpose(2, 0, 1)[None, :, None]
        s = jnp.where(rel >= 0, s, -jnp.inf)
        p = jax.nn.softmax(s, axis=-1)
        p = p[:, :, 0] - lam * p[:, :, 1]
        return jnp.einsum('bhqk,bkhe->bqhe', p.astype(v.dtype), v)

    o = lax.map(block, (qb, jnp.arange(nb)))
    return o.transpose(1, 0, 2, 3, 4).reshape(B, T, H, 2 * dh)

def first_inputs(seed: int = 0) -> dict:
    key = jax.random.key(seed)
    ks = jax.random.split(key, 20)
    f32 = jnp.float32
    nrm = lambda k, s, sc: jax.random.normal(k, s, f32) * sc
    x = jax.random.normal(ks[0], (BATCH, SEQ, D_MODEL), f32)
    attn_norm_w = 1.0 + nrm(ks[1], (DEPTH, D_MODEL), 0.1)
    w_in = nrm(ks[2], (DEPTH, D_MODEL, IN_DIM), D_MODEL ** -0.5)
    conv_w = nrm(ks[3], (DEPTH, CONV_K, LA_CONV_DIM), CONV_K ** -0.5)
    a_log = jnp.log(jax.random.uniform(ks[4], (DEPTH, LA_HEADS), f32, 1.0, 16.0))
    dt = jnp.exp(jax.random.uniform(ks[5], (DEPTH, LA_HEADS), f32, math.log(1e-3), math.log(1e-1)))
    dt_bias = jnp.log(jnp.expm1(dt))
    la_norm_w = 1.0 + nrm(ks[6], (DEPTH, LA_DV), 0.1)
    lambda_q1 = nrm(ks[7], (DEPTH, DIFF_DH), 0.1)
    lambda_k1 = nrm(ks[8], (DEPTH, DIFF_DH), 0.1)
    lambda_q2 = nrm(ks[9], (DEPTH, DIFF_DH), 0.1)
    lambda_k2 = nrm(ks[10], (DEPTH, DIFF_DH), 0.1)
    diff_norm_w = 1.0 + nrm(ks[11], (DEPTH, DIFF_DV), 0.1)
    rel_bias = nrm(ks[12], (NUM_BUCKETS, DIFF_HEADS), 0.5)
    w_out = nrm(ks[13], (DEPTH, D_MIX, D_MODEL), D_MIX ** -0.5)
    ffn_norm_w = 1.0 + nrm(ks[14], (DEPTH, D_MODEL), 0.1)
    w_gate_up = nrm(ks[15], (DEPTH, D_MODEL, 2 * D_FF), D_MODEL ** -0.5)
    w_down = nrm(ks[16], (DEPTH, D_FF, D_MODEL), D_FF ** -0.5)
    final_norm_w = 1.0 + nrm(ks[17], (D_MODEL,), 0.1)
    return {"x": x, "attn_norm_w": attn_norm_w, "w_in": w_in, "conv_w": conv_w,
            "a_log": a_log, "dt_bias": dt_bias, "la_norm_w": la_norm_w,
            "lambda_q1": lambda_q1, "lambda_k1": lambda_k1, "lambda_q2": lambda_q2,
            "lambda_k2": lambda_k2, "diff_norm_w": diff_norm_w, "rel_bias": rel_bias,
            "w_out": w_out, "ffn_norm_w": ffn_norm_w, "w_gate_up": w_gate_up,
            "w_down": w_down, "final_norm_w": final_norm_w}

def first_block(x, attn_norm_w, w_in, conv_w, a_log, dt_bias, la_norm_w, lambda_q1, lambda_k1,
              lambda_q2, lambda_k2, diff_norm_w, rel_bias, w_out, ffn_norm_w, w_gate_up,
              w_down, final_norm_w):
    f32 = jnp.float32
    B, T, _ = x.shape
    for l in range(DEPTH):
        h = rmsnorm(x, attn_norm_w[l])
        proj = h @ w_in[l]
        qkv_la, z_la, b_la, a_la, q_d, k_d, v_d = jnp.split(proj, SPLIT_IDX, axis=-1)

        qkv_la = jax.nn.silu(causal_conv(qkv_la, conv_w[l]))
        q_la, k_la, v_la = jnp.split(qkv_la, [LA_QK, 2 * LA_QK], axis=-1)
        q_la = q_la.reshape(B, T, LA_HEADS, LA_DK)
        k_la = k_la.reshape(B, T, LA_HEADS, LA_DK)
        v_la = v_la.reshape(B, T, LA_HEADS, LA_DV)
        beta = jax.nn.sigmoid(b_la.astype(f32))
        g = -jnp.exp(a_log[l].astype(f32)) * jax.nn.softplus(a_la.astype(f32) + dt_bias[l].astype(f32))
        o_la = gated_delta_rule(q_la, k_la, v_la, g, beta).astype(x.dtype)
        o_la = rmsnorm(o_la, la_norm_w[l]) * jax.nn.silu(z_la.reshape(B, T, LA_HEADS, LA_DV))
        o_la = o_la.reshape(B, T, LA_V)

        lam_init = 0.8 - 0.6 * math.exp(-0.3 * l)
        lam = (jnp.exp(jnp.sum(lambda_q1[l].astype(f32) * lambda_k1[l].astype(f32)))
               - jnp.exp(jnp.sum(lambda_q2[l].astype(f32) * lambda_k2[l].astype(f32))) + lam_init)
        o_d = diff_attention(q_d.reshape(B, T, DIFF_HEADS, 2, DIFF_DH),
                             k_d.reshape(B, T, DIFF_HEADS, 2, DIFF_DH),
                             v_d.reshape(B, T, DIFF_HEADS, DIFF_DV), lam, rel_bias)
        o_d = rmsnorm(o_d, diff_norm_w[l], eps=1e-5) * (1.0 - lam_init)
        o_d = o_d.reshape(B, T, DIFF_V)

        x = x + jnp.concatenate([o_la, o_d], axis=-1) @ w_out[l]

        h = rmsnorm(x, ffn_norm_w[l])
        gate, up = jnp.split(h @ w_gate_up[l], 2, axis=-1)
        x = x + (jax.nn.silu(gate) * up) @ w_down[l]
    return rmsnorm(x, final_norm_w)


GLA_HEADS = 4
GLA_DK = 64
GLA_DV = 128
GLA_LOWRANK = 16
GLA_TAU = 16.0
GLA_CHUNK = 64
MOBA_HEADS = 8
MOBA_DH = 64
MOBA_BLOCK = 256
MOBA_TOPK = 3
MOBA_QCHUNK = 128
REL_BUCKETS = 32
REL_MAX_DIST = 128
MEM_LEN = 256
MEM_HEADS = 4
MEM_DH = 128
N_GROUPS = 4
EXPERTS_PER_GROUP = 8
N_EXPERTS = N_GROUPS * EXPERTS_PER_GROUP
TOPK_IN_GROUP = 2
D_EXPERT = 512
MOE_BLOCK = 128
EPS = 1e-6

GLA_QK = GLA_HEADS * GLA_DK
GLA_V = GLA_HEADS * GLA_DV
MOBA_W = MOBA_HEADS * MOBA_DH
MEM_W = MEM_HEADS * MEM_DH
IN_SPLITS = (GLA_QK, GLA_QK, GLA_V, GLA_V, GLA_LOWRANK, MOBA_W, MOBA_W, MOBA_W, D_MODEL, D_MODEL)
D_IN = sum(IN_SPLITS)
SPLIT_POINTS = tuple(sum(IN_SPLITS[:i + 1]) for i in range(len(IN_SPLITS) - 1))


def rmsnorm_2(x, g):
    xf = x.astype(jnp.float32)
    y = xf * lax.rsqrt(jnp.mean(xf * xf, axis=-1, keepdims=True) + EPS)
    return (y * g.astype(jnp.float32)).astype(x.dtype)

def gla_chunked(q, k, v, log_a):
    B, S = q.shape[0], q.shape[1]
    C = GLA_CHUNK
    N = S // C

    def chunks(t):
        return t.astype(jnp.float32).reshape(B, N, C, GLA_HEADS, t.shape[-1]).transpose(0, 3, 1, 2, 4)

    q, k, v, log_a = chunks(q) * (GLA_DK ** -0.5), chunks(k), chunks(v), chunks(log_a)
    b = jnp.cumsum(log_a, axis=3)
    b_last = b[:, :, :, C - 1:]
    b_mid = b[:, :, :, C // 2 - 1:C // 2]
    att = jnp.einsum('bhncd,bhnsd->bhncs', q * jnp.exp(b - b_mid), k * jnp.exp(b_mid - b))
    causal = jnp.tril(jnp.ones((C, C), dtype=bool))
    att = jnp.where(causal, att, 0.0)
    o_intra = jnp.einsum('bhncs,bhnsv->bhncv', att, v)
    kv = jnp.einsum('bhncd,bhncv->bhndv', k * jnp.exp(b_last - b), v)
    decay = jnp.exp(b_last[:, :, :, 0])

    def step(state, inp):
        dec, kv_c = inp
        return dec[..., None] * state + kv_c, state

    init = jnp.zeros((B, GLA_HEADS, GLA_DK, GLA_DV), jnp.float32)
    _, states = lax.scan(step, init, (jnp.moveaxis(decay, 2, 0), jnp.moveaxis(kv, 2, 0)))
    states = jnp.moveaxis(states, 0, 2)
    o_inter = jnp.einsum('bhncd,bhndv->bhncv', q * jnp.exp(b), states)
    o = o_intra + o_inter
    return o.transpose(0, 2, 3, 1, 4).reshape(B, S, GLA_HEADS, GLA_DV)

def t5_bucket_2(dist):
    n = jnp.maximum(dist, 0)
    max_exact = REL_BUCKETS // 2
    nf = jnp.maximum(n, 1).astype(jnp.float32)
    large = max_exact + (jnp.log(nf / max_exact) / math.log(REL_MAX_DIST / max_exact)
                         * (REL_BUCKETS - max_exact)).astype(jnp.int32)
    large = jnp.minimum(large, REL_BUCKETS - 1)
    return jnp.where(n < max_exact, n, large)

def moba_attention(q, k, v, rel_bias):
    B, S = q.shape[0], q.shape[1]
    H, BS, QC = MOBA_HEADS, MOBA_BLOCK, MOBA_QCHUNK
    Sp = -(-S // BS) * BS
    NB = Sp // BS
    NC = Sp // QC
    K = min(MOBA_TOPK, NB)

    def heads(t):
        t = t.reshape(B, S, H, MOBA_DH).transpose(0, 2, 1, 3)
        return jnp.pad(t, ((0, 0), (0, 0), (0, Sp - S), (0, 0)))

    q = heads(q) * (MOBA_DH ** -0.5)
    kb = heads(k).reshape(B, H, NB, BS, MOBA_DH)
    vb = heads(v).reshape(B, H, NB, BS, MOBA_DH)
    k_mean = jnp.mean(kb.astype(jnp.float32), axis=3)
    gate = jnp.einsum('bhsd,bhnd->bhsn', q.astype(jnp.float32), k_mean)
    q_blk = jnp.arange(Sp) // BS
    fully_past = jnp.arange(NB)[None, :] < q_blk[:, None]
    gate = jnp.where(fully_past, gate, -jnp.inf)
    _, sel = lax.top_k(gate, K)
    sel_valid = sel < q_blk[:, None]

    def to_chunks(t):
        return jnp.moveaxis(t.reshape(B, H, NC, QC, t.shape[-1]), 2, 0)

    bias_hb = rel_bias.T.astype(jnp.float32)
    b_idx = jnp.arange(B)[:, None, None, None]
    h_idx = jnp.arange(H)[None, :, None, None]
    offs = jnp.arange(BS)

    def one_chunk(args):
        c, qc, selc, validc = args
        q_pos = c * QC + jnp.arange(QC)
        own = (c * QC) // BS
        k_own = lax.dynamic_index_in_dim(kb, own, axis=2, keepdims=False)
        v_own = lax.dynamic_index_in_dim(vb, own, axis=2, keepdims=False)
        d_own = q_pos[:, None] - (own * BS + offs)[None, :]
        s_own = jnp.einsum('bhqd,bhkd->bhqk', qc, k_own).astype(jnp.float32) + bias_hb[:, t5_bucket_2(d_own)]
        s_own = jnp.where(d_own >= 0, s_own, -jnp.inf)
        k_sel = kb[b_idx, h_idx, selc]
        v_sel = vb[b_idx, h_idx, selc]
        d_sel = q_pos[:, None, None] - (selc[..., None] * BS + offs)
        s_sel = (jnp.einsum('bhqd,bhqjkd->bhqjk', qc, k_sel).astype(jnp.float32)
                 + bias_hb[h_idx[..., None], t5_bucket_2(d_sel)])
        s_sel = jnp.where(validc[..., None], s_sel, -jnp.inf)
        logits = jnp.concatenate([s_own, s_sel.reshape(B, H, QC, K * BS)], axis=-1)
        p = jax.nn.softmax(logits, axis=-1)
        p_own = p[..., :BS].astype(v_own.dtype)
        p_sel = p[..., BS:].reshape(B, H, QC, K, BS).astype(v_sel.dtype)
        return (jnp.einsum('bhqk,bhkd->bhqd', p_own, v_own)
                + jnp.einsum('bhqjk,bhqjkd->bhqd', p_sel, v_sel))

    out = lax.map(one_chunk, (jnp.arange(NC), to_chunks(q), to_chunks(sel), to_chunks(sel_valid)))
    out = out.transpose(1, 0, 3, 2, 4).reshape(B, Sp, H * MOBA_DH)
    return out[:, :S]

def mixer(h, rel_bias, w_in, w_alpha_up, b_alpha, g_gla_head, w_proj_gla, w_proj_moba, w_out):
    B, S, _ = h.shape
    proj = h @ w_in
    q_g, k_g, v_g, r_g, a_lr, q_m, k_m, v_m, z_g, z_m = jnp.split(proj, SPLIT_POINTS, axis=-1)
    log_a = jax.nn.log_sigmoid((a_lr @ w_alpha_up + b_alpha).astype(jnp.float32)) / GLA_TAU
    o_g = gla_chunked(q_g.reshape(B, S, GLA_HEADS, GLA_DK), k_g.reshape(B, S, GLA_HEADS, GLA_DK),
                      v_g.reshape(B, S, GLA_HEADS, GLA_DV), log_a.reshape(B, S, GLA_HEADS, GLA_DK))
    o_g = rmsnorm_2(o_g, g_gla_head).reshape(B, S, GLA_V).astype(h.dtype) * jax.nn.silu(r_g)
    o_m = moba_attention(q_m, k_m, v_m, rel_bias)
    merged = jax.nn.sigmoid(z_g) * (o_g @ w_proj_gla) + jax.nn.sigmoid(z_m) * (o_m @ w_proj_moba)
    return merged @ w_out

def memory_attention(h, mem_n, w_cq, w_ckv, w_co):
    B, S, _ = h.shape
    M = mem_n.shape[1]
    q = (h @ w_cq).reshape(B, S, MEM_HEADS, MEM_DH)
    k, v = jnp.split((mem_n @ w_ckv).reshape(B, M, 2, MEM_HEADS, MEM_DH), 2, axis=2)
    k, v = k[:, :, 0], v[:, :, 0]
    s = jnp.einsum('bqhd,bkhd->bhqk', q, k).astype(jnp.float32) * (MEM_DH ** -0.5)
    p = jax.nn.softmax(s, axis=-1).astype(v.dtype)
    o = jnp.einsum('bhqk,bkhd->bqhd', p, v).reshape(B, S, MEM_W)
    return o @ w_co

def hier_moe(h, w_rg, b_rg, w_re, b_re, w_gate, w_up, w_down):
    B, S, D = h.shape
    T = B * S
    xt = h.reshape(T, D)
    g_prob = jax.nn.softmax((xt @ w_rg).astype(jnp.float32) + b_rg, axis=-1)
    p_grp, grp = lax.top_k(g_prob, 1)
    e_logits = ((xt @ w_re).astype(jnp.float32) + b_re).reshape(T, N_GROUPS, EXPERTS_PER_GROUP)
    e_in = jnp.take_along_axis(e_logits, grp[:, :, None], axis=1)[:, 0]
    top_p, top_i = lax.top_k(jax.nn.softmax(e_in, axis=-1), TOPK_IN_GROUP)
    weights = p_grp * top_p / jnp.sum(top_p, axis=-1, keepdims=True)
    expert = grp * EXPERTS_PER_GROUP + top_i
    A = T * TOPK_IN_GROUP
    flat_e = expert.reshape(A)
    flat_t = jnp.repeat(jnp.arange(T, dtype=jnp.int32), TOPK_IN_GROUP)
    flat_w = weights.reshape(A)
    order = jnp.argsort(flat_e)
    se = flat_e[order]
    counts = jnp.zeros((N_EXPERTS,), jnp.int32).at[flat_e].add(1)
    padded = (counts + MOE_BLOCK - 1) // MOE_BLOCK * MOE_BLOCK
    start = jnp.cumsum(counts) - counts
    pend = jnp.cumsum(padded)
    pstart = pend - padded
    dest = pstart[se] + (jnp.arange(A) - start[se])
    cap = (A + N_EXPERTS * (MOE_BLOCK - 1) + MOE_BLOCK - 1) // MOE_BLOCK * MOE_BLOCK
    n_blk = cap // MOE_BLOCK
    buf_t = jnp.zeros((cap,), jnp.int32).at[dest].set(flat_t[order])
    buf_w = jnp.zeros((cap,), jnp.float32).at[dest].set(flat_w[order])
    blk_e = jnp.minimum(jnp.searchsorted(pend, jnp.arange(n_blk) * MOE_BLOCK, side='right'), N_EXPERTS - 1)

    def run_block(args):
        e, tok, w = args
        xb = xt[tok]
        hid = jax.nn.silu(xb @ w_gate[e]) * (xb @ w_up[e])
        return (hid @ w_down[e]) * w[:, None].astype(xb.dtype)

    yb = lax.map(run_block, (blk_e, buf_t.reshape(n_blk, MOE_BLOCK), buf_w.reshape(n_blk, MOE_BLOCK)))
    out = jnp.zeros((T, D), h.dtype).at[buf_t].add(yb.reshape(cap, D).astype(h.dtype))
    return out.reshape(B, S, D)

def second_inputs(seed: int = 0) -> dict:
    key = jax.random.key(seed)
    ks = jax.random.split(key, 26)
    f32 = jnp.float32
    L = DEPTH

    def nrm(k, shape, scale):
        return jax.random.normal(k, shape, f32) * scale

    def gain(k, shape):
        return 1.0 + 0.02 * jax.random.normal(k, shape, f32)

    return {
        'x': nrm(ks[0], (BATCH, SEQ, D_MODEL), 1.0),
        'mem': nrm(ks[1], (BATCH, MEM_LEN, D_MODEL), 1.0),
        'g_mem': gain(ks[2], (D_MODEL,)),
        'rel_bias': nrm(ks[3], (REL_BUCKETS, MOBA_HEADS), 0.5),
        'g_mix': gain(ks[4], (L, D_MODEL)),
        'w_in': nrm(ks[5], (L, D_MODEL, D_IN), D_MODEL ** -0.5),
        'w_alpha_up': nrm(ks[6], (L, GLA_LOWRANK, GLA_QK), GLA_LOWRANK ** -0.5),
        'b_alpha': nrm(ks[7], (L, GLA_QK), 0.1),
        'g_gla_head': gain(ks[8], (L, GLA_HEADS, GLA_DV)),
        'w_proj_gla': nrm(ks[9], (L, GLA_V, D_MODEL), GLA_V ** -0.5),
        'w_proj_moba': nrm(ks[10], (L, MOBA_W, D_MODEL), MOBA_W ** -0.5),
        'w_out': nrm(ks[11], (L, D_MODEL, D_MODEL), D_MODEL ** -0.5),
        'g_cross': gain(ks[12], (L, D_MODEL)),
        'w_cq': nrm(ks[13], (L, D_MODEL, MEM_W), D_MODEL ** -0.5),
        'w_ckv': nrm(ks[14], (L, D_MODEL, 2 * MEM_W), D_MODEL ** -0.5),
        'w_co': nrm(ks[15], (L, MEM_W, D_MODEL), MEM_W ** -0.5),
        'g_moe': gain(ks[16], (L, D_MODEL)),
        'w_router_group': nrm(ks[17], (L, D_MODEL, N_GROUPS), D_MODEL ** -0.5),
        'b_router_group': nrm(ks[18], (L, N_GROUPS), 0.01),
        'w_router_expert': nrm(ks[19], (L, D_MODEL, N_EXPERTS), D_MODEL ** -0.5),
        'b_router_expert': nrm(ks[20], (L, N_EXPERTS), 0.01),
        'w_exp_gate': nrm(ks[21], (L, N_EXPERTS, D_MODEL, D_EXPERT), D_MODEL ** -0.5),
        'w_exp_up': nrm(ks[22], (L, N_EXPERTS, D_MODEL, D_EXPERT), D_MODEL ** -0.5),
        'w_exp_down': nrm(ks[23], (L, N_EXPERTS, D_EXPERT, D_MODEL), D_EXPERT ** -0.5),
        'g_final': gain(ks[24], (D_MODEL,)),
    }

def second_block(x, mem, g_mem, rel_bias, g_mix, w_in, w_alpha_up, b_alpha, g_gla_head, w_proj_gla,
              w_proj_moba, w_out, g_cross, w_cq, w_ckv, w_co, g_moe, w_router_group, b_router_group,
              w_router_expert, b_router_expert, w_exp_gate, w_exp_up, w_exp_down, g_final):
    mem_n = rmsnorm_2(mem, g_mem)
    for l in range(DEPTH):
        x = x + mixer(rmsnorm_2(x, g_mix[l]), rel_bias, w_in[l], w_alpha_up[l], b_alpha[l], g_gla_head[l],
                      w_proj_gla[l], w_proj_moba[l], w_out[l])
        x = x + memory_attention(rmsnorm_2(x, g_cross[l]), mem_n, w_cq[l], w_ckv[l], w_co[l])
        x = x + hier_moe(rmsnorm_2(x, g_moe[l]), w_router_group[l], b_router_group[l], w_router_expert[l],
                         b_router_expert[l], w_exp_gate[l], w_exp_up[l], w_exp_down[l])
    return rmsnorm_2(x, g_final)


def setup_inputs(seed=0):
    out = dict(first_inputs(seed))
    for name, value in second_inputs(seed + 1).items():
        if name != "x":
            out[name + "_2"] = value
    return out


def reference(
    x, attn_norm_w, w_in, conv_w, a_log, dt_bias, la_norm_w, lambda_q1, lambda_k1, lambda_q2,
    lambda_k2, diff_norm_w, rel_bias, w_out, ffn_norm_w, w_gate_up, w_down, final_norm_w, mem_2,
    g_mem_2, rel_bias_2, g_mix_2, w_in_2, w_alpha_up_2, b_alpha_2, g_gla_head_2, w_proj_gla_2,
    w_proj_moba_2, w_out_2, g_cross_2, w_cq_2, w_ckv_2, w_co_2, g_moe_2, w_router_group_2,
    b_router_group_2, w_router_expert_2, b_router_expert_2, w_exp_gate_2, w_exp_up_2,
    w_exp_down_2, g_final_2,
):
    x = first_block(
        x, attn_norm_w, w_in, conv_w, a_log, dt_bias, la_norm_w, lambda_q1, lambda_k1,
        lambda_q2, lambda_k2, diff_norm_w, rel_bias, w_out, ffn_norm_w, w_gate_up, w_down,
        final_norm_w,
    )
    return second_block(
        x, mem_2, g_mem_2, rel_bias_2, g_mix_2, w_in_2, w_alpha_up_2, b_alpha_2, g_gla_head_2,
        w_proj_gla_2, w_proj_moba_2, w_out_2, g_cross_2, w_cq_2, w_ckv_2, w_co_2, g_moe_2,
        w_router_group_2, b_router_group_2, w_router_expert_2, b_router_expert_2, w_exp_gate_2,
        w_exp_up_2, w_exp_down_2, g_final_2,
    )


_drawn_inputs = setup_inputs


def setup_inputs(seed=0):
    import zlib

    import numpy as np

    out = dict(_drawn_inputs(seed))
    spreads = {}
    factors = {'lambda_q2': 2.771,
     'lambda_k2': 6.929,
     'g_mem_2': 7.671,
     'g_mix_2': 2.674,
     'g_gla_head_2': 3.499,
     'g_cross_2': 6.492,
     'b_router_group_2': 21.424,
     'b_router_expert_2': 57.512,
     'g_final_2': 8.049,
     'g_moe_2': 8.0}
    for name, (base, spread) in spreads.items():
        noise = np.random.default_rng([zlib.crc32(name.encode()), seed]).standard_normal(out[name].shape)
        drawn = base * np.exp(spread * noise) if base else spread * noise
        out[name] = __import__('jax').numpy.asarray(drawn.astype(out[name].dtype))
    for name, factor in factors.items():
        out[name] = (out[name] * factor).astype(out[name].dtype)
    return out
```

```python
from contextlib import ExitStack

import numpy as np

import concourse.bass as bass
from concourse import mybir

F32 = mybir.dt.float32
ALU = mybir.AluOpType
ACT = mybir.ActivationFunctionType
AX_X = mybir.AxisListType.X

P = 128
T = 256
TT = T // P
D = 1024
KD = D // P
H = 4
CH = 64
NCH = T // CH
HT = H * TT
DFF = 2816
FT = DFF // P
NE = 32
NG = 4
EG = NE // NG
DE = 512
SL = 64
ROUNDS = T // SL
EPS = 1e-6
LAM_INIT = 0.8 - 0.6 * 1.0
MASKED = -1.0e30
SLOTS = 6
RING_A = 5
LEVELS = 5

C_Q, C_K, C_V, C_Z, C_BA, C_QD, C_KD, C_VD = 0, 512, 1024, 1536, 2048, 2056, 2568, 3080
C2_QK, C2_V, C2_R, C2_A, C2_QM, C2_KM, C2_VM, C2_ZG, C2_ZM = 0, 512, 1024, 1536, 1552, 2064, 2576, 3088, 4112

(K_ID, K_ONE, K_CAUSAL, K_STRICT, K_BELOW, K_PAIR, K_BEFORE, K_FLIP) = range(8)
K_LEVEL = 8
N_TILES = K_LEVEL + LEVELS
REL = 384


def shape_constants():
    s, c = np.meshgrid(np.arange(P), np.arange(P), indexing="ij")
    same = s // CH == c // CH
    tiles = [s == c, s >= 0, same & (s <= c), same & (s < c), same & (s > c),
             (s // 2 == c // 2) & (s < c), s < c, s + c == P - 1]
    for level in range(LEVELS):
        w = 2 << level
        tiles.append((s // (2 * w) == c // (2 * w)) & (s % (2 * w) < w) & (c % (2 * w) >= w))
    n = 255 - np.arange(REL)
    past = np.maximum(n, 0)
    far = 16 + (np.log(np.maximum(past, 1) / 16) / np.log(8.0) * 16 + 1e-6).astype(np.int64)
    bucket = np.where(past < 16, past, np.minimum(far, 31))
    table = np.zeros((P, REL))
    table[bucket[n >= 0], np.arange(REL)[n >= 0]] = 1.0
    table[32, n < 0] = MASKED
    index = np.broadcast_to(np.arange(P), (P, P))
    return np.concatenate([t.astype(np.float64) for t in tiles] + [table, index], axis=1).astype(np.float32)


def two_blocks(nc, a, const, out, dump=None):
    stack = ExitStack()
    with stack:
        def sb(name, shape):
            return stack.enter_context(nc.sbuf_tensor(name, shape, F32))

        sems = {}

        def sem(name):
            if name not in sems:
                sems[name] = stack.enter_context(nc.semaphore(name))
            return sems[name]

        ring = sb("ring", [P, RING_A, 4096])
        work = sb("work", [P, 13440])
        x = sb("x", [P, TT, D])
        hn = sb("hn", [P, TT, D])
        hT = sb("hT", [P, KD, T])
        qz = sb("qz", [P, H, 2, T])
        kf = sb("kf", [P, H, T])
        vt = sb("vt", [P, TT, 512])
        zt = sb("zt", [P, TT, 512])
        bias = sb("bias", [P, 8, T])
        cst = sb("cst", [P, N_TILES * P + REL + P])
        rows = sb("rows", [96, P])
        cols = sb("cols", [P, 96])
        relb = sb("relb", [33, 12])
        relr = sb("relr", [12, REL])
        rowv = sb("rowv", [P, 1088])
        w_ba = sb("w_ba", [P, KD, 8])
        w_al = sb("w_al", [P, KD, 16])
        w_up16 = sb("w_up16", [17, 256])
        w_rt = sb("w_rt", [P, KD, NG + NE])
        st = sb("st", [P, 512])
        S = sb("S", [P, H, P])
        rel_dram = nc.dram_tensor("rel_dram", [12, REL], F32, kind="Internal").ap()

        def tile(i):
            return cst[:, i * P:(i + 1) * P]

        ident, ones = tile(K_ID), tile(K_ONE)
        onehot = cst[0:33, N_TILES * P:N_TILES * P + REL]
        index = cst[:, N_TILES * P + REL:]
        G_ATTN, G_FFN, G_MIX, G_CROSS, G_MEM, G_MOE = range(6)
        R_DT, R_A, R_LA, R_DIFF, R_GLA, R_BG, R_BE, R_LAM = 0, 4, 8, 136, 264, 776, 780, 812

        at = [0]

        def area(*shape):
            n = int(np.prod(shape))
            v = work[:, at[0]:at[0] + n]
            at[0] += n
            assert at[0] <= 13440
            if len(shape) == 1:
                return v
            names = "abcd"[:len(shape)]
            return v.rearrange(f"p ({' '.join(names)}) -> p {' '.join(names)}",
                               **{k: s for k, s in zip(names, shape)})

        cvi = area(12, T + 3)
        cv = area(12, T)
        qn, kn, vc = cv[:, 0:4, :], cv[:, 4:8, :], cv[:, 8:12, :]
        dT, eB, aT, LT, Tn, Tt, vnew = (area(HT, P) for _ in range(7))
        at[0] = 0
        vb, kbg, kr = (area(HT, P) for _ in range(3))
        X = hT[:, 0:4, :].rearrange("p a (b c) -> p (a b) c", b=2)
        Ct = hT[:, 4:8, :].rearrange("p a (b c) -> p (a b) c", b=2)
        u, wT = X, Ct
        sqk = dT, eB
        gb, bb = aT, LT
        at[0] = 6180
        sc = area(8, T)
        pT = area(2, 8, P)
        at[0] = 0
        actT = area(FT, T)
        sil = area(2, 2, T)
        at[0] = 6700
        flip = area(8, T)
        at[0] = 0
        qg, kg = area(2, T), area(2, T)
        zg, zm = area(TT, D), area(TT, D)
        gnt = work[:, 5376:6400].rearrange("p (i c) -> p i c", c=P)
        at[0] = 10300
        memT = area(KD, T)
        at[0] = 0
        slot5 = area(4096)
        ehid, esil = area(2, 4, T), area(2, 2, T)
        Wt = area(TT, NE)
        rl, ro = area(TT, NG + NE), area(1024)
        at[0] = 5120
        alT = area(T)
        la, bc, e1, e2 = area(TT, T), area(2, T), area(2, T), area(2, T)
        kl, qb, qez, klt, atT = area(2, T), area(2, T), area(2, 2, T), area(TT, 2, P), area(HT, P)
        sts = area(NCH, 2, 256)

        bank = [stack.enter_context(nc.psum_tensor(f"bank{i}", [P, 512], F32)) for i in range(8)]
        filled = [sem(f"filled{i}") for i in range(8)]
        emptied = [sem(f"emptied{i}") for i in range(8)]
        turns = {}
        used = [0] * 8
        order = [0]
        base = [0] * 8

        loads = []
        released = {}

        def kp(w):
            return w.rearrange("(k p) n -> p k n", p=P)

        def load(name, src):
            loads.append((name, src))
            return len(loads) - 1

        w_in, w_in2 = kp(a["w_in"][0]), kp(a["w_in_2"][0])
        L = {}
        for name, c0 in (("q", C_Q), ("k", C_K), ("v", C_V), ("z", C_Z), ("qd", C_QD), ("kd", C_KD), ("vd", C_VD)):
            L[name] = load(name, w_in[:, :, c0:c0 + 512])
        for i in range(2):
            L["wo", i] = load("wo", kp(a["w_out"][0])[:, :, i * 512:(i + 1) * 512])
        for j in range(FT // 2):
            L["gu", j] = load("gu", a["w_gate_up"][0].rearrange("(k p) (g n) -> p k g n", p=P, g=2)[:, :, :, j * 256:(j + 1) * 256])
        for j in range(0, FT, 4):
            n = min(4, FT - j)
            L["dn", j] = load("dn", kp(a["w_down"][0])[:, j:j + n, :])
        for name, c0 in (("qkg", C2_QK), ("vg", C2_V), ("rg", C2_R), ("qm", C2_QM), ("km", C2_KM),
                         ("zg0", C2_ZG), ("zg1", C2_ZG + 512), ("zm0", C2_ZM), ("zm1", C2_ZM + 512), ("vm", C2_VM)):
            L[name] = load(name, w_in2[:, :, c0:c0 + 512])
        L["pg"] = load("pg", kp(a["w_proj_gla_2"][0]))
        L["pm"] = load("pm", kp(a["w_proj_moba_2"][0]))
        for i in range(2):
            L["wo2", i] = load("wo2", kp(a["w_out_2"][0])[:, :, i * 512:(i + 1) * 512])
        L["ck"] = load("ck", kp(a["w_ckv_2"][0])[:, :, 0:512])
        L["cv"] = load("cv", kp(a["w_ckv_2"][0])[:, :, 512:1024])
        L["cq"] = load("cq", kp(a["w_cq_2"][0]))
        L["co"] = load("co", kp(a["w_co_2"][0]))
        NA = len(loads)

        def slot(n):
            return ring[:, n % RING_A, :]

        def eslot(j):
            return ring[:, j, :] if j < RING_A else slot5

        loaded = [sem(f"loaded{i}") for i in range(RING_A)]

        def pieces(n):
            return 2 if loads[n][0] == "gu" else 1

        def wait_load(eng, n):
            eng.wait_ge(loaded[n % RING_A], 16 * sum(pieces(m) for m in range(n % RING_A, n + 1, RING_A)))

        class Engine:

            def __init__(self, eng, name):
                self.eng, self.own, self.count = eng, name, {}

            def step(self, ins, name=None):
                name = name or self.own
                self.count[name] = self.count.get(name, 0) + 1
                ins.then_inc(sem(name), 1)
                self.eng.wait_ge(sem(name), self.count[name])

            def filled(self, turn):
                b, k = turns[turn]
                self.eng.wait_ge(filled[b], k)
                return bank[b]

            def empty(self, ins, turn):
                b, k = turns[turn]
                ins.then_inc(emptied[b], 1)
                self.eng.wait_ge(emptied[b], k)

            def on(self, name, value=1):
                self.eng.wait_ge(sem(name), value)

            def after(self, turn):
                b, k = turns[turn]
                self.eng.wait_ge(emptied[b], k)

        N_SMALL = 26
        block = stack.enter_context(nc.Block())

        @block.tensor
        def _(eng):
            mm, tr = nc.tensor.matmul, nc.tensor.transpose
            e = Engine(eng, "pe_step")

            def begin(name):
                b = order[0] % 8
                order[0] += 1
                used[b] += 1
                turns[name] = (b, used[b])
                if used[b] > 1:
                    eng.wait_ge(emptied[b], used[b] - 1)
                return bank[b]

            def end(ins, name):
                ins.then_inc(filled[turns[name][0]], 1)

            def release(n, turn):
                b, k = turns[turn]
                released[n] = (filled[b], k)

            def transposes(name, pieces):
                b = begin(name)
                for i, piece in enumerate(pieces):
                    ins = tr(b[:, i * P:(i + 1) * P], piece, ident)
                end(ins, name)

            def norm_transposed(n):
                for j in range(4):
                    if j == 0:
                        e.on(f"normed{n}", TT)
                    transposes(f"hT{n}.{j}", [hn[:, t, k * P:(k + 1) * P] for k in (2 * j, 2 * j + 1) for t in range(TT)])

            def normed(n):
                for j in range(4):
                    e.after(f"hT{n}.{j}")

            def features(name, w, src, n, tiles=4, kk=KD):
                for half in range(tiles // 2):
                    b = begin(f"{name}.{half}")
                    for f in range(2):
                        for k in range(kk):
                            ins = mm(b[:, f * T:(f + 1) * T], w[:, k, (2 * half + f) * P:(2 * half + f + 1) * P],
                                     src[:, k, :], start=k == 0, stop=k == kk - 1)
                    end(ins, f"{name}.{half}")
                release(n, f"{name}.{half}")

            def tokens(name, w, src, n, kk=KD):
                for t in range(TT):
                    b = begin(f"{name}.{t}")
                    for k in range(kk):
                        ins = mm(b[:, :], src[:, k, t * P:(t + 1) * P], w[:, k, :], start=k == 0, stop=k == kk - 1)
                    end(ins, f"{name}.{t}")
                release(n, f"{name}.{t}")

            def slot8(n):
                wait_load(eng, n)
                return slot(n).rearrange("p (k n) -> p k n", k=KD)

            def attention(kind, maps, full):
                for t in range(TT):
                    nk = TT if full else t + 1
                    per = 512 // (nk * P)
                    for m0 in range(0, maps, per):
                        b = begin(f"{kind}s{t}.{m0}")
                        for m in range(m0, m0 + per):
                            q = qz[:, m // 2, m % 2, :] if not full else qz[:, m, 0, :]
                            k = kf[:, m // 2, :] if not full else kf[:, m, :]
                            ins = mm(b[:, (m - m0) * nk * P:(m - m0 + 1) * nk * P], q[:, t * P:(t + 1) * P],
                                     k[:, 0:nk * P], start=True, stop=True)
                        end(ins, f"{kind}s{t}.{m0}")
                    pm = 4 if kind == "df" else maps
                    e.on(f"{kind}_p", t + 1)
                    for kt in range(nk):
                        for m0 in range(0, pm, 4):
                            step = 2 if kind == "df" else 1
                            transposes(f"{kind}t{t}.{kt}.{m0}", [sc[:, m * step, kt * P:(kt + 1) * P] for m in range(m0, m0 + 4)])
                    b = begin(f"{kind}o{t}")
                    dv = 512 // pm
                    for kt in range(nk):
                        for m0 in range(0, pm, 4):
                            e.after(f"{kind}t{t}.{kt}.{m0}")
                    for m in range(pm):
                        for kt in range(nk):
                            ins = mm(b[:, m * dv:(m + 1) * dv], pT[:, kt, m, :], vt[:, kt, m * dv:(m + 1) * dv],
                                     start=kt == 0, stop=kt == nk - 1)
                    end(ins, f"{kind}o{t}")

            e.on("consts", 16)
            e.on("small", 16 * N_SMALL)
            b = begin("cols")
            end(tr(b[:, 0:96], rows[:, :], ident[0:96, 0:96]), "cols")
            b = begin("rel")
            e.on("relb_one")
            end(mm(b[0:12, 0:REL], relb[:, :], onehot, start=True, stop=True), "rel")

            norm_transposed(G_ATTN)
            normed(G_ATTN)
            b = begin("ba")
            for t in range(TT):
                for k in range(KD):
                    ins = mm(b[:, t * 8:(t + 1) * 8], hT[:, k, t * P:(t + 1) * P], w_ba[:, k, :], start=k == 0, stop=k == KD - 1)
            end(ins, "ba")
            for name in ("q", "k", "v"):
                features(name, slot8(L[name]), hT, L[name])
            tokens("z", slot8(L["z"]), hT, L["z"])
            for name in ("qd", "kd"):
                features(name, slot8(L[name]), hT, L[name])
            tokens("vd", slot8(L["vd"]), hT, L["vd"])

            for i in range(4):
                e.on("squares", i // 2 + 1)
                b = begin(f"ss{i}")
                end(mm(b[:, :], ones, sqk[i // 2][:, (i % 2) * 4:(i % 2) * 4 + 4, :], start=True, stop=True), f"ss{i}")
            e.on("g_wide")
            for j in range(2):
                b = begin(f"B{j}")
                for i in range(4):
                    ins = mm(b[:, i * P:(i + 1) * P], gb[:, 4 * j + i, :], tile(K_CAUSAL), start=True, stop=True)
                end(ins, f"B{j}")
            b = begin("gcol")
            mm(b[:, 0:HT], tile(K_CAUSAL), st[:, 0:HT], start=True, stop=True)
            end(mm(b[:, HT:2 * HT], tile(K_BELOW), st[:, 0:HT], start=True, stop=True), "gcol")
            e.on("beta_wide")
            for j in range(2):
                b = begin(f"beta{j}")
                for i in range(4):
                    ins = mm(b[:, i * P:(i + 1) * P], bb[:, 4 * j + i, :], ident, start=True, stop=True)
                end(ins, f"beta{j}")
            e.on("q_normed", 2)
            e.on("k_normed", 2)
            for name, src in (("kk", kn), ("qk", qn)):
                for j in range(2):
                    b = begin(f"{name}{j}")
                    for i in range(4):
                        h, t = (4 * j + i) // TT, i % TT
                        ins = mm(b[:, i * P:(i + 1) * P], kn[:, h, t * P:(t + 1) * P], src[:, h, t * P:(t + 1) * P],
                                 start=True, stop=True)
                    end(ins, f"{name}{j}")
            for name, src in (("vtr", vc), ("ktr", kn)):
                for j in range(2):
                    transposes(f"{name}{j}", [src[:, (4 * j + i) // TT, (i % TT) * P:(i % TT + 1) * P] for i in range(4)])
            e.on("pairs")
            for j in range(2):
                transposes(f"T0{j}", [Tt[:, 4 * j + i, :] for i in range(4)])
            for level in range(LEVELS):
                e.on("lower", level + 1)
                for j in range(2):
                    if level == 0:
                        e.after(f"T0{j}")
                    else:
                        e.after(f"Dt{level - 1}.{j}")
                        e.after(f"Dn{level - 1}.{j}")
                    b = begin(f"X{level}.{j}")
                    for i in range(4):
                        ins = mm(b[:, i * P:(i + 1) * P], Ct[:, 4 * j + i, :], Tn[:, 4 * j + i, :], start=True, stop=True)
                    end(ins, f"X{level}.{j}")
                for j in range(2):
                    e.after(f"X{level}.{j}")
                    for side in ("t", "n") if level < LEVELS - 1 else ("t",):
                        b = begin(f"D{side}{level}.{j}")
                        for i in range(4 * j, 4 * j + 4):
                            l, r = (X, Tt) if side == "t" else (Tt, X)
                            ins = mm(b[:, (i % 4) * P:(i % 4 + 1) * P], l[:, i, :], r[:, i, :], start=True, stop=True)
                        end(ins, f"D{side}{level}.{j}")
            e.after(f"Dt{LEVELS - 1}.0")
            e.after(f"Dt{LEVELS - 1}.1")
            e.on("k_scaled")
            for j in range(2):
                b = begin(f"u{j}")
                for i in range(4):
                    ins = mm(b[:, i * P:(i + 1) * P], Tt[:, 4 * j + i, :], vb[:, 4 * j + i, :], start=True, stop=True)
                end(ins, f"u{j}")
                b = begin(f"w{j}")
                for i in range(4):
                    ins = mm(b[:, i * P:(i + 1) * P], kbg[:, 4 * j + i, :], Tt[:, 4 * j + i, :], start=True, stop=True)
                end(ins, f"w{j}")
            e.after("w0")
            e.after("w1")
            e.on("q_scaled")
            e.on("state")
            qs = qn.rearrange("p h (t c) -> p (h t) c", t=TT)
            for c in range(NCH):
                t, lo = c // 2, (c % 2) * CH
                if c:
                    e.after(f"dS{c - 1}")
                b = begin(f"wS{c}")
                for h in range(H):
                    ins = mm(b[:, h * P:(h + 1) * P], wT[:, h * TT + t, :], S[:, h, :], start=True, stop=True)
                end(ins, f"wS{c}")
                e.after(f"wS{c}")
                if c < NCH - 1:
                    b = begin(f"dS{c}")
                    for h in range(H):
                        ins = mm(b[:, h * P:(h + 1) * P], kr[lo:lo + CH, h * TT + t, :], vnew[lo:lo + CH, h * TT + t, :],
                                 start=True, stop=True)
                    end(ins, f"dS{c}")
                b = begin(f"o{c}")
                for h in range(H):
                    mm(b[:, h * P:(h + 1) * P], qs[:, h * TT + t, :], S[:, h, :], start=True, stop=False)
                    ins = mm(b[:, h * P:(h + 1) * P], aT[:, h * TT + t, :], vnew[:, h * TT + t, :], start=False, stop=True)
                end(ins, f"o{c}")

            def unflip(n, src, heads):
                e.on("bias_in", 16 * n)
                for h in range(0, heads, 2):
                    b = begin(f"bias{n}.{h}")
                    end(mm(b[:, :], tile(K_FLIP), src[:, h:h + 2, :], start=True, stop=True), f"bias{n}.{h}")

            unflip(1, bias[:, 4:8, :], H)
            e.after("qd.0"); e.after("qd.1"); e.after("kd.0"); e.after("kd.1"); e.after("vd.0"); e.after("vd.1")
            attention("df", 8, False)

            def mixed(n, parts, w_names, name):
                e.on(f"mixed{n}", parts)
                for j in range(4):
                    transposes(f"m{n}.{j}", [hn[:, t, k * P:(k + 1) * P] for k in (2 * j, 2 * j + 1) for t in range(TT)])
                for j in range(4):
                    e.after(f"m{n}.{j}")
                for i in range(2):
                    tokens(f"{name}{i}", slot8(L[w_names, i]), hT, L[w_names, i])

            mixed(0, 2, "wo", "res0.")
            unflip(2, flip, 8)
            norm_transposed(G_FFN)
            normed(G_FFN)
            for j in range(FT // 2):
                n = L["gu", j]
                wait_load(eng, n)
                w = slot(n).rearrange("p (k g n) -> p k g n", k=KD, g=2)
                for g in range(2):
                    b = begin(f"gu{j}.{g}")
                    for f in range(2):
                        for k in range(KD):
                            ins = mm(b[:, f * T:(f + 1) * T], w[:, k, g, f * P:(f + 1) * P], hT[:, k, :], start=k == 0, stop=k == KD - 1)
                    end(ins, f"gu{j}.{g}")
                release(n, f"gu{j}.1")
            banks = [begin(f"dn{i}") for i in range(4)]
            for j0 in range(0, FT, 4):
                n = L["dn", j0]
                wait_load(eng, n)
                w = slot(n).rearrange("p (k n) -> p k n", k=4)
                for j in range(j0, min(j0 + 4, FT)):
                    if j % 2 == 0:
                        e.after(f"gu{j // 2}.1")
                for i in range(4):
                    t, half = i // 2, i % 2
                    for j in range(j0, min(j0 + 4, FT)):
                        ins = mm(banks[i][:, :], actT[:, j, t * P:(t + 1) * P], w[:, j - j0, half * 512:(half + 1) * 512],
                                 start=j == 0, stop=j == FT - 1)
                    if j0 + 4 >= FT:
                        end(ins, f"dn{i}")
                if j0 + 4 < FT:
                    ins.then_inc(sem("down_used"), 1)
                    released[n] = (sem("down_used"), j0 // 4 + 1)
                else:
                    release(n, "dn3")

            norm_transposed(G_MIX)
            normed(G_MIX)
            features("qkg", slot8(L["qkg"]), hT, L["qkg"])
            b = begin("al")
            for k in range(KD):
                ins = mm(b[0:16, 0:T], w_al[:, k, :], hT[:, k, :], start=k == 0, stop=k == KD - 1)
            end(ins, "al")
            tokens("vg", slot8(L["vg"]), hT, L["vg"])
            e.after("al")
            e.on("gla_zeroed", 3)
            b = begin("la")
            for t in range(TT):
                ins = mm(b[:, t * T:(t + 1) * T], alT[0:17, t * P:(t + 1) * P], w_up16[:, :], start=True, stop=True)
            end(ins, "la")
            tokens("rg", slot8(L["rg"]), hT, L["rg"])
            e.on("la_ready")
            b = begin("gb")
            for f in range(2):
                for t in range(TT):
                    ins = mm(b[:, f * T + t * P:f * T + (t + 1) * P], la[:, t, f * P:(f + 1) * P], tile(K_CAUSAL), start=True, stop=True)
            end(ins, "gb")
            for name in ("qm", "km"):
                features(name, slot8(L[name]), hT, L[name])
            for name in ("zg0", "zg1", "zm0", "zm1"):
                tokens(name, slot8(L[name]), hT, L[name])
            e.on("gla_q", 4)
            e.on("gla_k")
            for j in range(2):
                b = begin(f"ga{j}")
                for i in range(4):
                    h, t = (4 * j + i) // TT, i % TT
                    ins = mm(b[:, i * P:(i + 1) * P], e2[:, h // 2, t * P:(t + 1) * P], qez[:, h // 2, h % 2, t * P:(t + 1) * P],
                             start=True, stop=True)
                end(ins, f"ga{j}")
            e.on("gla_kl")
            transposes("klt", [kl[:, f, t * P:(t + 1) * P] for t in range(TT) for f in range(2)])
            e.after("klt")
            e.after("vg.0"); e.after("vg.1")
            e.after("ga0"); e.after("ga1")
            e.on("gla_qb")
            for c in range(NCH):
                t, lo = c // 2, (c % 2) * CH
                if c < NCH - 1:
                    b = begin(f"kv{c}")
                    for f in range(2):
                        ins = mm(b[:, f * T:(f + 1) * T], klt[lo:lo + CH, t, f, :], vt[lo:lo + CH, t, f * T:(f + 1) * T], start=True, stop=True)
                    end(ins, f"kv{c}")
            for c in range(NCH):
                t = c // 2
                if c:
                    e.after(f"kv{c - 1}")
                b = begin(f"go{c}")
                for f in range(2):
                    mm(b[:, f * T:(f + 1) * T], qb[:, f, t * P:(t + 1) * P], sts[:, c, f, :], start=True, stop=False)
                    for h in (2 * f, 2 * f + 1):
                        ins = mm(b[:, h * P:(h + 1) * P], atT[:, h * TT + t, :], vt[:, t, h * P:(h + 1) * P], start=False, stop=h % 2 == 1)
                end(ins, f"go{c}")
            tokens("vm", slot8(L["vm"]), hT, L["vm"])
            e.after("qm.0"); e.after("qm.1"); e.after("km.0"); e.after("km.1"); e.after("vm.0"); e.after("vm.1")
            attention("mo", 8, False)

            def half_transposed(name, c0):
                for j in range(2):
                    transposes(f"{name}.{j}", [hn[:, t, c0 + k * P:c0 + (k + 1) * P] for k in (2 * j, 2 * j + 1) for t in range(TT)])
                for j in range(2):
                    e.after(f"{name}.{j}")

            def half_product(name, n, src, k0):
                wait_load(eng, n)
                w = slot(n).rearrange("p (k n) -> p k n", k=4)
                for i in range(2):
                    for t in range(TT):
                        b = begin(f"{name}{i}.{t}")
                        for k in range(4):
                            ins = mm(b[:, :], src[:, k0 + k, t * P:(t + 1) * P], w[:, k, i * 512:(i + 1) * 512], start=k == 0, stop=k == 3)
                        end(ins, f"{name}{i}.{t}")
                release(n, f"{name}1.1")

            e.on("mixed1")
            for c0, k0 in ((0, 0), (512, 2)):
                if c0:
                    e.after("moo0"); e.after("moo1")
                for j in range(2):
                    transposes(f"m1.{k0 + j}", [hn[:, t, c0 + k * P:c0 + (k + 1) * P] for k in (2 * j, 2 * j + 1) for t in range(TT)])
            for j in range(4):
                e.after(f"m1.{j}")
            half_product("pg", L["pg"], hT, 0)
            half_product("pm", L["pm"], hT, 4)
            e.on("merged", 4)
            for j in range(4):
                transposes(f"m2.{j}", [zg[:, t, k * P:(k + 1) * P] for k in (2 * j, 2 * j + 1) for t in range(TT)])
            for j in range(4):
                e.after(f"m2.{j}")
            for i in range(2):
                tokens(f"res1.{i}", slot8(L["wo2", i]), hT, L["wo2", i])

            e.on(f"normed{G_MEM}", TT)
            for j in range(4):
                transposes(f"hT{G_MEM}.{j}", [zm[:, t, k * P:(k + 1) * P] for k in (2 * j, 2 * j + 1) for t in range(TT)])
            normed(G_MEM)
            features("ck", slot8(L["ck"]), memT, L["ck"])
            tokens("cv", slot8(L["cv"]), memT, L["cv"])
            norm_transposed(G_CROSS)
            normed(G_CROSS)
            features("cq", slot8(L["cq"]), hT, L["cq"])
            e.after("cq.0"); e.after("cq.1"); e.after("ck.0"); e.after("ck.1"); e.after("cv.0"); e.after("cv.1")
            attention("me", H, True)
            e.after("meo0"); e.after("meo1")
            half_transposed("m3", 512)
            half_product("res2.", L["co"], hT, 0)

            norm_transposed(G_MOE)
            normed(G_MOE)
            b = begin("rt")
            for t in range(TT):
                for k in range(KD):
                    ins = mm(b[:, t * (NG + NE):(t + 1) * (NG + NE)], hT[:, k, t * P:(t + 1) * P], w_rt[:, k, :], start=k == 0, stop=k == KD - 1)
            end(ins, "rt")
            base[:] = used
            with eng.Fori(0, NE // 2) as i:
                for s in range(2):
                    g, up, dn = (eslot(3 * s + j) for j in range(3))
                    for m, w in enumerate((g, up)):
                        eng.wait_ge(sem(f"expert_in{3 * s + m}"), 16 * i + 16)
                        w = w.rearrange("p (k n) -> p k n", k=KD)
                        for half in range(2):
                            bk = 2 * m + half
                            eng.wait_ge(emptied[bk], 2 * i + (base[bk] + s))
                            for f in range(2):
                                for k in range(KD):
                                    ins = mm(bank[bk][:, f * T:(f + 1) * T], w[:, k, (2 * half + f) * P:(2 * half + f + 1) * P],
                                             hT[:, k, :], start=k == 0, stop=k == KD - 1)
                            ins.then_inc(filled[bk], 1)
                    eng.wait_ge(sem(f"expert_in{3 * s + 2}"), 16 * i + 16)
                    w = dn.rearrange("p (k n) -> p k n", k=4)
                    for bk in (2, 3):
                        eng.wait_ge(emptied[bk], 2 * i + (base[bk] + s + 1))
                    for t in range(TT):
                        for half in range(2):
                            bk = 4 + 2 * t + half
                            eng.wait_ge(emptied[bk], 2 * i + (base[bk] + s))
                            for k in range(4):
                                ins = mm(bank[bk][:, :], ehid[:, s, k, t * P:(t + 1) * P], w[:, k, half * 512:(half + 1) * 512],
                                         start=k == 0, stop=k == 3)
                            ins.then_inc(filled[bk], 1)

        @block.sync
        def _(eng):
            eng.dma_start(x[:, :, :], a["x"][0].rearrange("(t p) d -> p t d", p=P)).then_inc(sem("x_in"), 16)
            for n, (name, src) in enumerate(loads):
                if n >= RING_A:
                    s, v = released[n - RING_A]
                    eng.wait_ge(s, v)
                dst = slot(n)
                if name == "gu":
                    w = dst.rearrange("p (k g n) -> p k g n", k=KD, g=2)
                    for g in range(2):
                        eng.dma_start(w[:, :, g, :], src[:, :, g, :]).then_inc(loaded[n % RING_A], 16)
                    continue
                k, c = src.shape[1], src.shape[2]
                eng.dma_start(dst[:, 0:k * c].rearrange("p (k n) -> p k n", k=k), src).then_inc(loaded[n % RING_A], 16)
            wg, wu, wd = (a[f"w_exp_{m}_2"][0] for m in ("gate", "up", "down"))

            def expert(j, at_):
                w = (wg, wu, wd)[j % 3]
                eng.dma_start(eslot(j).rearrange("p (k n) -> p k n", k=w.shape[1] // P),
                              w[at_].rearrange("o (k p) n -> p (o k) n", p=P)).then_inc(sem(f"expert_in{j}"), 16)

            for j in range(6):
                if j < RING_A:
                    last = max(n for n in range(NA) if n % RING_A == j)
                    s, v = released[last]
                    eng.wait_ge(s, v)
                else:
                    for n in range(2):
                        eng.wait_ge(emptied[turns[f"meo{n}"][0]], turns[f"meo{n}"][1])
                expert(j, slice(j // 3, j // 3 + 1))
            with eng.Fori(0, NE // 2 - 1) as i:
                for j in range(6):
                    s = j // 3
                    bk = (1, 3, 7)[j % 3]
                    eng.wait_ge(filled[bk], 2 * i + (base[bk] + s + 1))
                    expert(j, bass.ds(2 * i + (2 + s), 1))
            eng.wait_ge(sem("result"), TT)
            eng.dma_start(out[0].rearrange("(t p) d -> p t d", p=P), x[:, :, :]).then_inc(sem("out"), 16)
            eng.wait_ge(sem("out"), 16)

        @block.gpsimd
        def _(eng):
            g = nc.gpsimd
            g.memset(qz[64:128, :, 0, :], 0.0).then_inc(sem("zeroed"), 1)
            eng.wait_ge(sem("zeroed"), 1)
            g.memset(qz[0:64, :, 1, :], 0.0).then_inc(sem("zeroed"), 1)
            eng.wait_ge(sem("zeroed"), 2)
            g.memset(cvi[:, :, 0:3], 0.0).then_inc(sem("zeroed"), 1)
            eng.wait_ge(sem("zeroed"), 3)
            g.memset(relb[32:33, :], 1.0).then_inc(sem("relb_one"), 1)
            eng.wait_ge(sem("relb_one"), 1)
            g.memset(S[:, :, :], 0.0).then_inc(sem("state"), 1)
            eng.wait_ge(sem("state"), 1)
            eng.wait_ge(emptied[turns["rel"][0]], turns["rel"][1])
            eng.dma_start(rel_dram[:, :], relr[:, :]).then_inc(sem("rel_stored"), 16)
            eng.wait_ge(sem("rel_stored"), 16)

            def biases(dst, h0, n):
                src = bass.AP(tensor=rel_dram.tensor, offset=rel_dram.offset + h0 * REL, ap=[[1, P], [REL, n], [1, T]])
                eng.dma_start(dst, src).then_inc(sem("bias_in"), 16)

            biases(bias[:, 4:8, :], 0, 4)
            gain = zt.rearrange("p t d -> p (t d)")
            eng.wait_ge(sem("mixed0"), 1)
            eng.dma_start(gain, a["final_norm_w"].rearrange("(o n) -> o n", o=1).broadcast_to([P, D])).then_inc(sem("gain_row"), 16)
            eng.wait_ge(sem("mixed0"), 2)
            biases(flip, 4, 8)
            eng.wait_ge(sem("block1"), 2)
            g.memset(alT[0:32, :], 1.0).then_inc(sem("gla_zeroed"), 1)
            eng.wait_ge(sem("gla_zeroed"), 1)
            g.memset(qez[:, :, :, :], 0.0).then_inc(sem("gla_zeroed"), 1)
            eng.wait_ge(sem("gla_zeroed"), 2)
            g.memset(sts[:, :, :, :], 0.0).then_inc(sem("gla_zeroed"), 1)
            eng.wait_ge(sem("gla_zeroed"), 3)
            eng.wait_ge(sem("merged"), 4)
            eng.dma_start(zm, a["mem_2"][0].rearrange("(t p) d -> p t d", p=P)).then_inc(sem("mem_in"), 16)
            eng.wait_ge(sem("mixed1"), 1)
            eng.dma_start(gain, a["g_final_2"].rearrange("(o n) -> o n", o=1).broadcast_to([P, D])).then_inc(sem("gain_row"), 16)

        @block.scalar
        def _(eng):
            e = Engine(eng, "act_step")

            def act(out, in_, func, name=None, turn=None, **kw):
                ins = nc.scalar.activation(out, in_, func, **kw)
                if turn:
                    e.empty(ins, turn)
                else:
                    e.step(ins, name)

            nsmall = [0]

            def small(dst, src):
                eng.dma_start(dst, src).then_inc(sem("small"), 16)
                nsmall[0] += 1

            eng.dma_start(cst[:, :], const).then_inc(sem("consts"), 16)
            for i, name in enumerate(("attn_norm_w", "ffn_norm_w", "g_mix_2", "g_cross_2", "g_mem_2", "g_moe_2")):
                v = a[name] if name == "g_mem_2" else a[name][0]
                small(rows[i * KD:(i + 1) * KD, :], v.rearrange("(k p) -> k p", p=P))
            small(rows[48:96, :], a["conv_w"][0].rearrange("i (f p) -> (i f) p", p=P))
            small(relb[0:32, 0:4], a["rel_bias"])
            small(relb[0:32, 4:12], a["rel_bias_2"])

            def row(c0, n, v):
                small(rowv[:, c0:c0 + n], v.rearrange("(o n) -> o n", o=1).broadcast_to([P, n]))

            row(R_DT, 4, a["dt_bias"][0])
            row(R_A, 4, a["a_log"][0])
            row(R_LA, 128, a["la_norm_w"][0])
            row(R_DIFF, 128, a["diff_norm_w"][0])
            row(R_GLA, 512, a["g_gla_head_2"][0].rearrange("h d -> (h d)"))
            row(R_BG, NG, a["b_router_group_2"][0])
            row(R_BE, NE, a["b_router_expert_2"][0])
            for i, name in enumerate(("lambda_q1", "lambda_q2", "lambda_k1", "lambda_k2")):
                row(R_LAM + 64 * i, 64, a[name][0])
            small(w_ba[:, :, :], w_in[:, :, C_BA:C_BA + 8])
            small(w_al[:, :, :], w_in2[:, :, C2_A:C2_A + 16])
            small(w_up16[0:16, :], a["w_alpha_up_2"][0])
            small(w_up16[16:17, :], a["b_alpha_2"])
            small(w_rt[:, :, 0:NG], kp(a["w_router_group_2"][0]))
            small(w_rt[:, :, NG:], kp(a["w_router_expert_2"][0]))
            assert nsmall[0] == N_SMALL, nsmall

            def norm(n, src, junk=hn, ready=None):
                if ready:
                    e.on(*ready)
                c = 128 + 8 * n
                for t in range(TT):
                    act(junk[:, t, :], src[:, t, :], ACT.Square, f"ssq{n}", accum_out=st[:, c + t:c + t + 1])
                e.on(f"mean{n}")
                act(st[:, c + 4:c + 6], st[:, c + 2:c + 4], ACT.Ln)
                act(st[:, c + 4:c + 6], st[:, c + 4:c + 6], ACT.Exp, f"rstd{n}", scale=-0.5)

            def gained(n, hT=hT):
                for j in (0, 2):
                    b = e.filled(f"hT{n}.{j}")
                    for i in range(2):
                        k = 2 * j + i
                        act(hT[:, k, :], b[:, i * T:(i + 1) * T], ACT.Copy, turn=f"hT{n}.{j}" if i else None,
                            scale=cols[:, n * KD + k:n * KD + k + 1])

            def copy(dst, turn, view=None, func=ACT.Copy, **kw):
                b = e.filled(turn)
                act(dst, view(b) if view else b[:, :], func, turn=turn, **kw)

            def two(b):
                return b.rearrange("p (f t) -> p f t", f=2)

            def four(b):
                return b.rearrange("p (i c) -> p i c", i=4)

            def queries(turn, h0):
                b = e.filled(turn)
                act(qz[0:64, h0:h0 + 2, 0, :], two(b[0:64, :]), ACT.Copy)
                act(qz[64:128, h0:h0 + 2, 1, :], two(b[64:128, :]), ACT.Copy, turn=turn)

            def softmax(kind, maps, full):
                c = {"df": 300, "mo": 332, "me": 364}[kind]
                for t in range(TT):
                    w = T if full else (t + 1) * P
                    e.on(f"{kind}_max", t + 1)
                    for m in range(maps):
                        last = m == maps - 1
                        act(sc[:, m, 0:w], sc[:, m, 0:w], ACT.Exp,
                            (f"{kind}_e" if kind == "df" else f"{kind}_p") if last else None,
                            bias=st[:, c + m:c + m + 1], accum_out=st[:, c + 16 + m:c + 17 + m])
                    pm = 4 if kind == "df" else maps
                    for kt in range(w // P):
                        for m0 in range(0, pm, 4):
                            if (kt + m0 // 4) % 2 == 0:
                                copy(pT[:, kt, m0:m0 + 4, :], f"{kind}t{t}.{kt}.{m0}", four)
                    if kind == "df":
                        copy(hn[:, t, 512:1024], f"dfo{t}")

            def head_rstd(name, c, n):
                e.on(f"{name}_ms")
                act(st[:, c + n:c + 2 * n], st[:, c:c + n], ACT.Ln)
                act(st[:, c + n:c + 2 * n], st[:, c + n:c + 2 * n], ACT.Exp, f"{name}_rs", scale=-0.5)

            def after_residual(name):
                for i in range(2):
                    for t in range(TT):
                        e.after(f"{name}{i}.{t}")

            e.on("x_in", 16)
            norm(G_ATTN, x)
            e.after("cols")
            gained(G_ATTN)
            for g, name in enumerate(("q", "k", "v")):
                for half in range(2):
                    f = 4 * g + 2 * half
                    copy(cvi[:, f:f + 2, 3:3 + T], f"{name}.{half}", two)
                e.on("conv", g + 1)
                act(cv[:, 4 * g:4 * g + 4, :], cv[:, 4 * g:4 * g + 4, :], ACT.Silu, "silu")
                if g < 2:
                    act(sqk[g][:, :, :], cv[:, 4 * g:4 * g + 4, :].rearrange("p h (t c) -> p (h t) c", t=TT), ACT.Square, "squares")
            for t in range(TT):
                copy(zt[:, t, :], f"z.{t}", func=ACT.Silu)
            for half in range(2):
                queries(f"qd.{half}", 2 * half)
            for half in range(2):
                copy(kf[:, 2 * half:2 * half + 2, :], f"kd.{half}", two)
            for t in range(TT):
                copy(vt[:, t, :], f"vd.{t}")
            raw = st[:, 64:80].rearrange("p (t c) -> p c t", t=TT)
            ht = lambda c: st[:, c:c + HT].rearrange("p (h t) -> p h t", t=TT)
            e.after("ba")
            act(ht(56), raw[:, 0:H, :], ACT.Exp, "exp_b", scale=-1.0)
            e.on("abs_a")
            act(st[:, 96:104], st[:, 88:96], ACT.Exp, scale=-1.0)
            act(st[:, 104:112], st[:, 96:104], ACT.Ln, "softplus", bias=1.0)
            act(st[:, 120:124], rowv[:, R_A:R_A + H], ACT.Exp, "exp_a_log")
            e.on("lam_dots")
            act(st[:, 422:424], st[:, 420:422], ACT.Exp, "lam_exp")
            for i in range(4):
                v = sqk[i // 2][:, (i % 2) * 4:(i % 2) * 4 + 4, :]
                copy(v, f"ss{i}", four, ACT.Ln, bias=st[:, 510:511])
                act(v, v, ACT.Exp, "inv_norm", scale=-0.5)
            e.after("gcol")
            act(st[:, 32:48], st[:, 16:32], ACT.Exp, "exp_g")
            e.on("k_normed", 2)
            for j in range(2):
                b = e.filled(f"B{j}")
                act(eB[:, 4 * j:4 * j + 4, :], four(b), ACT.Exp, "exp_B")
            e.on("gdiff")
            act(dT[:, :, :], dT[:, :, :], ACT.Exp, "decay")
            for j in range(2):
                copy(Tn[:, 4 * j:4 * j + 4, :], f"T0{j}", four)
            for level in range(LEVELS):
                for j in range(2):
                    copy(X[:, 4 * j:4 * j + 4, :], f"X{level}.{j}", four)
            for j in range(2):
                copy(u[:, 4 * j:4 * j + 4, :], f"u{j}", four)
                copy(wT[:, 4 * j:4 * j + 4, :], f"w{j}", four)
            for c in range(NCH):
                lo = (c % 2) * CH
                copy(hn[lo:lo + CH, c // 2, 0:512], f"o{c}", lambda b: b[lo:lo + CH, :])
            head_rstd("la", 200, 8)
            softmax("df", 8, False)
            head_rstd("dh", 216, 8)
            for j in (0, 2):
                copy(hT[:, 2 * j:2 * j + 2, :], f"m0.{j}", two)
            after_residual("res0.")
            norm(G_FFN, x)
            gained(G_FFN)
            for j in range(FT // 2):
                if j >= 2:
                    e.after(f"gu{j - 2}.1")
                copy(sil[:, j % 2, :, :], f"gu{j}.0", two, ACT.Silu)
            for i in range(4):
                e.after(f"dn{i}")
            norm(6, x)
            norm(G_MIX, x, ready=("block1", 2))
            gained(G_MIX)
            copy(qg, "qkg.0", two)
            copy(kg, "qkg.1", two)
            e.on("gla_zeroed", 3)
            copy(alT[0:16, :], "al", lambda b: b[0:16, 0:T])
            for t in range(TT):
                copy(vt[:, t, :], f"vg.{t}")
            flat = lambda m: m.rearrange("p a b -> p (a b)")
            e.on("abs_la")
            act(flat(e2), flat(e1), ACT.Exp, scale=-1.0)
            act(flat(e2), flat(e2), ACT.Ln, "softplus_la", bias=1.0)
            for t in range(TT):
                copy(zt[:, t, :], f"rg.{t}", func=ACT.Silu)
            copy(flat(bc), "gb")
            for half in range(2):
                queries(f"qm.{half}", 2 * half)
            for half in range(2):
                copy(kf[:, 2 * half:2 * half + 2, :], f"km.{half}", two)
            e.on("gla_diff", 2)
            act(flat(e2), flat(e1), ACT.Exp, scale=-1.0)
            act(flat(e1), flat(e1), ACT.Exp)
            act(flat(kl), flat(kl), ACT.Exp)
            act(flat(qb), flat(bc), ACT.Exp, "gla_exp")
            for z, m in (("zg", zg), ("zm", zm)):
                for i in range(2):
                    for t in range(TT):
                        copy(m[:, t, i * 512:(i + 1) * 512], f"{z}{i}.{t}", func=ACT.Sigmoid)
            copy(klt.rearrange("p t f c -> p (t f) c"), "klt", four)
            for c in range(NCH):
                lo = (c % 2) * CH
                copy(hn[lo:lo + CH, c // 2, 0:512], f"go{c}", lambda b: b[lo:lo + CH, :])
            for t in range(TT):
                copy(vt[:, t, :], f"vm.{t}")
            head_rstd("gl", 232, 8)
            softmax("mo", 8, False)
            for j in (0, 2):
                copy(hT[:, 2 * j:2 * j + 2, :], f"m1.{j}", two)
            for j in (0, 2):
                copy(hT[:, 2 * j:2 * j + 2, :], f"m2.{j}", two)
            norm(G_MEM, zm, ready=("mem_in", 16))
            gained(G_MEM, memT)
            for half in range(2):
                copy(kf[:, 2 * half:2 * half + 2, :], f"ck.{half}", two)
            for t in range(TT):
                copy(vt[:, t, :], f"cv.{t}")
            after_residual("res1.")
            norm(G_CROSS, x)
            gained(G_CROSS)
            for half in range(2):
                copy(qz[:, 2 * half:2 * half + 2, 0, :], f"cq.{half}", two)
            softmax("me", H, True)
            copy(hT[:, 0:2, :], "m3.0", two)
            after_residual("res2.")
            norm(G_MOE, x)
            gained(G_MOE)
            e.on("router_max")
            act(ro[:, 16:24], ro[:, 16:24], ACT.Exp)
            e.on("router_top")
            act(ro[:, 200:202], ro[:, 200:202], ACT.Exp, "router_exp")
            with eng.Fori(0, NE // 2) as i:
                for s in range(2):
                    for half in range(2):
                        eng.wait_ge(filled[half], 2 * i + (base[half] + s + 1))
                        eng.wait_ge(emptied[2 + half], 2 * i + (base[2 + half] + s))
                        nc.scalar.activation(esil[:, half, :, :], two(bank[half]), ACT.Silu).then_inc(emptied[half], 1)
            e.on("expert_sum")
            norm(7, x)

        @block.vector
        def _(eng):
            e = Engine(eng, "dve_step")
            v = nc.vector

            def tt(out, in0, in1, op, name=None, turn=None):
                ins = v.tensor_tensor(out, in0, in1, op)
                e.empty(ins, turn) if turn else e.step(ins, name)

            def ts(out, in0, s1, s2, op0, op1=None, name=None, turn=None):
                ins = v.tensor_scalar(out, in0, s1, s2, op0, op1) if op1 is not None else v.tensor_scalar(out, in0, s1, None, op0)
                e.empty(ins, turn) if turn else e.step(ins, name)

            def stt(out, in0, scalar, in1, op0, op1, name=None, turn=None):
                ins = v.scalar_tensor_tensor(out=out, in0=in0, scalar=scalar, in1=in1, op0=op0, op1=op1)
                e.empty(ins, turn) if turn else e.step(ins, name)

            def copy(dst, turn, view=None):
                b = e.filled(turn)
                e.empty(v.tensor_copy(dst, view(b) if view else b[:, :]), turn)

            def two(b):
                return b.rearrange("p (f t) -> p f t", f=2)

            def four(b):
                return b.rearrange("p (i c) -> p i c", i=4)

            def wide(c, n, w):
                return st[:, c:c + n].unsqueeze(2).broadcast_to([P, n, w])

            def rep(m, n):
                return m.unsqueeze(1).broadcast_to([P, n, P])

            def norm_scale(n):
                c = 128 + 8 * n
                e.on(f"ssq{n}", TT)
                ts(st[:, c + 2:c + 4], st[:, c:c + 2], 1.0 / D, EPS, ALU.mult, ALU.add, f"mean{n}")
                e.on(f"rstd{n}")

            def norm(n, src, dst=hn):
                norm_scale(n)
                c = 128 + 8 * n
                for t in range(TT):
                    ts(dst[:, t, :], src[:, t, :], st[:, c + 4 + t:c + 5 + t], None, ALU.mult, name=f"normed{n}")

            def gained(n, hT=hT):
                for j in (1, 3):
                    b = e.filled(f"hT{n}.{j}")
                    for i in range(2):
                        k = 2 * j + i
                        ts(hT[:, k, :], b[:, i * T:(i + 1) * T], cols[:, n * KD + k:n * KD + k + 1], None, ALU.mult,
                           turn=f"hT{n}.{j}" if i else None)

            def attention(kind, maps, full, scale):
                c = {"df": 300, "mo": 332, "me": 364}[kind]
                for t in range(TT):
                    nk = TT if full else t + 1
                    w = nk * P
                    per = 512 // w
                    for m0 in range(0, maps, per):
                        turn = f"{kind}s{t}.{m0}"
                        b = e.filled(turn).rearrange("p (m k) -> p m k", m=per)
                        if kind == "df":
                            for i in range(2):
                                stt(sc[:, m0 + i:m0 + per:2, 0:w], b[:, i::2, :], scale, bias[:, m0 // 2:(m0 + per) // 2, T - w:],
                                    ALU.mult, ALU.add, turn=turn if i else None)
                        elif kind == "mo":
                            stt(sc[:, m0:m0 + per, 0:w], b, scale, bias[:, m0:m0 + per, T - w:], ALU.mult, ALU.add, turn=turn)
                        else:
                            ts(sc[:, m0:m0 + per, :], b, scale, None, ALU.mult, turn=turn)
                    e.step(v.tensor_reduce(st[:, c:c + maps], sc[:, 0:maps, 0:w], AX_X, ALU.max))
                    ts(st[:, c:c + maps], st[:, c:c + maps], -1.0, None, ALU.mult, name=f"{kind}_max")
                    e.on(f"{kind}_e" if kind == "df" else f"{kind}_p", t + 1)
                    r = c + 24
                    e.step(v.reciprocal(st[:, r:r + maps], st[:, c + 16:c + 16 + maps]))
                    if kind == "df":
                        ts(st[:, r + 1:r + 8:2], st[:, r + 1:r + 8:2], st[:, 425:426], None, ALU.mult)
                        for h in range(H):
                            ts(sc[:, 2 * h, 0:w], sc[:, 2 * h, 0:w], st[:, r + 2 * h:r + 2 * h + 1], None, ALU.mult)
                            stt(sc[:, 2 * h, 0:w], sc[:, 2 * h + 1, 0:w], st[:, r + 2 * h + 1:r + 2 * h + 2], sc[:, 2 * h, 0:w],
                                ALU.mult, ALU.add, name="df_p" if h == H - 1 else None)
                    pm = 4 if kind == "df" else maps
                    for kt in range(nk):
                        for m0 in range(0, pm, 4):
                            if (kt + m0 // 4) % 2:
                                copy(pT[:, kt, m0:m0 + 4, :], f"{kind}t{t}.{kt}.{m0}", four)
                    if kind != "df":
                        b = e.filled(f"{kind}o{t}")
                        dv = 512 // maps
                        tt(hn[:, t, 512:1024].rearrange("p (m d) -> p m d", d=dv), b.rearrange("p (m d) -> p m d", d=dv),
                           wide(r, maps, dv), ALU.mult, turn=f"{kind}o{t}")

            def head_norm(name, o, c, eps, gain, tmp, factor=1.0, done=None):
                tmp = tmp.rearrange("p (t h) d -> p t h d", t=TT)
                tt(tmp, o, o, ALU.mult)
                e.step(v.tensor_reduce(st[:, c:c + 8].rearrange("p (t h) -> p t h", t=TT), tmp, AX_X, ALU.add))
                ts(st[:, c:c + 8], st[:, c:c + 8], 1.0 / P, eps, ALU.mult, ALU.add, f"{name}_ms")
                e.on(f"{name}_rs")
                if factor != 1.0:
                    ts(st[:, c + 8:c + 16], st[:, c + 8:c + 16], factor, None, ALU.mult)
                for t in range(TT):
                    tt(o[:, t], o[:, t], wide(c + 8 + 4 * t, 4, P), ALU.mult)
                    tt(o[:, t], o[:, t], gain, ALU.mult, name=done if t else None)

            def residual(turns_):
                for turn, t, half in turns_:
                    b = e.filled(turn)
                    sl = x[:, t, half * 512:(half + 1) * 512]
                    tt(sl, sl, b[:, :], ALU.add, turn=turn)

            e.step(v.memset(st[:, 510:511], EPS), "eps_col")
            e.on("zeroed", 3)
            b = e.filled("cols")
            e.empty(v.tensor_copy(cols[:, :], b[:, 0:96]), "cols")
            b = e.filled("rel")
            e.empty(v.tensor_copy(relr[:, :], b[0:12, 0:REL]), "rel")
            e.on("x_in", 16)
            norm(G_ATTN, x)
            gained(G_ATTN)
            b = e.filled("ba")
            e.empty(v.tensor_copy(st[:, 64:80], b[:, 0:16]), "ba")
            for g in range(3):
                name = "qkv"[g]
                for f in range(4):
                    if f % 2 == 0:
                        e.after(f"{name}.{f // 2}")
                    F = 4 * g + f
                    tap = lambda i: cols[:, 48 + 12 * i + F:49 + 12 * i + F]
                    ts(cv[:, F, :], cvi[:, F, 0:T], tap(0), None, ALU.mult)
                    for i in range(1, 4):
                        stt(cv[:, F, :], cvi[:, F, i:i + T], tap(i), cv[:, F, :], ALU.mult, ALU.add,
                            name="conv" if i == 3 and f == 3 else None)
            raw = st[:, 64:80].rearrange("p (t c) -> p c t", t=TT)
            ht = lambda c: st[:, c:c + HT].rearrange("p (h t) -> p h t", t=TT)
            per_head = lambda v_: v_.unsqueeze(2).broadcast_to([P, H, TT])
            tt(ht(80), raw[:, H:2 * H, :], per_head(rowv[:, R_DT:R_DT + H]), ALU.add)
            stt(st[:, 88:96], st[:, 80:88], -1.0, st[:, 80:88], ALU.mult, ALU.max, name="abs_a")
            tt(work[:, 13348 - 1024:13348 - 1024 + 128], rowv[:, R_LAM:R_LAM + 128], rowv[:, R_LAM + 128:R_LAM + 256], ALU.mult)
            e.step(v.tensor_reduce(st[:, 420:422], work[:, 13348 - 1024:13348 - 1024 + 128].rearrange("p (i d) -> p i d", i=2), AX_X, ALU.add), "lam_dots")
            e.on("exp_b")
            ts(st[:, 56:64], st[:, 56:64], 1.0, None, ALU.add)
            e.step(v.reciprocal(st[:, 8:16], st[:, 56:64]))
            e.on("softplus")
            stt(st[:, 112:120], st[:, 80:88], 0.0, st[:, 104:112], ALU.max, ALU.add)
            e.on("exp_a_log")
            stt(ht(0), ht(112), -1.0, per_head(st[:, 120:124]), ALU.mult, ALU.mult)
            e.step(v.tensor_copy(gb[:, :, :], wide(0, HT, P)), "g_wide")
            e.step(v.tensor_copy(bb[:, :, :], wide(8, HT, P)), "beta_wide")
            e.on("lam_exp")
            tt(st[:, 424:425], st[:, 423:424], st[:, 422:423], ALU.subtract)
            ts(st[:, 425:426], st[:, 424:425], -LAM_INIT, None, ALU.add)
            for i in range(4):
                e.on("inv_norm", i + 1)
                r = sqk[i // 2][:, (i % 2) * 4:(i % 2) * 4 + 4, :]
                q = (qn, kn)[i // 2][:, 2 * (i % 2):2 * (i % 2) + 2, :].rearrange("p h (t c) -> p (h t) c", t=TT)
                stt(q, q, P ** -0.5 if i < 2 else 1.0, r, ALU.mult, ALU.mult, name="q_normed" if i < 2 else "k_normed")
            b = e.filled("gcol")
            e.empty(v.tensor_copy(st[:, 16:32], b[:, 0:16]), "gcol")
            for j in range(2):
                e.on("exp_B", j + 1)
                b = e.filled(f"B{j}")
                tt(dT[:, 4 * j:4 * j + 4, :], four(b), wide(16 + 4 * j, 4, P), ALU.subtract, turn=f"B{j}")
            tt(dT[:, :, :], dT[:, :, :], rep(tile(K_CAUSAL), HT), ALU.mult, name="gdiff")
            e.on("decay")
            tt(dT[:, :, :], dT[:, :, :], rep(tile(K_CAUSAL), HT), ALU.mult)
            for j in range(2):
                s = slice(4 * j, 4 * j + 4)
                b = e.filled(f"beta{j}")
                tt(LT[:, s, :], four(b), dT[:, s, :], ALU.mult, turn=f"beta{j}")
            tt(LT[:, :, :], LT[:, :, :], rep(tile(K_STRICT), HT), ALU.mult)
            for j in range(2):
                s = slice(4 * j, 4 * j + 4)
                b = e.filled(f"kk{j}")
                tt(LT[:, s, :], four(b), LT[:, s, :], ALU.mult, turn=f"kk{j}")
            tt(Tt[:, :, :], LT[:, :, :], rep(tile(K_PAIR), HT), ALU.mult)
            tt(Tt[:, :, :], rep(ident, HT), Tt[:, :, :], ALU.subtract, name="pairs")
            tt(Ct[:, :, :], LT[:, :, :], rep(tile(K_LEVEL), HT), ALU.mult, name="lower")
            for j in range(2):
                s = slice(4 * j, 4 * j + 4)
                b = e.filled(f"qk{j}")
                tt(aT[:, s, :], four(b), dT[:, s, :], ALU.mult, turn=f"qk{j}")
            e.on("exp_g")
            tt(st[:, 48:56], st[:, 8:16], st[:, 32:40], ALU.mult)
            for j in range(2):
                s = slice(4 * j, 4 * j + 4)
                b = e.filled(f"vtr{j}")
                tt(vb[:, s, :], four(b), wide(8 + 4 * j, 4, P), ALU.mult, turn=f"vtr{j}")
            for j in range(2):
                s = slice(4 * j, 4 * j + 4)
                b = e.filled(f"ktr{j}")
                tt(kbg[:, s, :], four(b), wide(48 + 4 * j, 4, P), ALU.mult)
                tt(kr[:, s, :], four(b), wide(40 + 4 * j, 4, P), ALU.mult, turn=f"ktr{j}")
            q = qn.rearrange("p h (t c) -> p (h t) c", t=TT)
            tt(q, q, eB[:, :, :], ALU.mult, name="q_scaled")
            e.step(v.memset(vnew[:, :, :], 0.0), "k_scaled")
            for level in range(LEVELS):
                for j in range(2):
                    e.filled(f"X{level}.{j}")
                if level < LEVELS - 1:
                    tt(Ct[:, :, :], LT[:, :, :], rep(tile(K_LEVEL + level + 1), HT), ALU.mult, name="lower")
                for j in range(2):
                    s = slice(4 * j, 4 * j + 4)
                    sides = ("t", "n") if level < LEVELS - 1 else ("t",)
                    for side in sides:
                        e.filled(f"D{side}{level}.{j}")
                    for side in sides:
                        m = Tt if side == "t" else Tn
                        turn = f"D{side}{level}.{j}"
                        tt(m[:, s, :], m[:, s, :], four(e.filled(turn)), ALU.subtract, turn=turn)
            by_t = lambda m, t: m.rearrange("p (h t) c -> p h t c", t=TT)[:, :, t, :]
            for c in range(NCH):
                t, lo = c // 2, (c % 2) * CH
                hi = lo + CH
                if c == 0:
                    e.after("u0")
                    e.after("u1")
                b = e.filled(f"wS{c}")
                tt(by_t(vnew, t)[lo:hi], by_t(u, t)[lo:hi], four(b)[lo:hi], ALU.subtract, turn=f"wS{c}")
                if c < NCH - 1:
                    e.filled(f"o{c}")
                    b = e.filled(f"dS{c}")
                    for h in range(H):
                        stt(S[:, h, :], S[:, h, :], eB[:, h * TT + t, hi - 1:hi], b[:, h * P:(h + 1) * P], ALU.mult, ALU.add,
                            turn=f"dS{c}" if h == H - 1 else None)
            heads = lambda c0: hn[:, :, c0:c0 + 512].rearrange("p t (h d) -> p t h d", h=H)
            for c in range(NCH):
                e.after(f"o{c}")
            head_norm("la", heads(0), 200, EPS, rep(rowv[:, R_LA:R_LA + P], 4), dT)
            for t in range(TT):
                e.after(f"z.{t}")
                tt(hn[:, t, 0:512], hn[:, t, 0:512], zt[:, t, :], ALU.mult, name="mixed0" if t else None)
            for h in (0, 2):
                copy(bias[:, h:h + 2, :], f"bias1.{h}", two)
            attention("df", 8, False, 0.125)
            for t in range(TT):
                e.after(f"dfo{t}")
            head_norm("dh", heads(512), 216, 1e-5, rep(rowv[:, R_DIFF:R_DIFF + P], 4), dT, 1.0 - LAM_INIT, done="mixed0")
            for j in (1, 3):
                copy(hT[:, 2 * j:2 * j + 2, :], f"m0.{j}", two)
            residual([(f"res0.{i}.{t}", t, i) for i in range(2) for t in range(TT)])
            norm(G_FFN, x)
            for h in (0, 2, 4, 6):
                copy(bias[:, h:h + 2, :], f"bias2.{h}", two)
            gained(G_FFN)
            for j in range(FT // 2):
                e.after(f"gu{j}.0")
                b = e.filled(f"gu{j}.1")
                tt(actT[:, 2 * j:2 * j + 2, :], two(b), sil[:, j % 2, :, :], ALU.mult, turn=f"gu{j}.1")
            residual([(f"dn{i}", i // 2, i % 2) for i in range(4)])
            norm_scale(6)
            gain = zt.rearrange("p t d -> p (t d)")
            e.on("gain_row", 16)
            for t in range(TT):
                c = 128 + 48 + 4 + t
                ts(x[:, t, :], x[:, t, :], st[:, c:c + 1], None, ALU.mult)
                tt(x[:, t, :], x[:, t, :], gain, ALU.mult, name="block1")
            norm(G_MIX, x)
            gained(G_MIX)
            flat = lambda m: m.rearrange("p a b -> p (a b)")
            b = e.filled("la")
            e.step(v.tensor_copy(flat(la), b[:, :]))
            stt(flat(e1), flat(la), -1.0, flat(la), ALU.mult, ALU.max, name="abs_la")
            e.on("softplus_la")
            stt(flat(la), b[:, :], 0.0, flat(e2), ALU.min, ALU.subtract, turn="la")
            ts(flat(la), flat(la), 1.0 / 16.0, None, ALU.mult, name="la_ready")
            e.after("gb")
            chunks = lambda m: m.rearrange("p f (i c) -> p (f i) c", c=CH)
            col = lambda m, c: chunks(m)[:, :, c:c + 1].broadcast_to([P, 2 * NCH, CH])
            tt(chunks(e1), chunks(bc), col(bc, CH // 2 - 1), ALU.subtract, name="gla_diff")
            tt(chunks(kl), col(bc, CH - 1), chunks(bc), ALU.subtract, name="gla_diff")
            e.on("gla_exp")
            e.on("gla_zeroed", 3)
            e.step(v.tensor_copy(st[:, 432:440].unsqueeze(2), chunks(qb)[:, :, CH - 1:CH]))
            e.after("qkg.0")
            e.after("qkg.1")
            for f in range(2):
                for m in range(2):
                    r = slice(64 * m, 64 * m + 64)
                    stt(qez[r, f, m, :], qg[r, f, :], 0.125, e1[r, f, :], ALU.mult, ALU.mult, name="gla_q")
            tt(flat(e2), flat(e2), flat(kg), ALU.mult, name="gla_k")
            tt(flat(kl), flat(kl), flat(kg), ALU.mult, name="gla_kl")
            stt(flat(qb), flat(qg), 0.125, flat(qb), ALU.mult, ALU.mult, name="gla_qb")
            for j in range(2):
                b = e.filled(f"ga{j}")
                tt(atT[:, 4 * j:4 * j + 4, :], four(b), rep(tile(K_CAUSAL), 4), ALU.mult, turn=f"ga{j}")
            for c in range(NCH - 1):
                b = e.filled(f"kv{c}")
                for f in range(2):
                    for m in range(2):
                        r = slice(64 * m, 64 * m + 64)
                        sl = slice(m * P, (m + 1) * P)
                        d = 432 + f * NCH + c
                        stt(sts[r, c + 1, f, sl], sts[r, c, f, sl], st[r, d:d + 1], b[r, f * T + m * P:f * T + (m + 1) * P],
                            ALU.mult, ALU.add, turn=f"kv{c}" if f and m else None)
            for c in range(NCH):
                e.after(f"go{c}")
            head_norm("gl", heads(0), 232, EPS, rowv[:, R_GLA:R_GLA + 512].rearrange("p (h d) -> p h d", h=H), gnt)
            for t in range(TT):
                e.after(f"rg.{t}")
                tt(hn[:, t, 0:512], hn[:, t, 0:512], zt[:, t, :], ALU.mult, name="mixed1" if t else None)
            attention("mo", 8, False, 0.125)
            for j in (1, 3):
                copy(hT[:, 2 * j:2 * j + 2, :], f"m1.{j}", two)
            for name, z in (("pg", zg), ("pm", zm)):
                for i in range(2):
                    for t in range(TT):
                        sl = z[:, t, i * 512:(i + 1) * 512]
                        e.after(f"{name[:0]}z{name[1]}{i}.{t}")
                        tt(sl, e.filled(f"{name}{i}.{t}")[:, :], sl, ALU.mult, turn=f"{name}{i}.{t}")
                        if name == "pm":
                            sg = zg[:, t, i * 512:(i + 1) * 512]
                            tt(sg, sg, sl, ALU.add, name="merged")
            for j in (1, 3):
                copy(hT[:, 2 * j:2 * j + 2, :], f"m2.{j}", two)
            norm(G_MEM, zm, zm)
            gained(G_MEM, memT)
            residual([(f"res1.{i}.{t}", t, i) for i in range(2) for t in range(TT)])
            norm(G_CROSS, x)
            gained(G_CROSS)
            attention("me", H, True, P ** -0.5)
            copy(hT[:, 2:4, :], "m3.1", two)
            residual([(f"res2.{i}.{t}", t, i) for i in range(2) for t in range(TT)])
            norm(G_MOE, x)
            gained(G_MOE)
            b = e.filled("rt")
            tt(rl[:, :, :], b[:, 0:TT * (NG + NE)].rearrange("p (t n) -> p t n", t=TT),
               rowv[:, R_BG:R_BG + NG + NE].unsqueeze(1).broadcast_to([P, TT, NG + NE]), ALU.add, turn="rt")
            r3 = lambda c, n: ro[:, c:c + TT * n].rearrange("p (t n) -> p t n", t=TT)
            bcast = lambda m, n: m.unsqueeze(2).broadcast_to([P, TT, n])
            rank = lambda n: ro[:, 0:n].unsqueeze(1).broadcast_to([P, TT, n])
            ts(ro[:, 0:8], index[:, 0:8], -1.0, 100.0, ALU.mult, ALU.add)

            def first_best(values, n, top, onehot_):
                e.step(v.tensor_reduce(top, values, AX_X, ALU.max))
                tt(onehot_, values, bcast(top, n), ALU.is_ge)
                tt(onehot_, onehot_, rank(n), ALU.mult)
                e.step(v.tensor_reduce(ro[:, 8:10], onehot_, AX_X, ALU.max))
                tt(onehot_, onehot_, bcast(ro[:, 8:10], n), ALU.is_equal)

            gmax, ohg = ro[:, 10:12], r3(32, NG)
            first_best(rl[:, :, 0:NG], NG, gmax, ohg)
            tt(r3(16, NG), rl[:, :, 0:NG], bcast(gmax, NG), ALU.subtract, name="router_max")
            prod = ro[:, 512:512 + TT * NE].rearrange("p (t g n) -> p t g n", t=TT, g=NG)
            tt(prod, rl[:, :, NG:].rearrange("p t (g n) -> p t g n", g=NG), ohg.unsqueeze(3).broadcast_to([P, TT, NG, EG]), ALU.mult)
            ein = r3(64, EG)
            for t in range(TT):
                e.step(v.tensor_reduce(ein[:, t], prod[:, t].rearrange("p g n -> p n g"), AX_X, ALU.add))
            oh1, oh2, rest = r3(96, EG), r3(128, EG), r3(160, EG)
            m1, m2 = ro[:, 12:14], ro[:, 14:16]
            first_best(ein, EG, m1, oh1)
            stt(rest, oh1, MASKED, ein, ALU.mult, ALU.add)
            first_best(rest, EG, m2, oh2)
            tt(ro[:, 200:202], m2, m1, ALU.subtract, name="router_top")
            e.on("router_exp")
            e.step(v.tensor_reduce(ro[:, 204:206], r3(16, NG), AX_X, ALU.add))
            ts(ro[:, 206:208], ro[:, 200:202], 1.0, None, ALU.add)
            tt(ro[:, 206:208], ro[:, 206:208], ro[:, 204:206], ALU.mult)
            e.step(v.reciprocal(ro[:, 208:210], ro[:, 206:208]))
            tt(ro[:, 210:212], ro[:, 208:210], ro[:, 200:202], ALU.mult)
            tt(oh1, oh1, bcast(ro[:, 208:210], EG), ALU.mult)
            tt(oh2, oh2, bcast(ro[:, 210:212], EG), ALU.mult)
            tt(oh1, oh1, oh2, ALU.add)
            for t in range(TT):
                tt(Wt[:, t, :].rearrange("p (g n) -> p g n", g=NG), ohg[:, t].unsqueeze(2).broadcast_to([P, NG, EG]),
                   oh1[:, t].unsqueeze(1).broadcast_to([P, NG, EG]), ALU.mult)
            with eng.Fori(0, NE // 2) as i:
                for s in range(2):
                    for half in range(2):
                        eng.wait_ge(emptied[half], 2 * i + (base[half] + s + 1))
                        eng.wait_ge(filled[2 + half], 2 * i + (base[2 + half] + s + 1))
                        v.tensor_tensor(ehid[:, s, 2 * half:2 * half + 2, :], two(bank[2 + half]), esil[:, half, :, :], ALU.mult)\
                            .then_inc(emptied[2 + half], 1)
                    for t in range(TT):
                        for half in range(2):
                            bk = 4 + 2 * t + half
                            sl = x[:, t, half * 512:(half + 1) * 512]
                            eng.wait_ge(filled[bk], 2 * i + (base[bk] + s + 1))
                            eng.wait_ge(emptied[bk], 2 * i + (base[bk] + s))
                            v.scalar_tensor_tensor(out=sl, in0=bank[bk][:, :], scalar=Wt[:, t, bass.ds(2 * i + s, 1)], in1=sl,
                                                   op0=ALU.mult, op1=ALU.add).then_inc(emptied[bk], 1)
            for bk in range(4, 8):
                eng.wait_ge(emptied[bk], base[bk] + NE)
            e.step(v.memset(st[:, 508:509], 0.0), "expert_sum")
            norm_scale(7)
            e.on("gain_row", 32)
            for t in range(TT):
                c = 128 + 56 + 4 + t
                ts(x[:, t, :], x[:, t, :], st[:, c:c + 1], None, ALU.mult)
                tt(x[:, t, :], x[:, t, :], gain, ALU.mult, name="result")


def kernel(**inputs):
    import concourse.bacc as bacc
    from concourse.bass_utils import run_bass_kernel_spmd

    nc = bacc.Bacc("TRN2", target_bir_lowering=False, num_devices=1)
    arrays, access = {}, {}
    for name, value in inputs.items():
        value = np.ascontiguousarray(value)
        arrays[f"in_{name}"] = value
        access[name] = nc.dram_tensor(f"in_{name}", value.shape, F32, kind="ExternalInput").ap()
    const = shape_constants()
    arrays["shape_const"] = const
    const_ap = nc.dram_tensor("shape_const", const.shape, F32, kind="ExternalInput").ap()
    result = nc.dram_tensor("out", (1, T, D), F32, kind="ExternalOutput").ap()
    two_blocks(nc, access, const_ap, result)
    ran = run_bass_kernel_spmd(nc, [arrays], core_ids=[0])
    return ran.results[0]["out"]
```

```python
from contextlib import ExitStack

import numpy as np

import concourse.bass as bass
from concourse import mybir

F32 = mybir.dt.float32
ALU = mybir.AluOpType
ACT = mybir.ActivationFunctionType
AX_X = mybir.AxisListType.X

P = 128
T = 256
TT = T // P
D = 1024
KD = D // P
H = 4
CH = 64
NCH = T // CH
HT = H * TT
DFF = 2816
FT = DFF // P
NE = 32
NP = NE // 2
NG = 4
EG = NE // NG
DE = 512
SL = 64
ROUNDS = T // SL
EPS = 1e-6
LAM_INIT = 0.8 - 0.6 * 1.0
MASKED = -1.0e30
SLOTS = 6
RING_A = 5
LEVELS = 5

C_Q, C_K, C_V, C_Z, C_BA, C_QD, C_KD, C_VD = 0, 512, 1024, 1536, 2048, 2056, 2568, 3080
C2_QK, C2_V, C2_R, C2_A, C2_QM, C2_KM, C2_VM, C2_ZG, C2_ZM = 0, 512, 1024, 1536, 1552, 2064, 2576, 3088, 4112

(K_ID, K_ONE, K_CAUSAL, K_STRICT, K_BELOW, K_PAIR, K_BEFORE, K_FLIP) = range(8)
K_LEVEL = 8
N_TILES = K_LEVEL + LEVELS
REL = 384


def shape_constants():
    s, c = np.meshgrid(np.arange(P), np.arange(P), indexing="ij")
    same = s // CH == c // CH
    tiles = [s == c, s >= 0, same & (s <= c), same & (s < c), same & (s > c),
             (s // 2 == c // 2) & (s < c), s < c, s + c == P - 1]
    for level in range(LEVELS):
        w = 2 << level
        tiles.append((s // (2 * w) == c // (2 * w)) & (s % (2 * w) < w) & (c % (2 * w) >= w))
    n = 255 - np.arange(REL)
    past = np.maximum(n, 0)
    far = 16 + (np.log(np.maximum(past, 1) / 16) / np.log(8.0) * 16 + 1e-6).astype(np.int64)
    bucket = np.where(past < 16, past, np.minimum(far, 31))
    table = np.zeros((P, REL))
    table[bucket[n >= 0], np.arange(REL)[n >= 0]] = 1.0
    table[32, n < 0] = MASKED
    index = np.broadcast_to(np.arange(P), (P, P))
    return np.concatenate([t.astype(np.float64) for t in tiles] + [table, index], axis=1).astype(np.float32)


def two_blocks(nc, a, const, out, dump=None):
    stack = ExitStack()
    with stack:
        def sb(name, shape):
            return stack.enter_context(nc.sbuf_tensor(name, shape, F32))

        sems = {}

        def sem(name):
            if name not in sems:
                sems[name] = stack.enter_context(nc.semaphore(name))
            return sems[name]

        ring = sb("ring", [P, RING_A, 4096])
        work = sb("work", [P, 13440])
        x = sb("x", [P, TT, D])
        hn = sb("hn", [P, TT, D])
        hT = sb("hT", [P, KD, T])
        qz = sb("qz", [P, H, 2, T])
        kf = sb("kf", [P, H, T])
        vt = sb("vt", [P, TT, 512])
        zt = sb("zt", [P, TT, 512])
        bias = sb("bias", [P, 8, T])
        cst = sb("cst", [P, N_TILES * P + REL + P])
        rows = sb("rows", [96, P])
        cols = sb("cols", [P, 96])
        relb = sb("relb", [33, 12])
        relr = sb("relr", [12, REL])
        rowv = sb("rowv", [P, 1088])
        w_ba = sb("w_ba", [P, KD, 8])
        w_al = sb("w_al", [P, KD, 16])
        w_up16 = sb("w_up16", [17, 256])
        w_rt = sb("w_rt", [P, KD, NG + NE])
        st = sb("st", [P, 512])
        S = sb("S", [P, H, P])
        over = stack.enter_context(nc.sbuf_tensor("over", [P, 1], mybir.dt.int32))
        rel_dram = nc.dram_tensor("rel_dram", [12, REL], F32, kind="Internal").ap()

        def tile(i):
            return cst[:, i * P:(i + 1) * P]

        ident, ones = tile(K_ID), tile(K_ONE)
        onehot = cst[0:33, N_TILES * P:N_TILES * P + REL]
        index = cst[:, N_TILES * P + REL:]
        G_ATTN, G_FFN, G_MIX, G_CROSS, G_MEM, G_MOE = range(6)
        R_DT, R_A, R_LA, R_DIFF, R_GLA, R_BG, R_BE, R_LAM = 0, 4, 8, 136, 264, 776, 780, 812

        at = [0]

        def area(*shape):
            n = int(np.prod(shape))
            v = work[:, at[0]:at[0] + n]
            at[0] += n
            assert at[0] <= 13440
            if len(shape) == 1:
                return v
            names = "abcd"[:len(shape)]
            return v.rearrange(f"p ({' '.join(names)}) -> p {' '.join(names)}",
                               **{k: s for k, s in zip(names, shape)})

        cvi = area(12, T + 3)
        cv = area(12, T)
        qn, kn, vc = cv[:, 0:4, :], cv[:, 4:8, :], cv[:, 8:12, :]
        dT, eB, aT, LT, Tn, Tt, vnew = (area(HT, P) for _ in range(7))
        at[0] = 0
        vb, kbg, kr = (area(HT, P) for _ in range(3))
        X = hT[:, 0:4, :].rearrange("p a (b c) -> p (a b) c", b=2)
        Ct = hT[:, 4:8, :].rearrange("p a (b c) -> p (a b) c", b=2)
        u, wT = X, Ct
        sqk = dT, eB
        gb, bb = aT, LT
        at[0] = 6180
        sc = area(8, T)
        pT = area(2, 8, P)
        at[0] = 0
        actT = area(FT, T)
        sil = area(2, 2, T)
        at[0] = 6700
        flip = area(8, T)
        at[0] = 0
        qg, kg = area(2, T), area(2, T)
        zg, zm = area(TT, D), area(TT, D)
        gnt = work[:, 5376:6400].rearrange("p (i c) -> p i c", c=P)
        at[0] = 10300
        memT = area(KD, T)
        at[0] = 5120
        alT = area(T)
        la, bc, e1, e2 = area(TT, T), area(2, T), area(2, T), area(2, T)
        kl, qb, qez, klt, atT = area(2, T), area(2, T), area(2, 2, T), area(TT, 2, P), area(HT, P)
        sts = area(NCH, 2, 256)
        at[0] = 0
        slot5 = area(4096)
        pick = area(TT, NE + 2, SL)
        put = area(NE // 2 + 1, T)
        xg = kf.rearrange("p h t -> p (h t)").rearrange("p (k j) -> p k j", k=KD)
        es = vt[:, 1, :]
        eh = vt[:, 0, :].rearrange("p (k j) -> p k j", k=DE // P)
        ys = qz[:, 0:2, :, :].rearrange("p a b t -> p (a b t)")
        pw = hT.rearrange("p (b c) t -> p b (c t)", b=2)
        accT = hT
        eb = bias.rearrange("p h t -> p (h t)")
        Wt, Mk, rk = (eb[:, i * 64:(i + 1) * 64].rearrange("p (t n) -> p t n", t=TT) for i in range(3))
        rl = eb[:, 192:264].rearrange("p (t n) -> p t n", t=TT)
        ro = eb[:, 1024:2048]

        bank = [stack.enter_context(nc.psum_tensor(f"bank{i}", [P, 512], F32)) for i in range(8)]
        filled = [sem(f"filled{i}") for i in range(8)]
        emptied = [sem(f"emptied{i}") for i in range(8)]
        turns = {}
        used = [0] * 8
        order = [0]
        B_G, B_U, B_X, B_ACC = 0, 1, (2, 3), (4, 5, 6, 7)
        B_T, B_Y, PLACE, B_TAIL = B_G, B_X, (B_G, B_U), (0, 1, 2, 3)

        loads = []
        released = {}

        def kp(w):
            return w.rearrange("(k p) n -> p k n", p=P)

        def load(name, src):
            loads.append((name, src))
            return len(loads) - 1

        w_in, w_in2 = kp(a["w_in"][0]), kp(a["w_in_2"][0])
        L = {}
        for name, c0 in (("q", C_Q), ("k", C_K), ("v", C_V), ("z", C_Z), ("qd", C_QD), ("kd", C_KD), ("vd", C_VD)):
            L[name] = load(name, w_in[:, :, c0:c0 + 512])
        for i in range(2):
            L["wo", i] = load("wo", kp(a["w_out"][0])[:, :, i * 512:(i + 1) * 512])
        for j in range(FT // 2):
            L["gu", j] = load("gu", a["w_gate_up"][0].rearrange("(k p) (g n) -> p k g n", p=P, g=2)[:, :, :, j * 256:(j + 1) * 256])
        for j in range(0, FT, 4):
            n = min(4, FT - j)
            L["dn", j] = load("dn", kp(a["w_down"][0])[:, j:j + n, :])
        for name, c0 in (("qkg", C2_QK), ("vg", C2_V), ("rg", C2_R), ("qm", C2_QM), ("km", C2_KM),
                         ("zg0", C2_ZG), ("zg1", C2_ZG + 512), ("zm0", C2_ZM), ("zm1", C2_ZM + 512), ("vm", C2_VM)):
            L[name] = load(name, w_in2[:, :, c0:c0 + 512])
        L["pg"] = load("pg", kp(a["w_proj_gla_2"][0]))
        L["pm"] = load("pm", kp(a["w_proj_moba_2"][0]))
        for i in range(2):
            L["wo2", i] = load("wo2", kp(a["w_out_2"][0])[:, :, i * 512:(i + 1) * 512])
        L["ck"] = load("ck", kp(a["w_ckv_2"][0])[:, :, 0:512])
        L["cv"] = load("cv", kp(a["w_ckv_2"][0])[:, :, 512:1024])
        L["cq"] = load("cq", kp(a["w_cq_2"][0]))
        L["co"] = load("co", kp(a["w_co_2"][0]))
        NA = len(loads)

        def slot(n):
            return ring[:, n % RING_A, :]

        expert_slots = [RING_A] + sorted(range(RING_A), key=lambda r: max(n for n in range(NA) if n % RING_A == r))

        def eslot(m, s):
            j = expert_slots[2 * m + s]
            return ring[:, j, :] if j < RING_A else slot5

        loaded = [sem(f"loaded{i}") for i in range(RING_A)]

        def pieces(n):
            return 2 if loads[n][0] == "gu" else 1

        def wait_load(eng, n):
            eng.wait_ge(loaded[n % RING_A], 16 * sum(pieces(m) for m in range(n % RING_A, n + 1, RING_A)))

        class Engine:

            def __init__(self, eng, name):
                self.eng, self.own, self.count = eng, name, {}

            def step(self, ins, name=None):
                name = name or self.own
                self.count[name] = self.count.get(name, 0) + 1
                ins.then_inc(sem(name), 1)
                self.eng.wait_ge(sem(name), self.count[name])

            def filled(self, turn):
                b, k = turns[turn]
                self.eng.wait_ge(filled[b], k)
                return bank[b]

            def empty(self, ins, turn):
                b, k = turns[turn]
                ins.then_inc(emptied[b], 1)
                self.eng.wait_ge(emptied[b], k)

            def on(self, name, value=1):
                self.eng.wait_ge(sem(name), value)

            def after(self, turn):
                b, k = turns[turn]
                self.eng.wait_ge(emptied[b], k)

        N_SMALL = 26
        block = stack.enter_context(nc.Block())

        @block.tensor
        def _(eng):
            mm, tr = nc.tensor.matmul, nc.tensor.transpose
            e = Engine(eng, "pe_step")

            def begin(name):
                b = order[0] % 8
                order[0] += 1
                used[b] += 1
                turns[name] = (b, used[b])
                if used[b] > 1:
                    eng.wait_ge(emptied[b], used[b] - 1)
                return bank[b]

            def end(ins, name):
                ins.then_inc(filled[turns[name][0]], 1)

            def release(n, turn):
                b, k = turns[turn]
                released[n] = (filled[b], k)

            def transposes(name, pieces):
                b = begin(name)
                for i, piece in enumerate(pieces):
                    ins = tr(b[:, i * P:(i + 1) * P], piece, ident)
                end(ins, name)

            def norm_transposed(n):
                for j in range(4):
                    if j == 0:
                        e.on(f"normed{n}", TT)
                    transposes(f"hT{n}.{j}", [hn[:, t, k * P:(k + 1) * P] for k in (2 * j, 2 * j + 1) for t in range(TT)])

            def normed(n):
                for j in range(4):
                    e.after(f"hT{n}.{j}")

            def features(name, w, src, n, tiles=4, kk=KD):
                for half in range(tiles // 2):
                    b = begin(f"{name}.{half}")
                    for f in range(2):
                        for k in range(kk):
                            ins = mm(b[:, f * T:(f + 1) * T], w[:, k, (2 * half + f) * P:(2 * half + f + 1) * P],
                                     src[:, k, :], start=k == 0, stop=k == kk - 1)
                    end(ins, f"{name}.{half}")
                release(n, f"{name}.{half}")

            def tokens(name, w, src, n, kk=KD):
                for t in range(TT):
                    b = begin(f"{name}.{t}")
                    for k in range(kk):
                        ins = mm(b[:, :], src[:, k, t * P:(t + 1) * P], w[:, k, :], start=k == 0, stop=k == kk - 1)
                    end(ins, f"{name}.{t}")
                release(n, f"{name}.{t}")

            def slot8(n):
                wait_load(eng, n)
                return slot(n).rearrange("p (k n) -> p k n", k=KD)

            def attention(kind, maps, full):
                for t in range(TT):
                    nk = TT if full else t + 1
                    per = 512 // (nk * P)
                    for m0 in range(0, maps, per):
                        b = begin(f"{kind}s{t}.{m0}")
                        for m in range(m0, m0 + per):
                            q = qz[:, m // 2, m % 2, :] if not full else qz[:, m, 0, :]
                            k = kf[:, m // 2, :] if not full else kf[:, m, :]
                            ins = mm(b[:, (m - m0) * nk * P:(m - m0 + 1) * nk * P], q[:, t * P:(t + 1) * P],
                                     k[:, 0:nk * P], start=True, stop=True)
                        end(ins, f"{kind}s{t}.{m0}")
                    pm = 4 if kind == "df" else maps
                    e.on(f"{kind}_p", t + 1)
                    for kt in range(nk):
                        for m0 in range(0, pm, 4):
                            step = 2 if kind == "df" else 1
                            transposes(f"{kind}t{t}.{kt}.{m0}", [sc[:, m * step, kt * P:(kt + 1) * P] for m in range(m0, m0 + 4)])
                    b = begin(f"{kind}o{t}")
                    dv = 512 // pm
                    for kt in range(nk):
                        for m0 in range(0, pm, 4):
                            e.after(f"{kind}t{t}.{kt}.{m0}")
                    for m in range(pm):
                        for kt in range(nk):
                            ins = mm(b[:, m * dv:(m + 1) * dv], pT[:, kt, m, :], vt[:, kt, m * dv:(m + 1) * dv],
                                     start=kt == 0, stop=kt == nk - 1)
                    end(ins, f"{kind}o{t}")

            e.on("consts", 16)
            e.on("small", 16 * N_SMALL)
            b = begin("cols")
            end(tr(b[:, 0:96], rows[:, :], ident[0:96, 0:96]), "cols")
            b = begin("rel")
            e.on("relb_one")
            end(mm(b[0:12, 0:REL], relb[:, :], onehot, start=True, stop=True), "rel")

            norm_transposed(G_ATTN)
            normed(G_ATTN)
            b = begin("ba")
            for t in range(TT):
                for k in range(KD):
                    ins = mm(b[:, t * 8:(t + 1) * 8], hT[:, k, t * P:(t + 1) * P], w_ba[:, k, :], start=k == 0, stop=k == KD - 1)
            end(ins, "ba")
            for name in ("q", "k", "v"):
                features(name, slot8(L[name]), hT, L[name])
            tokens("z", slot8(L["z"]), hT, L["z"])
            for name in ("qd", "kd"):
                features(name, slot8(L[name]), hT, L[name])
            tokens("vd", slot8(L["vd"]), hT, L["vd"])

            for i in range(4):
                e.on("squares", i // 2 + 1)
                b = begin(f"ss{i}")
                end(mm(b[:, :], ones, sqk[i // 2][:, (i % 2) * 4:(i % 2) * 4 + 4, :], start=True, stop=True), f"ss{i}")
            e.on("g_wide")
            for j in range(2):
                b = begin(f"B{j}")
                for i in range(4):
                    ins = mm(b[:, i * P:(i + 1) * P], gb[:, 4 * j + i, :], tile(K_CAUSAL), start=True, stop=True)
                end(ins, f"B{j}")
            b = begin("gcol")
            mm(b[:, 0:HT], tile(K_CAUSAL), st[:, 0:HT], start=True, stop=True)
            end(mm(b[:, HT:2 * HT], tile(K_BELOW), st[:, 0:HT], start=True, stop=True), "gcol")
            e.on("beta_wide")
            for j in range(2):
                b = begin(f"beta{j}")
                for i in range(4):
                    ins = mm(b[:, i * P:(i + 1) * P], bb[:, 4 * j + i, :], ident, start=True, stop=True)
                end(ins, f"beta{j}")
            e.on("q_normed", 2)
            e.on("k_normed", 2)
            for name, src in (("kk", kn), ("qk", qn)):
                for j in range(2):
                    b = begin(f"{name}{j}")
                    for i in range(4):
                        h, t = (4 * j + i) // TT, i % TT
                        ins = mm(b[:, i * P:(i + 1) * P], kn[:, h, t * P:(t + 1) * P], src[:, h, t * P:(t + 1) * P],
                                 start=True, stop=True)
                    end(ins, f"{name}{j}")
            for name, src in (("vtr", vc), ("ktr", kn)):
                for j in range(2):
                    transposes(f"{name}{j}", [src[:, (4 * j + i) // TT, (i % TT) * P:(i % TT + 1) * P] for i in range(4)])
            e.on("pairs")
            for j in range(2):
                transposes(f"T0{j}", [Tt[:, 4 * j + i, :] for i in range(4)])
            for level in range(LEVELS):
                e.on("lower", level + 1)
                for j in range(2):
                    if level == 0:
                        e.after(f"T0{j}")
                    else:
                        e.after(f"Dt{level - 1}.{j}")
                        e.after(f"Dn{level - 1}.{j}")
                    b = begin(f"X{level}.{j}")
                    for i in range(4):
                        ins = mm(b[:, i * P:(i + 1) * P], Ct[:, 4 * j + i, :], Tn[:, 4 * j + i, :], start=True, stop=True)
                    end(ins, f"X{level}.{j}")
                for j in range(2):
                    e.after(f"X{level}.{j}")
                    for side in ("t", "n") if level < LEVELS - 1 else ("t",):
                        b = begin(f"D{side}{level}.{j}")
                        for i in range(4 * j, 4 * j + 4):
                            l, r = (X, Tt) if side == "t" else (Tt, X)
                            ins = mm(b[:, (i % 4) * P:(i % 4 + 1) * P], l[:, i, :], r[:, i, :], start=True, stop=True)
                        end(ins, f"D{side}{level}.{j}")
            e.after(f"Dt{LEVELS - 1}.0")
            e.after(f"Dt{LEVELS - 1}.1")
            e.on("k_scaled")
            for j in range(2):
                b = begin(f"u{j}")
                for i in range(4):
                    ins = mm(b[:, i * P:(i + 1) * P], Tt[:, 4 * j + i, :], vb[:, 4 * j + i, :], start=True, stop=True)
                end(ins, f"u{j}")
                b = begin(f"w{j}")
                for i in range(4):
                    ins = mm(b[:, i * P:(i + 1) * P], kbg[:, 4 * j + i, :], Tt[:, 4 * j + i, :], start=True, stop=True)
                end(ins, f"w{j}")
            e.after("w0")
            e.after("w1")
            e.on("q_scaled")
            e.on("state")
            qs = qn.rearrange("p h (t c) -> p (h t) c", t=TT)
            for c in range(NCH):
                t, lo = c // 2, (c % 2) * CH
                if c:
                    e.after(f"dS{c - 1}")
                b = begin(f"wS{c}")
                for h in range(H):
                    ins = mm(b[:, h * P:(h + 1) * P], wT[:, h * TT + t, :], S[:, h, :], start=True, stop=True)
                end(ins, f"wS{c}")
                e.after(f"wS{c}")
                if c < NCH - 1:
                    b = begin(f"dS{c}")
                    for h in range(H):
                        ins = mm(b[:, h * P:(h + 1) * P], kr[lo:lo + CH, h * TT + t, :], vnew[lo:lo + CH, h * TT + t, :],
                                 start=True, stop=True)
                    end(ins, f"dS{c}")
                b = begin(f"o{c}")
                for h in range(H):
                    mm(b[:, h * P:(h + 1) * P], qs[:, h * TT + t, :], S[:, h, :], start=True, stop=False)
                    ins = mm(b[:, h * P:(h + 1) * P], aT[:, h * TT + t, :], vnew[:, h * TT + t, :], start=False, stop=True)
                end(ins, f"o{c}")

            def unflip(n, src, heads):
                e.on("bias_in", 16 * n)
                for h in range(0, heads, 2):
                    b = begin(f"bias{n}.{h}")
                    end(mm(b[:, :], tile(K_FLIP), src[:, h:h + 2, :], start=True, stop=True), f"bias{n}.{h}")

            unflip(1, bias[:, 4:8, :], H)
            e.after("qd.0"); e.after("qd.1"); e.after("kd.0"); e.after("kd.1"); e.after("vd.0"); e.after("vd.1")
            attention("df", 8, False)

            def mixed(n, parts, w_names, name):
                e.on(f"mixed{n}", parts)
                for j in range(4):
                    transposes(f"m{n}.{j}", [hn[:, t, k * P:(k + 1) * P] for k in (2 * j, 2 * j + 1) for t in range(TT)])
                for j in range(4):
                    e.after(f"m{n}.{j}")
                for i in range(2):
                    tokens(f"{name}{i}", slot8(L[w_names, i]), hT, L[w_names, i])

            mixed(0, 2, "wo", "res0.")
            unflip(2, flip, 8)
            norm_transposed(G_FFN)
            normed(G_FFN)
            for j in range(FT // 2):
                n = L["gu", j]
                wait_load(eng, n)
                w = slot(n).rearrange("p (k g n) -> p k g n", k=KD, g=2)
                for g in range(2):
                    b = begin(f"gu{j}.{g}")
                    for f in range(2):
                        for k in range(KD):
                            ins = mm(b[:, f * T:(f + 1) * T], w[:, k, g, f * P:(f + 1) * P], hT[:, k, :], start=k == 0, stop=k == KD - 1)
                    end(ins, f"gu{j}.{g}")
                release(n, f"gu{j}.1")
            banks = [begin(f"dn{i}") for i in range(4)]
            for j0 in range(0, FT, 4):
                n = L["dn", j0]
                wait_load(eng, n)
                w = slot(n).rearrange("p (k n) -> p k n", k=4)
                for j in range(j0, min(j0 + 4, FT)):
                    if j % 2 == 0:
                        e.after(f"gu{j // 2}.1")
                for i in range(4):
                    t, half = i // 2, i % 2
                    for j in range(j0, min(j0 + 4, FT)):
                        ins = mm(banks[i][:, :], actT[:, j, t * P:(t + 1) * P], w[:, j - j0, half * 512:(half + 1) * 512],
                                 start=j == 0, stop=j == FT - 1)
                    if j0 + 4 >= FT:
                        end(ins, f"dn{i}")
                if j0 + 4 < FT:
                    ins.then_inc(sem("down_used"), 1)
                    released[n] = (sem("down_used"), j0 // 4 + 1)
                else:
                    release(n, "dn3")

            norm_transposed(G_MIX)
            normed(G_MIX)
            features("qkg", slot8(L["qkg"]), hT, L["qkg"])
            b = begin("al")
            for k in range(KD):
                ins = mm(b[0:16, 0:T], w_al[:, k, :], hT[:, k, :], start=k == 0, stop=k == KD - 1)
            end(ins, "al")
            tokens("vg", slot8(L["vg"]), hT, L["vg"])
            e.after("al")
            e.on("gla_zeroed", 3)
            b = begin("la")
            for t in range(TT):
                ins = mm(b[:, t * T:(t + 1) * T], alT[0:17, t * P:(t + 1) * P], w_up16[:, :], start=True, stop=True)
            end(ins, "la")
            tokens("rg", slot8(L["rg"]), hT, L["rg"])
            e.on("la_ready")
            b = begin("gb")
            for f in range(2):
                for t in range(TT):
                    ins = mm(b[:, f * T + t * P:f * T + (t + 1) * P], la[:, t, f * P:(f + 1) * P], tile(K_CAUSAL), start=True, stop=True)
            end(ins, "gb")
            for name in ("qm", "km"):
                features(name, slot8(L[name]), hT, L[name])
            for name in ("zg0", "zg1", "zm0", "zm1"):
                tokens(name, slot8(L[name]), hT, L[name])
            e.on("gla_q", 4)
            e.on("gla_k")
            for j in range(2):
                b = begin(f"ga{j}")
                for i in range(4):
                    h, t = (4 * j + i) // TT, i % TT
                    ins = mm(b[:, i * P:(i + 1) * P], e2[:, h // 2, t * P:(t + 1) * P], qez[:, h // 2, h % 2, t * P:(t + 1) * P],
                             start=True, stop=True)
                end(ins, f"ga{j}")
            e.on("gla_kl")
            transposes("klt", [kl[:, f, t * P:(t + 1) * P] for t in range(TT) for f in range(2)])
            e.after("klt")
            e.after("vg.0"); e.after("vg.1")
            e.after("ga0"); e.after("ga1")
            e.on("gla_qb")
            for c in range(NCH):
                t, lo = c // 2, (c % 2) * CH
                if c < NCH - 1:
                    b = begin(f"kv{c}")
                    for f in range(2):
                        ins = mm(b[:, f * T:(f + 1) * T], klt[lo:lo + CH, t, f, :], vt[lo:lo + CH, t, f * T:(f + 1) * T], start=True, stop=True)
                    end(ins, f"kv{c}")
            for c in range(NCH):
                t = c // 2
                if c:
                    e.after(f"kv{c - 1}")
                b = begin(f"go{c}")
                for f in range(2):
                    mm(b[:, f * T:(f + 1) * T], qb[:, f, t * P:(t + 1) * P], sts[:, c, f, :], start=True, stop=False)
                    for h in (2 * f, 2 * f + 1):
                        ins = mm(b[:, h * P:(h + 1) * P], atT[:, h * TT + t, :], vt[:, t, h * P:(h + 1) * P], start=False, stop=h % 2 == 1)
                end(ins, f"go{c}")
            tokens("vm", slot8(L["vm"]), hT, L["vm"])
            e.after("qm.0"); e.after("qm.1"); e.after("km.0"); e.after("km.1"); e.after("vm.0"); e.after("vm.1")
            attention("mo", 8, False)

            def half_transposed(name, c0):
                for j in range(2):
                    transposes(f"{name}.{j}", [hn[:, t, c0 + k * P:c0 + (k + 1) * P] for k in (2 * j, 2 * j + 1) for t in range(TT)])
                for j in range(2):
                    e.after(f"{name}.{j}")

            def half_product(name, n, src, k0):
                wait_load(eng, n)
                w = slot(n).rearrange("p (k n) -> p k n", k=4)
                for i in range(2):
                    for t in range(TT):
                        b = begin(f"{name}{i}.{t}")
                        for k in range(4):
                            ins = mm(b[:, :], src[:, k0 + k, t * P:(t + 1) * P], w[:, k, i * 512:(i + 1) * 512], start=k == 0, stop=k == 3)
                        end(ins, f"{name}{i}.{t}")
                release(n, f"{name}1.1")

            e.on("mixed1")
            for c0, k0 in ((0, 0), (512, 2)):
                if c0:
                    e.after("moo0"); e.after("moo1")
                for j in range(2):
                    transposes(f"m1.{k0 + j}", [hn[:, t, c0 + k * P:c0 + (k + 1) * P] for k in (2 * j, 2 * j + 1) for t in range(TT)])
            for j in range(4):
                e.after(f"m1.{j}")
            half_product("pg", L["pg"], hT, 0)
            half_product("pm", L["pm"], hT, 4)
            e.on("merged", 4)
            for j in range(4):
                transposes(f"m2.{j}", [zg[:, t, k * P:(k + 1) * P] for k in (2 * j, 2 * j + 1) for t in range(TT)])
            for j in range(4):
                e.after(f"m2.{j}")
            for i in range(2):
                tokens(f"res1.{i}", slot8(L["wo2", i]), hT, L["wo2", i])

            e.on(f"normed{G_MEM}", TT)
            for j in range(4):
                transposes(f"hT{G_MEM}.{j}", [zm[:, t, k * P:(k + 1) * P] for k in (2 * j, 2 * j + 1) for t in range(TT)])
            normed(G_MEM)
            features("ck", slot8(L["ck"]), memT, L["ck"])
            tokens("cv", slot8(L["cv"]), memT, L["cv"])
            norm_transposed(G_CROSS)
            normed(G_CROSS)
            features("cq", slot8(L["cq"]), hT, L["cq"])
            e.after("cq.0"); e.after("cq.1"); e.after("ck.0"); e.after("ck.1"); e.after("cv.0"); e.after("cv.1")
            attention("me", H, True)
            e.after("meo0"); e.after("meo1")
            half_transposed("m3", 512)
            half_product("res2.", L["co"], hT, 0)

            norm_transposed(G_MOE)
            normed(G_MOE)
            b = begin("rt")
            for t in range(TT):
                for k in range(KD):
                    ins = mm(b[:, t * (NG + NE):(t + 1) * (NG + NE)], hT[:, k, t * P:(t + 1) * P], w_rt[:, k, :], start=k == 0, stop=k == KD - 1)
            end(ins, "rt")
            e.on("masked")
            b = begin("rank")
            mm(b[:, 0:NE], tile(K_BEFORE), Mk[:, 0, :], start=True, stop=True)
            mm(b[:, NE:2 * NE], ones, Mk[:, 0, :], start=True, stop=False)
            mm(b[:, NE:2 * NE], tile(K_BEFORE), Mk[:, 1, :], start=False, stop=True)
            mm(b[:, 2 * NE:3 * NE], ones, Mk[:, 0, :], start=True, stop=False)
            end(mm(b[:, 2 * NE:3 * NE], ones, Mk[:, 1, :], start=False, stop=True), "rank")

            def places(r):
                eng.wait_ge(sem("hidden"), NP * r + 1)
                for g in range(4):
                    eng.wait_ge(sem("weighted"), 4 * r + (g + 1))
                    for t in range(TT):
                        bk = PLACE[t]
                        eng.wait_ge(sem(f"placed{t}"), 4 * r + (g + 1))
                        for i in range(4):
                            ins = tr(bank[bk][:, i * P:(i + 1) * P], pw[:, g % 2, t * 512 + i * P:t * 512 + (i + 1) * P], ident)
                        ins.then_inc(sem(f"place{t}"), 1)

            def gather(r, i):
                for k in range(KD):
                    for t in range(TT):
                        rhs = pick[:, t, bass.ds(2 * i, 2), :].rearrange("p o j -> p (o j)")
                        ins = mm(bank[B_X[k // 4]][:, (k % 4) * P:(k % 4 + 1) * P], hn[:, t, k * P:(k + 1) * P], rhs,
                                 start=t == 0, stop=t == TT - 1)
                    if k % 4 == 3:
                        ins.then_inc(sem("gathered"), 1)

            def column_pair(out, lhs, weights, kk, half=0):
                for k in range(kk):
                    for s in range(2):
                        ins = mm(out[SL * s:SL * s + SL, :], lhs[:, k, SL * s:SL * s + SL], weights[s][:, k, half * 512:(half + 1) * 512],
                                 start=k == 0, stop=k == kk - 1)
                return ins

            def gate_up(r, i):
                n = NP * r + i
                eng.wait_ge(sem("gathered_out"), 2 * (NP + 1) * r + 2 * i + 2)
                eng.wait_ge(sem("hidden"), n + 1)
                for m in range(2):
                    for s in range(2):
                        eng.wait_ge(sem(f"expert_in{2 * m + s}"), 16 * n + 16)
                    w = [eslot(m, s).rearrange("p (k n) -> p k n", k=KD) for s in range(2)]
                    column_pair(bank[(B_G, B_U)[m]], xg, w, KD).then_inc(sem(("gate_done", "up_done")[m]), 1)

            def turn_hidden(r, i):
                eng.wait_ge(sem("h_ready"), NP * r + i + 1)
                for f in range(DE // P):
                    ins = tr(bank[B_T][:, f * P:(f + 1) * P], es[:, f * P:(f + 1) * P], ident)
                ins.then_inc(sem("turned"), 1)

            def down(r, i):
                n = NP * r + i
                eng.wait_ge(sem("gathered_out"), 2 * (NP + 1) * r + 2 * i + 4)
                eng.wait_ge(sem("hidden"), n + 2)
                for s in range(2):
                    eng.wait_ge(sem(f"expert_in{4 + s}"), 16 * n + 16)
                w = [eslot(2, s).rearrange("p (k n) -> p k n", k=DE // P) for s in range(2)]
                for half in range(2):
                    column_pair(bank[B_Y[half]], eh, w, DE // P, half).then_inc(sem("y_done"), 1)

            def scatter(r, i):
                n = NP * r + i
                eng.wait_ge(sem("y_out_a"), n + 1)
                eng.wait_ge(sem("y_out_v"), n + 1)
                for k in range(KD):
                    rhs = put[:, i, :] if isinstance(i, int) else put[:, bass.ds(i, 1), :].rearrange("p o t -> p (o t)")
                    mm(bank[B_ACC[k // 2]][:, (k % 2) * T:(k % 2 + 1) * T], ys[:, k * P:(k + 1) * P], rhs,
                       start=False, stop=False, skip_group_check=True)

            def round_(r):
                places(r)
                for t in range(TT):
                    eng.wait_ge(sem(f"placed{t}"), 4 * r + 5)
                eng.wait_ge(sem("picked"), TT * r + TT)
                eng.wait_ge(sem("y_out_a"), NP * r + 1)
                eng.wait_ge(sem("y_out_v"), NP * r + 1)
                gather(r, 0)
                with eng.Fori(0, NP) as i:
                    gate_up(r, i)
                    scatter(r, i)
                    gather(r, i + 1)
                    turn_hidden(r, i)
                    down(r, i)
                scatter(r, NP)

            for bk in range(8):
                eng.wait_ge(emptied[bk], used[bk])
            e.on("credits")
            e.on("moe_zeroed", 3)
            for k in range(KD):
                for t in range(TT):
                    ins = mm(bank[B_ACC[k // 2]][:, (k % 2) * T + t * P:(k % 2) * T + (t + 1) * P], x[:, t, k * P:(k + 1) * P], ident,
                             start=k % 2 == 0 and t == 0, stop=False, skip_group_check=True)
            round_(0)
            e.on("over_known")
            flag = eng.value_load(over[0:1, 0:1], min_val=0, max_val=1)
            with eng.If(flag > 0):
                with eng.Fori(1, ROUNDS) as r:
                    round_(r)
            for k in range(KD // 2):
                ins = mm(bank[B_ACC[k]][:, 0:2], ones, put[:, 0, 0:2], start=False, stop=True, skip_group_check=True)
            ins.then_inc(sem("sum_done"), 1)
            e.on("sum_out_a", 2)
            e.on("sum_out_v", 2)
            for k in range(2):
                for t in range(TT):
                    bk = B_TAIL[2 * t + k]
                    for i in range(4):
                        ins = tr(bank[bk][:, i * P:(i + 1) * P], accT[:, 4 * k + i, t * P:(t + 1) * P], ident)
                    ins.then_inc(sem("sum_back"), 1)

        @block.sync
        def _(eng):
            eng.dma_start(x[:, :, :], a["x"][0].rearrange("(t p) d -> p t d", p=P)).then_inc(sem("x_in"), 16)
            for n, (name, src) in enumerate(loads):
                if n >= RING_A:
                    s, v = released[n - RING_A]
                    eng.wait_ge(s, v)
                dst = slot(n)
                if name == "gu":
                    w = dst.rearrange("p (k g n) -> p k g n", k=KD, g=2)
                    for g in range(2):
                        eng.dma_start(w[:, :, g, :], src[:, :, g, :]).then_inc(loaded[n % RING_A], 16)
                    continue
                k, c = src.shape[1], src.shape[2]
                eng.dma_start(dst[:, 0:k * c].rearrange("p (k n) -> p k n", k=k), src).then_inc(loaded[n % RING_A], 16)
            wg, wu, wd = (a[f"w_exp_{m}_2"][0] for m in ("gate", "up", "down"))

            def expert(m, s, at_):
                w = (wg, wu, wd)[m]
                eng.dma_start(eslot(m, s).rearrange("p (k n) -> p k n", k=w.shape[1] // P),
                              w[at_].rearrange("o (k p) n -> p (o k) n", p=P)).then_inc(sem(f"expert_in{2 * m + s}"), 16)

            for m in range(3):
                for s in range(2):
                    j = expert_slots[2 * m + s]
                    if j < RING_A:
                        sem_, value = released[max(n for n in range(NA) if n % RING_A == j)]
                        eng.wait_ge(sem_, value)
                    else:
                        bk, k = turns[f"hT{G_MEM}.3"]
                        eng.wait_ge(filled[bk], k)
                    expert(m, s, slice(s, s + 1))

            def refill(number, n):
                for m in range(3):
                    for s in range(2):
                        eng.wait_ge(sem(("gate_done", "up_done", "y_done")[m]), 2 * n if m == 2 else n)
                        expert(m, s, bass.ds(number + s, 1))

            with eng.Fori(0, NP - 1) as i:
                refill(2 * i + 2, i + 1)
            eng.wait_ge(sem("over_known"), 1)
            flag = eng.value_load(over[0:1, 0:1], min_val=0, max_val=1)
            with eng.If(flag > 0):
                with eng.Fori(1, ROUNDS) as r:
                    with eng.Fori(0, NP) as i:
                        refill(2 * i, NP * r + i)
            eng.wait_ge(sem("result"), TT)
            eng.dma_start(out[0].rearrange("(t p) d -> p t d", p=P), x[:, :, :]).then_inc(sem("out"), 16)
            eng.wait_ge(sem("out"), 16)

        @block.gpsimd
        def _(eng):
            g = nc.gpsimd
            g.memset(qz[64:128, :, 0, :], 0.0).then_inc(sem("zeroed"), 1)
            eng.wait_ge(sem("zeroed"), 1)
            g.memset(qz[0:64, :, 1, :], 0.0).then_inc(sem("zeroed"), 1)
            eng.wait_ge(sem("zeroed"), 2)
            g.memset(cvi[:, :, 0:3], 0.0).then_inc(sem("zeroed"), 1)
            eng.wait_ge(sem("zeroed"), 3)
            g.memset(relb[32:33, :], 1.0).then_inc(sem("relb_one"), 1)
            eng.wait_ge(sem("relb_one"), 1)
            g.memset(S[:, :, :], 0.0).then_inc(sem("state"), 1)
            eng.wait_ge(sem("state"), 1)
            eng.wait_ge(emptied[turns["rel"][0]], turns["rel"][1])
            eng.dma_start(rel_dram[:, :], relr[:, :]).then_inc(sem("rel_stored"), 16)
            eng.wait_ge(sem("rel_stored"), 16)

            def biases(dst, h0, n):
                src = bass.AP(tensor=rel_dram.tensor, offset=rel_dram.offset + h0 * REL, ap=[[1, P], [REL, n], [1, T]])
                eng.dma_start(dst, src).then_inc(sem("bias_in"), 16)

            biases(bias[:, 4:8, :], 0, 4)
            gain = zt.rearrange("p t d -> p (t d)")
            eng.wait_ge(sem("mixed0"), 1)
            eng.dma_start(gain, a["final_norm_w"].rearrange("(o n) -> o n", o=1).broadcast_to([P, D])).then_inc(sem("gain_row"), 16)
            eng.wait_ge(sem("mixed0"), 2)
            biases(flip, 4, 8)
            eng.wait_ge(sem("block1"), 2)
            g.memset(alT[0:32, :], 1.0).then_inc(sem("gla_zeroed"), 1)
            eng.wait_ge(sem("gla_zeroed"), 1)
            g.memset(qez[:, :, :, :], 0.0).then_inc(sem("gla_zeroed"), 1)
            eng.wait_ge(sem("gla_zeroed"), 2)
            g.memset(sts[:, :, :, :], 0.0).then_inc(sem("gla_zeroed"), 1)
            eng.wait_ge(sem("gla_zeroed"), 3)
            eng.wait_ge(sem("merged"), 4)
            eng.dma_start(zm, a["mem_2"][0].rearrange("(t p) d -> p t d", p=P)).then_inc(sem("mem_in"), 16)
            eng.wait_ge(sem("mixed1"), 1)
            eng.dma_start(gain, a["g_final_2"].rearrange("(o n) -> o n", o=1).broadcast_to([P, D])).then_inc(sem("gain_row"), 16)

        @block.scalar
        def _(eng):
            e = Engine(eng, "act_step")

            def act(out, in_, func, name=None, turn=None, **kw):
                ins = nc.scalar.activation(out, in_, func, **kw)
                if turn:
                    e.empty(ins, turn)
                else:
                    e.step(ins, name)

            nsmall = [0]

            def small(dst, src):
                eng.dma_start(dst, src).then_inc(sem("small"), 16)
                nsmall[0] += 1

            eng.dma_start(cst[:, :], const).then_inc(sem("consts"), 16)
            for i, name in enumerate(("attn_norm_w", "ffn_norm_w", "g_mix_2", "g_cross_2", "g_mem_2", "g_moe_2")):
                v = a[name] if name == "g_mem_2" else a[name][0]
                small(rows[i * KD:(i + 1) * KD, :], v.rearrange("(k p) -> k p", p=P))
            small(rows[48:96, :], a["conv_w"][0].rearrange("i (f p) -> (i f) p", p=P))
            small(relb[0:32, 0:4], a["rel_bias"])
            small(relb[0:32, 4:12], a["rel_bias_2"])

            def row(c0, n, v):
                small(rowv[:, c0:c0 + n], v.rearrange("(o n) -> o n", o=1).broadcast_to([P, n]))

            row(R_DT, 4, a["dt_bias"][0])
            row(R_A, 4, a["a_log"][0])
            row(R_LA, 128, a["la_norm_w"][0])
            row(R_DIFF, 128, a["diff_norm_w"][0])
            row(R_GLA, 512, a["g_gla_head_2"][0].rearrange("h d -> (h d)"))
            row(R_BG, NG, a["b_router_group_2"][0])
            row(R_BE, NE, a["b_router_expert_2"][0])
            for i, name in enumerate(("lambda_q1", "lambda_q2", "lambda_k1", "lambda_k2")):
                row(R_LAM + 64 * i, 64, a[name][0])
            small(w_ba[:, :, :], w_in[:, :, C_BA:C_BA + 8])
            small(w_al[:, :, :], w_in2[:, :, C2_A:C2_A + 16])
            small(w_up16[0:16, :], a["w_alpha_up_2"][0])
            small(w_up16[16:17, :], a["b_alpha_2"])
            small(w_rt[:, :, 0:NG], kp(a["w_router_group_2"][0]))
            small(w_rt[:, :, NG:], kp(a["w_router_expert_2"][0]))
            assert nsmall[0] == N_SMALL, nsmall

            def norm(n, src, junk=hn, ready=None):
                if ready:
                    e.on(*ready)
                c = 128 + 8 * n
                for t in range(TT):
                    act(junk[:, t, :], src[:, t, :], ACT.Square, f"ssq{n}", accum_out=st[:, c + t:c + t + 1])
                e.on(f"mean{n}")
                act(st[:, c + 4:c + 6], st[:, c + 2:c + 4], ACT.Ln)
                act(st[:, c + 4:c + 6], st[:, c + 4:c + 6], ACT.Exp, f"rstd{n}", scale=-0.5)

            def gained(n, hT=hT):
                for j in (0, 2):
                    b = e.filled(f"hT{n}.{j}")
                    for i in range(2):
                        k = 2 * j + i
                        act(hT[:, k, :], b[:, i * T:(i + 1) * T], ACT.Copy, turn=f"hT{n}.{j}" if i else None,
                            scale=cols[:, n * KD + k:n * KD + k + 1])

            def copy(dst, turn, view=None, func=ACT.Copy, **kw):
                b = e.filled(turn)
                act(dst, view(b) if view else b[:, :], func, turn=turn, **kw)

            def two(b):
                return b.rearrange("p (f t) -> p f t", f=2)

            def four(b):
                return b.rearrange("p (i c) -> p i c", i=4)

            def queries(turn, h0):
                b = e.filled(turn)
                act(qz[0:64, h0:h0 + 2, 0, :], two(b[0:64, :]), ACT.Copy)
                act(qz[64:128, h0:h0 + 2, 1, :], two(b[64:128, :]), ACT.Copy, turn=turn)

            def softmax(kind, maps, full):
                c = {"df": 300, "mo": 332, "me": 364}[kind]
                for t in range(TT):
                    w = T if full else (t + 1) * P
                    e.on(f"{kind}_max", t + 1)
                    for m in range(maps):
                        last = m == maps - 1
                        act(sc[:, m, 0:w], sc[:, m, 0:w], ACT.Exp,
                            (f"{kind}_e" if kind == "df" else f"{kind}_p") if last else None,
                            bias=st[:, c + m:c + m + 1], accum_out=st[:, c + 16 + m:c + 17 + m])
                    pm = 4 if kind == "df" else maps
                    for kt in range(w // P):
                        for m0 in range(0, pm, 4):
                            if (kt + m0 // 4) % 2 == 0:
                                copy(pT[:, kt, m0:m0 + 4, :], f"{kind}t{t}.{kt}.{m0}", four)
                    if kind == "df":
                        copy(hn[:, t, 512:1024], f"dfo{t}")

            def head_rstd(name, c, n):
                e.on(f"{name}_ms")
                act(st[:, c + n:c + 2 * n], st[:, c:c + n], ACT.Ln)
                act(st[:, c + n:c + 2 * n], st[:, c + n:c + 2 * n], ACT.Exp, f"{name}_rs", scale=-0.5)

            def after_residual(name):
                for i in range(2):
                    for t in range(TT):
                        e.after(f"{name}{i}.{t}")

            e.on("x_in", 16)
            norm(G_ATTN, x)
            e.after("cols")
            gained(G_ATTN)
            for g, name in enumerate(("q", "k", "v")):
                for half in range(2):
                    f = 4 * g + 2 * half
                    copy(cvi[:, f:f + 2, 3:3 + T], f"{name}.{half}", two)
                e.on("conv", g + 1)
                act(cv[:, 4 * g:4 * g + 4, :], cv[:, 4 * g:4 * g + 4, :], ACT.Silu, "silu")
                if g < 2:
                    act(sqk[g][:, :, :], cv[:, 4 * g:4 * g + 4, :].rearrange("p h (t c) -> p (h t) c", t=TT), ACT.Square, "squares")
            for t in range(TT):
                copy(zt[:, t, :], f"z.{t}", func=ACT.Silu)
            for half in range(2):
                queries(f"qd.{half}", 2 * half)
            for half in range(2):
                copy(kf[:, 2 * half:2 * half + 2, :], f"kd.{half}", two)
            for t in range(TT):
                copy(vt[:, t, :], f"vd.{t}")
            raw = st[:, 64:80].rearrange("p (t c) -> p c t", t=TT)
            ht = lambda c: st[:, c:c + HT].rearrange("p (h t) -> p h t", t=TT)
            e.after("ba")
            act(ht(56), raw[:, 0:H, :], ACT.Exp, "exp_b", scale=-1.0)
            e.on("abs_a")
            act(st[:, 96:104], st[:, 88:96], ACT.Exp, scale=-1.0)
            act(st[:, 104:112], st[:, 96:104], ACT.Ln, "softplus", bias=1.0)
            act(st[:, 120:124], rowv[:, R_A:R_A + H], ACT.Exp, "exp_a_log")
            e.on("lam_dots")
            act(st[:, 422:424], st[:, 420:422], ACT.Exp, "lam_exp")
            for i in range(4):
                v = sqk[i // 2][:, (i % 2) * 4:(i % 2) * 4 + 4, :]
                copy(v, f"ss{i}", four, ACT.Ln, bias=st[:, 510:511])
                act(v, v, ACT.Exp, "inv_norm", scale=-0.5)
            e.after("gcol")
            act(st[:, 32:48], st[:, 16:32], ACT.Exp, "exp_g")
            e.on("k_normed", 2)
            for j in range(2):
                b = e.filled(f"B{j}")
                act(eB[:, 4 * j:4 * j + 4, :], four(b), ACT.Exp, "exp_B")
            e.on("gdiff")
            act(dT[:, :, :], dT[:, :, :], ACT.Exp, "decay")
            for j in range(2):
                copy(Tn[:, 4 * j:4 * j + 4, :], f"T0{j}", four)
            for level in range(LEVELS):
                for j in range(2):
                    copy(X[:, 4 * j:4 * j + 4, :], f"X{level}.{j}", four)
            for j in range(2):
                copy(u[:, 4 * j:4 * j + 4, :], f"u{j}", four)
                copy(wT[:, 4 * j:4 * j + 4, :], f"w{j}", four)
            for c in range(NCH):
                lo = (c % 2) * CH
                copy(hn[lo:lo + CH, c // 2, 0:512], f"o{c}", lambda b: b[lo:lo + CH, :])
            head_rstd("la", 200, 8)
            softmax("df", 8, False)
            head_rstd("dh", 216, 8)
            for j in (0, 2):
                copy(hT[:, 2 * j:2 * j + 2, :], f"m0.{j}", two)
            after_residual("res0.")
            norm(G_FFN, x)
            gained(G_FFN)
            for j in range(FT // 2):
                if j >= 2:
                    e.after(f"gu{j - 2}.1")
                copy(sil[:, j % 2, :, :], f"gu{j}.0", two, ACT.Silu)
            for i in range(4):
                e.after(f"dn{i}")
            norm(6, x)
            norm(G_MIX, x, ready=("block1", 2))
            gained(G_MIX)
            copy(qg, "qkg.0", two)
            copy(kg, "qkg.1", two)
            e.on("gla_zeroed", 3)
            copy(alT[0:16, :], "al", lambda b: b[0:16, 0:T])
            for t in range(TT):
                copy(vt[:, t, :], f"vg.{t}")
            flat = lambda m: m.rearrange("p a b -> p (a b)")
            e.on("abs_la")
            act(flat(e2), flat(e1), ACT.Exp, scale=-1.0)
            act(flat(e2), flat(e2), ACT.Ln, "softplus_la", bias=1.0)
            for t in range(TT):
                copy(zt[:, t, :], f"rg.{t}", func=ACT.Silu)
            copy(flat(bc), "gb")
            for half in range(2):
                queries(f"qm.{half}", 2 * half)
            for half in range(2):
                copy(kf[:, 2 * half:2 * half + 2, :], f"km.{half}", two)
            e.on("gla_diff", 2)
            act(flat(e2), flat(e1), ACT.Exp, scale=-1.0)
            act(flat(e1), flat(e1), ACT.Exp)
            act(flat(kl), flat(kl), ACT.Exp)
            act(flat(qb), flat(bc), ACT.Exp, "gla_exp")
            for z, m in (("zg", zg), ("zm", zm)):
                for i in range(2):
                    for t in range(TT):
                        copy(m[:, t, i * 512:(i + 1) * 512], f"{z}{i}.{t}", func=ACT.Sigmoid)
            copy(klt.rearrange("p t f c -> p (t f) c"), "klt", four)
            for c in range(NCH):
                lo = (c % 2) * CH
                copy(hn[lo:lo + CH, c // 2, 0:512], f"go{c}", lambda b: b[lo:lo + CH, :])
            for t in range(TT):
                copy(vt[:, t, :], f"vm.{t}")
            head_rstd("gl", 232, 8)
            softmax("mo", 8, False)
            for j in (0, 2):
                copy(hT[:, 2 * j:2 * j + 2, :], f"m1.{j}", two)
            for j in (0, 2):
                copy(hT[:, 2 * j:2 * j + 2, :], f"m2.{j}", two)
            norm(G_MEM, zm, ready=("mem_in", 16))
            gained(G_MEM, memT)
            for half in range(2):
                copy(kf[:, 2 * half:2 * half + 2, :], f"ck.{half}", two)
            for t in range(TT):
                copy(vt[:, t, :], f"cv.{t}")
            after_residual("res1.")
            norm(G_CROSS, x)
            gained(G_CROSS)
            for half in range(2):
                copy(qz[:, 2 * half:2 * half + 2, 0, :], f"cq.{half}", two)
            softmax("me", H, True)
            copy(hT[:, 0:2, :], "m3.0", two)
            after_residual("res2.")
            norm(G_MOE, x)
            gained(G_MOE)
            e.on("router_max")
            act(ro[:, 16:24], ro[:, 16:24], ACT.Exp)
            e.on("router_top")
            act(ro[:, 200:202], ro[:, 200:202], ACT.Exp, "router_exp")
            def places(r):
                for g in range(4):
                    for t in range(TT):
                        eng.wait_ge(sem(f"place{t}"), 4 * r + (g + 1))
                        nc.scalar.activation(put[:, 4 * g + 1:4 * g + 5, t * P:(t + 1) * P], four(bank[PLACE[t]]), ACT.Copy)\
                            .then_inc(sem(f"placed{t}"), 1)

            def pair(r, i):
                n = NP * r + i
                eng.wait_ge(sem("gate_done"), n + 1)
                eng.wait_ge(sem("hidden"), n + 1)
                nc.scalar.activation(es, bank[B_G][:, :], ACT.Silu).then_inc(sem("silu_done"), 1)
                eng.wait_ge(sem("turned"), n + 1)
                nc.scalar.activation(eh.rearrange("p k j -> p (k j)"), bank[B_T][:, :], ACT.Copy).then_inc(sem("hidden"), 1)
                eng.wait_ge(sem("y_done"), 2 * n + 1)
                nc.scalar.activation(ys[:, 0:512], bank[B_Y[0]][:, :], ACT.Copy).then_inc(sem("y_out_a"), 1)

            def round_(r):
                places(r)
                with eng.Fori(0, NP) as i:
                    pair(r, i)

            e.on("credits")
            e.on("moe_zeroed", 3)
            for t in range(TT):
                act(st[:, 500 + t:501 + t], st[:, 510:511], ACT.Copy, f"placed{t}")
            act(st[:, 502:503], st[:, 510:511], ACT.Copy, "y_out_a")
            act(st[:, 505:506], st[:, 510:511], ACT.Copy, "hidden")
            round_(0)
            e.on("over_known")
            flag = eng.value_load(over[0:1, 0:1], min_val=0, max_val=1)
            with eng.If(flag > 0):
                with eng.Fori(1, ROUNDS) as r:
                    round_(r)
            e.on("sum_done")
            for k in (0, 2):
                act(accT[:, 2 * k:2 * k + 2, :], two(bank[B_ACC[k]]), ACT.Copy, "sum_out_a")
            for m in (0, 2):
                e.on("sum_back", m // 2 + 1)
                act(x[:, m // 2, 0:512], bank[B_TAIL[m]][:, :], ACT.Copy, "x_back_a")
            e.on("x_back_v", 2)
            norm(7, x)

        @block.vector
        def _(eng):
            e = Engine(eng, "dve_step")
            v = nc.vector

            def tt(out, in0, in1, op, name=None, turn=None):
                ins = v.tensor_tensor(out, in0, in1, op)
                e.empty(ins, turn) if turn else e.step(ins, name)

            def ts(out, in0, s1, s2, op0, op1=None, name=None, turn=None):
                ins = v.tensor_scalar(out, in0, s1, s2, op0, op1) if op1 is not None else v.tensor_scalar(out, in0, s1, None, op0)
                e.empty(ins, turn) if turn else e.step(ins, name)

            def stt(out, in0, scalar, in1, op0, op1, name=None, turn=None):
                ins = v.scalar_tensor_tensor(out=out, in0=in0, scalar=scalar, in1=in1, op0=op0, op1=op1)
                e.empty(ins, turn) if turn else e.step(ins, name)

            def copy(dst, turn, view=None):
                b = e.filled(turn)
                e.empty(v.tensor_copy(dst, view(b) if view else b[:, :]), turn)

            def two(b):
                return b.rearrange("p (f t) -> p f t", f=2)

            def four(b):
                return b.rearrange("p (i c) -> p i c", i=4)

            def wide(c, n, w):
                return st[:, c:c + n].unsqueeze(2).broadcast_to([P, n, w])

            def rep(m, n):
                return m.unsqueeze(1).broadcast_to([P, n, P])

            def norm_scale(n):
                c = 128 + 8 * n
                e.on(f"ssq{n}", TT)
                ts(st[:, c + 2:c + 4], st[:, c:c + 2], 1.0 / D, EPS, ALU.mult, ALU.add, f"mean{n}")
                e.on(f"rstd{n}")

            def norm(n, src, dst=hn):
                norm_scale(n)
                c = 128 + 8 * n
                for t in range(TT):
                    ts(dst[:, t, :], src[:, t, :], st[:, c + 4 + t:c + 5 + t], None, ALU.mult, name=f"normed{n}")

            def gained(n, hT=hT):
                for j in (1, 3):
                    b = e.filled(f"hT{n}.{j}")
                    for i in range(2):
                        k = 2 * j + i
                        ts(hT[:, k, :], b[:, i * T:(i + 1) * T], cols[:, n * KD + k:n * KD + k + 1], None, ALU.mult,
                           turn=f"hT{n}.{j}" if i else None)

            def attention(kind, maps, full, scale):
                c = {"df": 300, "mo": 332, "me": 364}[kind]
                for t in range(TT):
                    nk = TT if full else t + 1
                    w = nk * P
                    per = 512 // w
                    for m0 in range(0, maps, per):
                        turn = f"{kind}s{t}.{m0}"
                        b = e.filled(turn).rearrange("p (m k) -> p m k", m=per)
                        if kind == "df":
                            for i in range(2):
                                stt(sc[:, m0 + i:m0 + per:2, 0:w], b[:, i::2, :], scale, bias[:, m0 // 2:(m0 + per) // 2, T - w:],
                                    ALU.mult, ALU.add, turn=turn if i else None)
                        elif kind == "mo":
                            stt(sc[:, m0:m0 + per, 0:w], b, scale, bias[:, m0:m0 + per, T - w:], ALU.mult, ALU.add, turn=turn)
                        else:
                            ts(sc[:, m0:m0 + per, :], b, scale, None, ALU.mult, turn=turn)
                    e.step(v.tensor_reduce(st[:, c:c + maps], sc[:, 0:maps, 0:w], AX_X, ALU.max))
                    ts(st[:, c:c + maps], st[:, c:c + maps], -1.0, None, ALU.mult, name=f"{kind}_max")
                    e.on(f"{kind}_e" if kind == "df" else f"{kind}_p", t + 1)
                    r = c + 24
                    e.step(v.reciprocal(st[:, r:r + maps], st[:, c + 16:c + 16 + maps]))
                    if kind == "df":
                        ts(st[:, r + 1:r + 8:2], st[:, r + 1:r + 8:2], st[:, 425:426], None, ALU.mult)
                        for h in range(H):
                            ts(sc[:, 2 * h, 0:w], sc[:, 2 * h, 0:w], st[:, r + 2 * h:r + 2 * h + 1], None, ALU.mult)
                            stt(sc[:, 2 * h, 0:w], sc[:, 2 * h + 1, 0:w], st[:, r + 2 * h + 1:r + 2 * h + 2], sc[:, 2 * h, 0:w],
                                ALU.mult, ALU.add, name="df_p" if h == H - 1 else None)
                    pm = 4 if kind == "df" else maps
                    for kt in range(nk):
                        for m0 in range(0, pm, 4):
                            if (kt + m0 // 4) % 2:
                                copy(pT[:, kt, m0:m0 + 4, :], f"{kind}t{t}.{kt}.{m0}", four)
                    if kind != "df":
                        b = e.filled(f"{kind}o{t}")
                        dv = 512 // maps
                        tt(hn[:, t, 512:1024].rearrange("p (m d) -> p m d", d=dv), b.rearrange("p (m d) -> p m d", d=dv),
                           wide(r, maps, dv), ALU.mult, turn=f"{kind}o{t}")

            def head_norm(name, o, c, eps, gain, tmp, factor=1.0, done=None):
                tmp = tmp.rearrange("p (t h) d -> p t h d", t=TT)
                tt(tmp, o, o, ALU.mult)
                e.step(v.tensor_reduce(st[:, c:c + 8].rearrange("p (t h) -> p t h", t=TT), tmp, AX_X, ALU.add))
                ts(st[:, c:c + 8], st[:, c:c + 8], 1.0 / P, eps, ALU.mult, ALU.add, f"{name}_ms")
                e.on(f"{name}_rs")
                if factor != 1.0:
                    ts(st[:, c + 8:c + 16], st[:, c + 8:c + 16], factor, None, ALU.mult)
                for t in range(TT):
                    tt(o[:, t], o[:, t], wide(c + 8 + 4 * t, 4, P), ALU.mult)
                    tt(o[:, t], o[:, t], gain, ALU.mult, name=done if t else None)

            def residual(turns_):
                for turn, t, half in turns_:
                    b = e.filled(turn)
                    sl = x[:, t, half * 512:(half + 1) * 512]
                    tt(sl, sl, b[:, :], ALU.add, turn=turn)

            e.step(v.memset(st[:, 510:511], EPS), "eps_col")
            e.on("zeroed", 3)
            b = e.filled("cols")
            e.empty(v.tensor_copy(cols[:, :], b[:, 0:96]), "cols")
            b = e.filled("rel")
            e.empty(v.tensor_copy(relr[:, :], b[0:12, 0:REL]), "rel")
            e.on("x_in", 16)
            norm(G_ATTN, x)
            gained(G_ATTN)
            b = e.filled("ba")
            e.empty(v.tensor_copy(st[:, 64:80], b[:, 0:16]), "ba")
            for g in range(3):
                name = "qkv"[g]
                for f in range(4):
                    if f % 2 == 0:
                        e.after(f"{name}.{f // 2}")
                    F = 4 * g + f
                    tap = lambda i: cols[:, 48 + 12 * i + F:49 + 12 * i + F]
                    ts(cv[:, F, :], cvi[:, F, 0:T], tap(0), None, ALU.mult)
                    for i in range(1, 4):
                        stt(cv[:, F, :], cvi[:, F, i:i + T], tap(i), cv[:, F, :], ALU.mult, ALU.add,
                            name="conv" if i == 3 and f == 3 else None)
            raw = st[:, 64:80].rearrange("p (t c) -> p c t", t=TT)
            ht = lambda c: st[:, c:c + HT].rearrange("p (h t) -> p h t", t=TT)
            per_head = lambda v_: v_.unsqueeze(2).broadcast_to([P, H, TT])
            tt(ht(80), raw[:, H:2 * H, :], per_head(rowv[:, R_DT:R_DT + H]), ALU.add)
            stt(st[:, 88:96], st[:, 80:88], -1.0, st[:, 80:88], ALU.mult, ALU.max, name="abs_a")
            tt(work[:, 13348 - 1024:13348 - 1024 + 128], rowv[:, R_LAM:R_LAM + 128], rowv[:, R_LAM + 128:R_LAM + 256], ALU.mult)
            e.step(v.tensor_reduce(st[:, 420:422], work[:, 13348 - 1024:13348 - 1024 + 128].rearrange("p (i d) -> p i d", i=2), AX_X, ALU.add), "lam_dots")
            e.on("exp_b")
            ts(st[:, 56:64], st[:, 56:64], 1.0, None, ALU.add)
            e.step(v.reciprocal(st[:, 8:16], st[:, 56:64]))
            e.on("softplus")
            stt(st[:, 112:120], st[:, 80:88], 0.0, st[:, 104:112], ALU.max, ALU.add)
            e.on("exp_a_log")
            stt(ht(0), ht(112), -1.0, per_head(st[:, 120:124]), ALU.mult, ALU.mult)
            e.step(v.tensor_copy(gb[:, :, :], wide(0, HT, P)), "g_wide")
            e.step(v.tensor_copy(bb[:, :, :], wide(8, HT, P)), "beta_wide")
            e.on("lam_exp")
            tt(st[:, 424:425], st[:, 423:424], st[:, 422:423], ALU.subtract)
            ts(st[:, 425:426], st[:, 424:425], -LAM_INIT, None, ALU.add)
            for i in range(4):
                e.on("inv_norm", i + 1)
                r = sqk[i // 2][:, (i % 2) * 4:(i % 2) * 4 + 4, :]
                q = (qn, kn)[i // 2][:, 2 * (i % 2):2 * (i % 2) + 2, :].rearrange("p h (t c) -> p (h t) c", t=TT)
                stt(q, q, P ** -0.5 if i < 2 else 1.0, r, ALU.mult, ALU.mult, name="q_normed" if i < 2 else "k_normed")
            b = e.filled("gcol")
            e.empty(v.tensor_copy(st[:, 16:32], b[:, 0:16]), "gcol")
            for j in range(2):
                e.on("exp_B", j + 1)
                b = e.filled(f"B{j}")
                tt(dT[:, 4 * j:4 * j + 4, :], four(b), wide(16 + 4 * j, 4, P), ALU.subtract, turn=f"B{j}")
            tt(dT[:, :, :], dT[:, :, :], rep(tile(K_CAUSAL), HT), ALU.mult, name="gdiff")
            e.on("decay")
            tt(dT[:, :, :], dT[:, :, :], rep(tile(K_CAUSAL), HT), ALU.mult)
            for j in range(2):
                s = slice(4 * j, 4 * j + 4)
                b = e.filled(f"beta{j}")
                tt(LT[:, s, :], four(b), dT[:, s, :], ALU.mult, turn=f"beta{j}")
            tt(LT[:, :, :], LT[:, :, :], rep(tile(K_STRICT), HT), ALU.mult)
            for j in range(2):
                s = slice(4 * j, 4 * j + 4)
                b = e.filled(f"kk{j}")
                tt(LT[:, s, :], four(b), LT[:, s, :], ALU.mult, turn=f"kk{j}")
            tt(Tt[:, :, :], LT[:, :, :], rep(tile(K_PAIR), HT), ALU.mult)
            tt(Tt[:, :, :], rep(ident, HT), Tt[:, :, :], ALU.subtract, name="pairs")
            tt(Ct[:, :, :], LT[:, :, :], rep(tile(K_LEVEL), HT), ALU.mult, name="lower")
            for j in range(2):
                s = slice(4 * j, 4 * j + 4)
                b = e.filled(f"qk{j}")
                tt(aT[:, s, :], four(b), dT[:, s, :], ALU.mult, turn=f"qk{j}")
            e.on("exp_g")
            tt(st[:, 48:56], st[:, 8:16], st[:, 32:40], ALU.mult)
            for j in range(2):
                s = slice(4 * j, 4 * j + 4)
                b = e.filled(f"vtr{j}")
                tt(vb[:, s, :], four(b), wide(8 + 4 * j, 4, P), ALU.mult, turn=f"vtr{j}")
            for j in range(2):
                s = slice(4 * j, 4 * j + 4)
                b = e.filled(f"ktr{j}")
                tt(kbg[:, s, :], four(b), wide(48 + 4 * j, 4, P), ALU.mult)
                tt(kr[:, s, :], four(b), wide(40 + 4 * j, 4, P), ALU.mult, turn=f"ktr{j}")
            q = qn.rearrange("p h (t c) -> p (h t) c", t=TT)
            tt(q, q, eB[:, :, :], ALU.mult, name="q_scaled")
            e.step(v.memset(vnew[:, :, :], 0.0), "k_scaled")
            for level in range(LEVELS):
                for j in range(2):
                    e.filled(f"X{level}.{j}")
                if level < LEVELS - 1:
                    tt(Ct[:, :, :], LT[:, :, :], rep(tile(K_LEVEL + level + 1), HT), ALU.mult, name="lower")
                for j in range(2):
                    s = slice(4 * j, 4 * j + 4)
                    sides = ("t", "n") if level < LEVELS - 1 else ("t",)
                    for side in sides:
                        e.filled(f"D{side}{level}.{j}")
                    for side in sides:
                        m = Tt if side == "t" else Tn
                        turn = f"D{side}{level}.{j}"
                        tt(m[:, s, :], m[:, s, :], four(e.filled(turn)), ALU.subtract, turn=turn)
            by_t = lambda m, t: m.rearrange("p (h t) c -> p h t c", t=TT)[:, :, t, :]
            for c in range(NCH):
                t, lo = c // 2, (c % 2) * CH
                hi = lo + CH
                if c == 0:
                    e.after("u0")
                    e.after("u1")
                b = e.filled(f"wS{c}")
                tt(by_t(vnew, t)[lo:hi], by_t(u, t)[lo:hi], four(b)[lo:hi], ALU.subtract, turn=f"wS{c}")
                if c < NCH - 1:
                    e.filled(f"o{c}")
                    b = e.filled(f"dS{c}")
                    for h in range(H):
                        stt(S[:, h, :], S[:, h, :], eB[:, h * TT + t, hi - 1:hi], b[:, h * P:(h + 1) * P], ALU.mult, ALU.add,
                            turn=f"dS{c}" if h == H - 1 else None)
            heads = lambda c0: hn[:, :, c0:c0 + 512].rearrange("p t (h d) -> p t h d", h=H)
            for c in range(NCH):
                e.after(f"o{c}")
            head_norm("la", heads(0), 200, EPS, rep(rowv[:, R_LA:R_LA + P], 4), dT)
            for t in range(TT):
                e.after(f"z.{t}")
                tt(hn[:, t, 0:512], hn[:, t, 0:512], zt[:, t, :], ALU.mult, name="mixed0" if t else None)
            for h in (0, 2):
                copy(bias[:, h:h + 2, :], f"bias1.{h}", two)
            attention("df", 8, False, 0.125)
            for t in range(TT):
                e.after(f"dfo{t}")
            head_norm("dh", heads(512), 216, 1e-5, rep(rowv[:, R_DIFF:R_DIFF + P], 4), dT, 1.0 - LAM_INIT, done="mixed0")
            for j in (1, 3):
                copy(hT[:, 2 * j:2 * j + 2, :], f"m0.{j}", two)
            residual([(f"res0.{i}.{t}", t, i) for i in range(2) for t in range(TT)])
            norm(G_FFN, x)
            for h in (0, 2, 4, 6):
                copy(bias[:, h:h + 2, :], f"bias2.{h}", two)
            gained(G_FFN)
            for j in range(FT // 2):
                e.after(f"gu{j}.0")
                b = e.filled(f"gu{j}.1")
                tt(actT[:, 2 * j:2 * j + 2, :], two(b), sil[:, j % 2, :, :], ALU.mult, turn=f"gu{j}.1")
            residual([(f"dn{i}", i // 2, i % 2) for i in range(4)])
            norm_scale(6)
            gain = zt.rearrange("p t d -> p (t d)")
            e.on("gain_row", 16)
            for t in range(TT):
                c = 128 + 48 + 4 + t
                ts(x[:, t, :], x[:, t, :], st[:, c:c + 1], None, ALU.mult)
                tt(x[:, t, :], x[:, t, :], gain, ALU.mult, name="block1")
            norm(G_MIX, x)
            gained(G_MIX)
            flat = lambda m: m.rearrange("p a b -> p (a b)")
            b = e.filled("la")
            e.step(v.tensor_copy(flat(la), b[:, :]))
            stt(flat(e1), flat(la), -1.0, flat(la), ALU.mult, ALU.max, name="abs_la")
            e.on("softplus_la")
            stt(flat(la), b[:, :], 0.0, flat(e2), ALU.min, ALU.subtract, turn="la")
            ts(flat(la), flat(la), 1.0 / 16.0, None, ALU.mult, name="la_ready")
            e.after("gb")
            chunks = lambda m: m.rearrange("p f (i c) -> p (f i) c", c=CH)
            col = lambda m, c: chunks(m)[:, :, c:c + 1].broadcast_to([P, 2 * NCH, CH])
            tt(chunks(e1), chunks(bc), col(bc, CH // 2 - 1), ALU.subtract, name="gla_diff")
            tt(chunks(kl), col(bc, CH - 1), chunks(bc), ALU.subtract, name="gla_diff")
            e.on("gla_exp")
            e.on("gla_zeroed", 3)
            e.step(v.tensor_copy(st[:, 432:440].unsqueeze(2), chunks(qb)[:, :, CH - 1:CH]))
            e.after("qkg.0")
            e.after("qkg.1")
            for f in range(2):
                for m in range(2):
                    r = slice(64 * m, 64 * m + 64)
                    stt(qez[r, f, m, :], qg[r, f, :], 0.125, e1[r, f, :], ALU.mult, ALU.mult, name="gla_q")
            tt(flat(e2), flat(e2), flat(kg), ALU.mult, name="gla_k")
            tt(flat(kl), flat(kl), flat(kg), ALU.mult, name="gla_kl")
            stt(flat(qb), flat(qg), 0.125, flat(qb), ALU.mult, ALU.mult, name="gla_qb")
            for j in range(2):
                b = e.filled(f"ga{j}")
                tt(atT[:, 4 * j:4 * j + 4, :], four(b), rep(tile(K_CAUSAL), 4), ALU.mult, turn=f"ga{j}")
            for c in range(NCH - 1):
                b = e.filled(f"kv{c}")
                for f in range(2):
                    for m in range(2):
                        r = slice(64 * m, 64 * m + 64)
                        sl = slice(m * P, (m + 1) * P)
                        d = 432 + f * NCH + c
                        stt(sts[r, c + 1, f, sl], sts[r, c, f, sl], st[r, d:d + 1], b[r, f * T + m * P:f * T + (m + 1) * P],
                            ALU.mult, ALU.add, turn=f"kv{c}" if f and m else None)
            for c in range(NCH):
                e.after(f"go{c}")
            head_norm("gl", heads(0), 232, EPS, rowv[:, R_GLA:R_GLA + 512].rearrange("p (h d) -> p h d", h=H), gnt)
            for t in range(TT):
                e.after(f"rg.{t}")
                tt(hn[:, t, 0:512], hn[:, t, 0:512], zt[:, t, :], ALU.mult, name="mixed1" if t else None)
            attention("mo", 8, False, 0.125)
            for j in (1, 3):
                copy(hT[:, 2 * j:2 * j + 2, :], f"m1.{j}", two)
            for name, z in (("pg", zg), ("pm", zm)):
                for i in range(2):
                    for t in range(TT):
                        sl = z[:, t, i * 512:(i + 1) * 512]
                        e.after(f"{name[:0]}z{name[1]}{i}.{t}")
                        tt(sl, e.filled(f"{name}{i}.{t}")[:, :], sl, ALU.mult, turn=f"{name}{i}.{t}")
                        if name == "pm":
                            sg = zg[:, t, i * 512:(i + 1) * 512]
                            tt(sg, sg, sl, ALU.add, name="merged")
            for j in (1, 3):
                copy(hT[:, 2 * j:2 * j + 2, :], f"m2.{j}", two)
            norm(G_MEM, zm, zm)
            gained(G_MEM, memT)
            residual([(f"res1.{i}.{t}", t, i) for i in range(2) for t in range(TT)])
            norm(G_CROSS, x)
            gained(G_CROSS)
            attention("me", H, True, P ** -0.5)
            copy(hT[:, 2:4, :], "m3.1", two)
            residual([(f"res2.{i}.{t}", t, i) for i in range(2) for t in range(TT)])
            norm(G_MOE, x)
            gained(G_MOE)
            b = e.filled("rt")
            tt(rl[:, :, :], b[:, 0:TT * (NG + NE)].rearrange("p (t n) -> p t n", t=TT),
               rowv[:, R_BG:R_BG + NG + NE].unsqueeze(1).broadcast_to([P, TT, NG + NE]), ALU.add, turn="rt")
            r3 = lambda c, n: ro[:, c:c + TT * n].rearrange("p (t n) -> p t n", t=TT)
            bcast = lambda m, n: m.unsqueeze(2).broadcast_to([P, TT, n])
            rank = lambda n: ro[:, 0:n].unsqueeze(1).broadcast_to([P, TT, n])
            ts(ro[:, 0:8], index[:, 0:8], -1.0, 100.0, ALU.mult, ALU.add)

            def first_best(values, n, top, onehot_):
                e.step(v.tensor_reduce(top, values, AX_X, ALU.max))
                tt(onehot_, values, bcast(top, n), ALU.is_ge)
                tt(onehot_, onehot_, rank(n), ALU.mult)
                e.step(v.tensor_reduce(ro[:, 8:10], onehot_, AX_X, ALU.max))
                tt(onehot_, onehot_, bcast(ro[:, 8:10], n), ALU.is_equal)

            gmax, ohg = ro[:, 10:12], r3(32, NG)
            first_best(rl[:, :, 0:NG], NG, gmax, ohg)
            tt(r3(16, NG), rl[:, :, 0:NG], bcast(gmax, NG), ALU.subtract, name="router_max")
            prod = ro[:, 512:512 + TT * NE].rearrange("p (t g n) -> p t g n", t=TT, g=NG)
            tt(prod, rl[:, :, NG:].rearrange("p t (g n) -> p t g n", g=NG), ohg.unsqueeze(3).broadcast_to([P, TT, NG, EG]), ALU.mult)
            ein = r3(64, EG)
            for t in range(TT):
                e.step(v.tensor_reduce(ein[:, t], prod[:, t].rearrange("p g n -> p n g"), AX_X, ALU.add))
            oh1, oh2, rest = r3(96, EG), r3(128, EG), r3(160, EG)
            m1, m2 = ro[:, 12:14], ro[:, 14:16]
            first_best(ein, EG, m1, oh1)
            stt(rest, oh1, MASKED, ein, ALU.mult, ALU.add)
            first_best(rest, EG, m2, oh2)
            tt(ro[:, 200:202], m2, m1, ALU.subtract, name="router_top")
            e.on("router_exp")
            e.step(v.tensor_reduce(ro[:, 204:206], r3(16, NG), AX_X, ALU.add))
            ts(ro[:, 206:208], ro[:, 200:202], 1.0, None, ALU.add)
            tt(ro[:, 206:208], ro[:, 206:208], ro[:, 204:206], ALU.mult)
            e.step(v.reciprocal(ro[:, 208:210], ro[:, 206:208]))
            tt(ro[:, 210:212], ro[:, 208:210], ro[:, 200:202], ALU.mult)
            by_group = lambda m, t: m[:, t, :].rearrange("p (g n) -> p g n", g=NG)
            group = lambda t: ohg[:, t].unsqueeze(2).broadcast_to([P, NG, EG])
            within = lambda m, t: m[:, t].unsqueeze(1).broadcast_to([P, NG, EG])
            tt(rest, oh1, oh2, ALU.add)
            for t in range(TT):
                tt(by_group(Mk, t), group(t), within(rest, t), ALU.mult, name="masked" if t else None)
            tt(oh1, oh1, bcast(ro[:, 208:210], EG), ALU.mult)
            tt(oh2, oh2, bcast(ro[:, 210:212], EG), ALU.mult)
            tt(oh1, oh1, oh2, ALU.add)
            for t in range(TT):
                tt(by_group(Wt, t), group(t), within(oh1, t), ALU.mult)
            b = e.filled("rank")
            stt(rk, b[:, 0:2 * NE].rearrange("p (t n) -> p t n", t=TT), 1.0, Mk, ALU.add, ALU.mult)
            ts(rk, rk, -1.0, None, ALU.add)
            e.step(v.tensor_reduce(ro[:, 212:213], b[:, 2 * NE:3 * NE], AX_X, ALU.max))
            ts(over[:, :], ro[:, 212:213], float(SL), None, ALU.is_gt, turn="rank")
            e.step(v.memset(st[:, 503:504], 0.0), "over_known")

            def picks(r):
                if not isinstance(r, int):
                    v.tensor_scalar(rk, rk, -float(SL), None, ALU.add).then_inc(sem("rank_shifted"), 1)
                    eng.wait_ge(sem("rank_shifted"), r)
                for t in range(TT):
                    ins = v.tensor_tensor(pick[:, t, 0:NE, :], index[:, 0:SL].unsqueeze(1).broadcast_to([P, NE, SL]),
                                          rk[:, t, :].unsqueeze(2).broadcast_to([P, NE, SL]), ALU.is_equal)
                    ins.then_inc(sem("picked"), 1)
                eng.wait_ge(sem("picked"), TT * r + TT)
                for g in range(4):
                    if g >= 2:
                        for t in range(TT):
                            eng.wait_ge(sem(f"place{t}"), 4 * r + (g - 1))
                    src = pick[:, :, 8 * g:8 * g + 8, :]
                    dst = pw[:, g % 2, :].rearrange("p (t n j) -> p t n j", t=TT, n=8)
                    w = Wt[:, :, 8 * g:8 * g + 8].unsqueeze(3).broadcast_to([P, TT, 8, SL])
                    v.tensor_tensor(dst, src, w, ALU.mult).then_inc(sem("weighted"), 1)

            def gathered(n):
                for half in range(2):
                    eng.wait_ge(sem("gathered"), 2 * n + (half + 1))
                    c = G_MOE * KD + 4 * half
                    ins = v.tensor_tensor(xg[:, 4 * half:4 * half + 4, :], four(bank[B_X[half]]),
                                          cols[:, c:c + 4].unsqueeze(2).broadcast_to([P, 4, P]), ALU.mult)
                    ins.then_inc(sem("gathered_out"), 1)

            def pair(r, i):
                n = NP * r + i
                eng.wait_ge(sem("up_done"), n + 1)
                eng.wait_ge(sem("silu_done"), n + 1)
                v.tensor_tensor(es, bank[B_U][:, :], es, ALU.mult).then_inc(sem("h_ready"), 1)
                gathered((NP + 1) * r + (i + 1))
                eng.wait_ge(sem("y_done"), 2 * n + 2)
                v.tensor_copy(ys[:, 512:1024], bank[B_Y[1]][:, :]).then_inc(sem("y_out_v"), 1)

            def round_(r):
                picks(r)
                gathered((NP + 1) * r)
                with eng.Fori(0, NP) as i:
                    pair(r, i)

            e.step(v.memset(put[:, 0, :], 0.0), "moe_zeroed")
            e.step(v.memset(pick[:, :, NE:NE + 2, :], 0.0), "moe_zeroed")
            e.step(v.memset(ys, 0.0), "moe_zeroed")
            e.step(v.memset(st[:, 504:505], 0.0), "y_out_v")
            e.step(v.memset(st[:, 504:505], 0.0), "credits")
            round_(0)
            e.on("over_known")
            flag = eng.value_load(over[0:1, 0:1], min_val=0, max_val=1)
            with eng.If(flag > 0):
                with eng.Fori(1, ROUNDS) as r:
                    round_(r)
            e.on("sum_done")
            for k in (1, 3):
                e.step(v.tensor_copy(accT[:, 2 * k:2 * k + 2, :], two(bank[B_ACC[k]])), "sum_out_v")
            for m in (1, 3):
                e.on("sum_back", m // 2 + 3)
                e.step(v.tensor_copy(x[:, m // 2, 512:1024], bank[B_TAIL[m]][:, :]), "x_back_v")
            e.on("x_back_a", 2)
            norm_scale(7)
            e.on("gain_row", 32)
            for t in range(TT):
                c = 128 + 56 + 4 + t
                ts(x[:, t, :], x[:, t, :], st[:, c:c + 1], None, ALU.mult)
                tt(x[:, t, :], x[:, t, :], gain, ALU.mult, name="result")


def kernel(**inputs):
    import concourse.bacc as bacc
    from concourse.bass_utils import run_bass_kernel_spmd

    nc = bacc.Bacc("TRN2", target_bir_lowering=False, num_devices=1)
    arrays, access = {}, {}
    for name, value in inputs.items():
        value = np.ascontiguousarray(value)
        arrays[f"in_{name}"] = value
        access[name] = nc.dram_tensor(f"in_{name}", value.shape, F32, kind="ExternalInput").ap()
    const = shape_constants()
    arrays["shape_const"] = const
    const_ap = nc.dram_tensor("shape_const", const.shape, F32, kind="ExternalInput").ap()
    result = nc.dram_tensor("out", (1, T, D), F32, kind="ExternalOutput").ap()
    two_blocks(nc, access, const_ap, result)
    ran = run_bass_kernel_spmd(nc, [arrays], core_ids=[0])
    return ran.results[0]["out"]
```

```python
from contextlib import ExitStack

import numpy as np

import concourse.bass as bass
from concourse import mybir

F32 = mybir.dt.float32
ALU = mybir.AluOpType
ACT = mybir.ActivationFunctionType
AX_X = mybir.AxisListType.X

P = 128
T = 256
TT = T // P
D = 1024
KD = D // P
H = 4
CH = 64
NCH = T // CH
HT = H * TT
DFF = 2816
FT = DFF // P
NE = 32
NP = NE // 2
NG = 4
EG = NE // NG
DE = 512
SL = 64
ROUNDS = T // SL
EPS = 1e-6
LAM_INIT = 0.8 - 0.6 * 1.0
MASKED = -1.0e30
RING = 5
RING_A = 4
LEVELS = 5

C_Q, C_K, C_V, C_Z, C_BA, C_QD, C_KD, C_VD = 0, 512, 1024, 1536, 2048, 2056, 2568, 3080
C2_QK, C2_V, C2_R, C2_A, C2_QM, C2_KM, C2_VM, C2_ZG, C2_ZM = 0, 512, 1024, 1536, 1552, 2064, 2576, 3088, 4112

(K_ID, K_ONE, K_CAUSAL, K_STRICT, K_BELOW, K_PAIR, K_BEFORE, K_FLIP) = range(8)
K_LEVEL = 8
N_TILES = K_LEVEL + LEVELS
REL = 384


def shape_constants():
    s, c = np.meshgrid(np.arange(P), np.arange(P), indexing="ij")
    same = s // CH == c // CH
    tiles = [s == c, s >= 0, same & (s <= c), same & (s < c), same & (s > c),
             (s // 2 == c // 2) & (s < c), s < c, s + c == P - 1]
    for level in range(LEVELS):
        w = 2 << level
        tiles.append((s // (2 * w) == c // (2 * w)) & (s % (2 * w) < w) & (c % (2 * w) >= w))
    n = 255 - np.arange(REL)
    past = np.maximum(n, 0)
    far = 16 + (np.log(np.maximum(past, 1) / 16) / np.log(8.0) * 16 + 1e-6).astype(np.int64)
    bucket = np.where(past < 16, past, np.minimum(far, 31))
    table = np.zeros((P, REL))
    table[bucket[n >= 0], np.arange(REL)[n >= 0]] = 1.0
    table[32, n < 0] = MASKED
    index = np.broadcast_to(np.arange(P), (P, P))
    return np.concatenate([t.astype(np.float64) for t in tiles] + [table, index], axis=1).astype(np.float32)


def two_blocks(nc, a, const, out):
    stack = ExitStack()
    with stack:
        def sb(name, shape):
            return stack.enter_context(nc.sbuf_tensor(name, shape, F32))

        sems = {}

        def sem(name):
            if name not in sems:
                sems[name] = stack.enter_context(nc.semaphore(name))
            return sems[name]

        ring = sb("ring", [P, RING, 4096])
        work = sb("work", [P, 13440])
        x = sb("x", [P, TT, D])
        hn = sb("hn", [P, TT, D])
        hT = sb("hT", [P, KD, T])
        qz = sb("qz", [P, H, 2, T])
        kf = sb("kf", [P, H, T])
        vt = sb("vt", [P, TT, 512])
        zt = sb("zt", [P, TT, 512])
        bias = sb("bias", [P, 8, T])
        cst = sb("cst", [P, N_TILES * P + REL + P])
        rows = sb("rows", [96, P])
        cols = sb("cols", [P, 96])
        relb = sb("relb", [33, 12])
        relr = sb("relr", [12, REL])
        rowv = sb("rowv", [P, 1088])
        w_ba = sb("w_ba", [P, KD, 8])
        w_al = sb("w_al", [P, KD, 16])
        w_up16 = sb("w_up16", [17, 256])
        w_rt = sb("w_rt", [P, KD, NG + NE])
        st = sb("st", [P, 512])
        S = sb("S", [P, H, P])
        over = stack.enter_context(nc.sbuf_tensor("over", [P, 1], mybir.dt.int32))
        rel_dram = nc.dram_tensor("rel_dram", [12, REL], F32, kind="Internal").ap()

        def tile(i):
            return cst[:, i * P:(i + 1) * P]

        ident, ones = tile(K_ID), tile(K_ONE)
        onehot = cst[0:33, N_TILES * P:N_TILES * P + REL]
        index = cst[:, N_TILES * P + REL:]
        G_ATTN, G_FFN, G_MIX, G_CROSS, G_MEM, G_MOE = range(6)
        R_DT, R_A, R_LA, R_DIFF, R_GLA, R_BG, R_BE, R_LAM = 0, 4, 8, 136, 264, 776, 780, 812

        at = [0]

        def area(*shape):
            n = int(np.prod(shape))
            v = work[:, at[0]:at[0] + n]
            at[0] += n
            assert at[0] <= 13440
            if len(shape) == 1:
                return v
            names = "abcd"[:len(shape)]
            return v.rearrange(f"p ({' '.join(names)}) -> p {' '.join(names)}",
                               **{k: s for k, s in zip(names, shape)})

        cvi = area(12, T + 3)
        cv = area(12, T)
        qn, kn, vc = cv[:, 0:4, :], cv[:, 4:8, :], cv[:, 8:12, :]
        dT, eB, aT, LT, Tn, Tt, vnew = (area(HT, P) for _ in range(7))
        at[0] = 0
        vb, kbg, kr = (area(HT, P) for _ in range(3))
        X, Ct = (ring[:, RING - 1, i * HT * P:(i + 1) * HT * P].rearrange("p (i c) -> p i c", c=P) for i in range(2))
        u, wT = X, Ct
        sqk = dT, eB
        gb, bb = aT, LT
        at[0] = 6180
        sc = area(8, T)
        pT = area(2, 8, P)
        sc_first = area(8, P)

        def sc_tile(kind, t):
            if kind == "df":
                return sc_df1 if t else sc_df0
            return sc[:, 4 * t:4 * t + 4, :] if kind == "me" else sc if t else sc_first

        def pt_of(kind):
            return pT_df if kind == "df" else pT

        def sc_cols(kind, t):
            return 248 if t else {"df": 300, "mo": 332, "me": 364}[kind]
        df_squares = eB
        sc_df1 = work[:, 0:8 * T].rearrange("p (m k) -> p m k", m=8)
        sc_df0 = kn.rearrange("p a (b k) -> p (a b) k", k=P)
        pT_df = vc.rearrange("p (a b) (c k) -> p a (b c) k", a=2, k=P)
        at[0] = 0
        actT = area(FT, T)
        sil = area(2, 2, T)
        at[0] = 6700
        flip = area(8, T)
        at[0] = 0
        qg, kg = area(2, T), area(2, T)
        zg, zm = area(TT, D), area(TT, D)
        gnt = work[:, 5376:6400].rearrange("p (i c) -> p i c", c=P)
        at[0] = 10300
        memT = area(KD, T)
        at[0] = 5120
        alT = area(T)
        la, bc, e1, e2 = area(TT, T), area(2, T), area(2, T), area(2, T)
        kl, qb, qez, klt, atT = area(2, T), area(2, T), area(2, 2, T), area(TT, 2, P), area(HT, P)
        sts = area(NCH, 2, 256)
        at[0] = 0
        slot5 = area(4096)
        pick = area(TT, NE + 2, SL)
        put = area(NE // 2 + 1, T)
        xg = kf.rearrange("p h t -> p (h t)").rearrange("p (k j) -> p k j", k=KD)
        es = vt[:, 1, :]
        eh = vt[:, 0, :].rearrange("p (k j) -> p k j", k=DE // P)
        ys = qz[:, 0:2, :, :].rearrange("p a b t -> p (a b t)")
        pw = hT.rearrange("p (b c) t -> p b (c t)", b=2)
        accT = hT
        eb = bias.rearrange("p h t -> p (h t)")
        Wt, Mk, rk = (eb[:, i * 64:(i + 1) * 64].rearrange("p (t n) -> p t n", t=TT) for i in range(3))
        rl = eb[:, 192:264].rearrange("p (t n) -> p t n", t=TT)
        ro = eb[:, 1024:2048]

        bank = [stack.enter_context(nc.psum_tensor(f"bank{i}", [P, 512], F32)) for i in range(8)]
        filled = [sem(f"filled{i}") for i in range(8)]
        emptied = [sem(f"emptied{i}") for i in range(8)]
        turns = {}
        used = [0] * 8
        order = [0]
        B_G, B_U, B_X, B_ACC = 0, 1, (2, 3), (4, 5, 6, 7)
        B_T, B_Y, PLACE, B_TAIL = B_G, B_X, (B_G, B_U), (0, 1, 2, 3)

        loads = []
        released = {}

        def kp(w):
            return w.rearrange("(k p) n -> p k n", p=P)

        def load(name, src):
            loads.append((name, src))
            return len(loads) - 1

        w_in, w_in2 = kp(a["w_in"][0]), kp(a["w_in_2"][0])
        L = {}
        for name, c0 in (("q", C_Q), ("k", C_K), ("v", C_V), ("qd", C_QD), ("kd", C_KD), ("vd", C_VD), ("z", C_Z)):
            L[name] = load(name, w_in[:, :, c0:c0 + 512])
        for i in range(2):
            L["wo", i] = load("wo", kp(a["w_out"][0])[:, :, i * 512:(i + 1) * 512])
        for j in range(FT // 2):
            L["gu", j] = load("gu", a["w_gate_up"][0].rearrange("(k p) (g n) -> p k g n", p=P, g=2)[:, :, :, j * 256:(j + 1) * 256])
        for j in range(0, FT, 4):
            n = min(4, FT - j)
            L["dn", j] = load("dn", kp(a["w_down"][0])[:, j:j + n, :])
        for name, c0 in (("qkg", C2_QK), ("vg", C2_V), ("rg", C2_R), ("qm", C2_QM), ("km", C2_KM),
                         ("zg0", C2_ZG), ("zg1", C2_ZG + 512), ("zm0", C2_ZM), ("zm1", C2_ZM + 512), ("vm", C2_VM)):
            L[name] = load(name, w_in2[:, :, c0:c0 + 512])
        L["pm"] = load("pm", kp(a["w_proj_moba_2"][0]))
        L["pg"] = load("pg", kp(a["w_proj_gla_2"][0]))
        for i in range(2):
            L["wo2", i] = load("wo2", kp(a["w_out_2"][0])[:, :, i * 512:(i + 1) * 512])
        L["ck"] = load("ck", kp(a["w_ckv_2"][0])[:, :, 0:512])
        L["cv"] = load("cv", kp(a["w_ckv_2"][0])[:, :, 512:1024])
        L["cq"] = load("cq", kp(a["w_cq_2"][0]))
        L["co"] = load("co", kp(a["w_co_2"][0]))
        NA = len(loads)

        def slot(n):
            return ring[:, n % RING_A, :]

        expert_slots = [RING - 1, RING] + sorted(range(RING_A), key=lambda r: max(n for n in range(NA) if n % RING_A == r))

        def eslot(m, s):
            j = expert_slots[2 * m + s]
            return ring[:, j, :] if j < RING else slot5

        loaded = [sem(f"loaded{i}") for i in range(RING_A)]

        def pieces(n):
            return 2 if loads[n][0] == "gu" else 1

        def wait_load(eng, n):
            eng.wait_ge(loaded[n % RING_A], 16 * sum(pieces(m) for m in range(n % RING_A, n + 1, RING_A)))

        class Engine:

            def __init__(self, eng, name):
                self.eng, self.own, self.count = eng, name, {}

            def step(self, ins, name=None):
                name = name or self.own
                self.count[name] = self.count.get(name, 0) + 1
                ins.then_inc(sem(name), 1)
                self.eng.wait_ge(sem(name), self.count[name])

            def filled(self, turn):
                b, k = turns[turn]
                self.eng.wait_ge(filled[b], k)
                return bank[b]

            def empty(self, ins, turn):
                b, k = turns[turn]
                ins.then_inc(emptied[b], 1)
                self.eng.wait_ge(emptied[b], k)

            def on(self, name, value=1):
                self.eng.wait_ge(sem(name), value)

            def after(self, turn):
                b, k = turns[turn]
                self.eng.wait_ge(emptied[b], k)

        N_ROWS, N_SMALL = 8, 20
        block = stack.enter_context(nc.Block())

        @block.tensor
        def _(eng):
            mm, tr = nc.tensor.matmul, nc.tensor.transpose
            e = Engine(eng, "pe_step")

            def begin(name):
                b = order[0] % 8
                order[0] += 1
                used[b] += 1
                turns[name] = (b, used[b])
                if used[b] > 1:
                    eng.wait_ge(emptied[b], used[b] - 1)
                return bank[b]

            def end(ins, name):
                ins.then_inc(filled[turns[name][0]], 1)

            def release(n, turn):
                b, k = turns[turn]
                released[n] = (filled[b], k)

            def transposes(name, pieces):
                b = begin(name)
                for i, piece in enumerate(pieces):
                    ins = tr(b[:, i * P:(i + 1) * P], piece, ident)
                end(ins, name)

            def norm_transposed(n, src=hn):
                for j in range(4):
                    t, q = j // 2, j % 2
                    e.on(f"normed{n}", t + 1)
                    transposes(f"hT{n}.{j}", [src[:, t, k * P:(k + 1) * P] for k in range(4 * q, 4 * q + 4)])

            def normed(n):
                for j in range(4):
                    e.after(f"hT{n}.{j}")

            def features(name, w, src, n, tiles=4, kk=KD):
                for half in range(tiles // 2):
                    b = begin(f"{name}.{half}")
                    for f in range(2):
                        for k in range(kk):
                            ins = mm(b[:, f * T:(f + 1) * T], w[:, k, (2 * half + f) * P:(2 * half + f + 1) * P],
                                     src[:, k, :], start=k == 0, stop=k == kk - 1)
                    end(ins, f"{name}.{half}")
                release(n, f"{name}.{half}")

            def tokens(name, w, src, n, kk=KD, tiles=range(TT)):
                for t in tiles:
                    b = begin(f"{name}.{t}")
                    for k in range(kk):
                        ins = mm(b[:, :], src[:, k, t * P:(t + 1) * P], w[:, k, :], start=k == 0, stop=k == kk - 1)
                    end(ins, f"{name}.{t}")
                if t == TT - 1:
                    release(n, f"{name}.{t}")

            def quarter(name, i):
                t, q = i // 2, i % 2
                w = slot8(L[name])
                b = begin(f"{name}.{i}")
                for k in range(KD):
                    ins = mm(b[:, 0:256], hT[:, k, t * P:(t + 1) * P], w[:, k, q * 256:(q + 1) * 256], start=k == 0, stop=k == KD - 1)
                end(ins, f"{name}.{i}")
                if i == 3:
                    release(L[name], f"{name}.{i}")

            def tokens_wide(name, key, between=None):
                w = [slot8(L[key, i]) for i in range(2)]
                for t in range(TT):
                    if t and between:
                        between()
                    for i in range(2):
                        b = begin(f"{name}{i}.{t}")
                        for k in range(KD):
                            ins = mm(b[:, :], hT[:, k, t * P:(t + 1) * P], w[i][:, k, :], start=k == 0, stop=k == KD - 1)
                        end(ins, f"{name}{i}.{t}")
                for i in range(2):
                    release(L[key, i], f"{name}{i}.{TT - 1}")

            def slot8(n):
                wait_load(eng, n)
                return slot(n).rearrange("p (k n) -> p k n", k=KD)

            def scores(kind, maps, full, tiles=range(TT)):
                for t in tiles:
                    nk = TT if full else t + 1
                    per = 512 // (nk * P)
                    for m0 in range(0, maps, per):
                        b = begin(f"{kind}s{t}.{m0}")
                        for m in range(m0, m0 + per):
                            q = qz[:, m // 2, m % 2, :] if not full else qz[:, m, 0, :]
                            k = kf[:, m // 2, :] if not full else kf[:, m, :]
                            ins = mm(b[:, (m - m0) * nk * P:(m - m0 + 1) * nk * P], q[:, t * P:(t + 1) * P],
                                     k[:, 0:nk * P], start=True, stop=True)
                        end(ins, f"{kind}s{t}.{m0}")

            def values(kind, maps, full):
                for t in range(TT):
                    nk = TT if full else t + 1
                    sct = sc_tile(kind, t)
                    pm = 4 if kind == "df" else maps
                    e.on(f"{kind}_p", t + 1)
                    for kt in range(nk):
                        for m0 in range(0, pm, 4):
                            step = 2 if kind == "df" else 1
                            transposes(f"{kind}t{t}.{kt}.{m0}", [sct[:, m * step, kt * P:(kt + 1) * P] for m in range(m0, m0 + 4)])
                    b = begin(f"{kind}o{t}")
                    dv = 512 // pm
                    for kt in range(nk):
                        for m0 in range(0, pm, 4):
                            e.after(f"{kind}t{t}.{kt}.{m0}")
                    for m in range(pm):
                        for kt in range(nk):
                            ins = mm(b[:, m * dv:(m + 1) * dv], pt_of(kind)[:, kt, m, :], vt[:, kt, m * dv:(m + 1) * dv],
                                     start=kt == 0, stop=kt == nk - 1)
                    end(ins, f"{kind}o{t}")

            e.on("consts", 16 * N_ROWS)
            b = begin("cols")
            end(tr(b[:, 0:96], rows[:, :], ident[0:96, 0:96]), "cols")
            norm_transposed(G_ATTN)
            normed(G_ATTN)
            for name in ("q", "k", "v"):
                features(name, slot8(L[name]), hT, L[name])
            e.on("small", 16 * N_SMALL)
            e.on("relb_one")
            b = begin("rel")
            end(mm(b[0:12, 0:REL], relb[:, :], onehot, start=True, stop=True), "rel")
            b = begin("ba")
            for t in range(TT):
                for k in range(KD):
                    ins = mm(b[:, t * 8:(t + 1) * 8], hT[:, k, t * P:(t + 1) * P], w_ba[:, k, :], start=k == 0, stop=k == KD - 1)
            end(ins, "ba")
            for name in ("qd", "kd"):
                features(name, slot8(L[name]), hT, L[name])

            for i in range(4):
                e.on("squares", i // 2 + 1)
                b = begin(f"ss{i}")
                end(mm(b[:, :], ones, sqk[i // 2][:, (i % 2) * 4:(i % 2) * 4 + 4, :], start=True, stop=True), f"ss{i}")
            quarter("vd", 0)
            e.on("g_wide")
            for j in range(2):
                b = begin(f"B{j}")
                for i in range(4):
                    ins = mm(b[:, i * P:(i + 1) * P], gb[:, 4 * j + i, :], tile(K_CAUSAL), start=True, stop=True)
                end(ins, f"B{j}")
            b = begin("gcol")
            mm(b[:, 0:HT], tile(K_CAUSAL), st[:, 0:HT], start=True, stop=True)
            end(mm(b[:, HT:2 * HT], tile(K_BELOW), st[:, 0:HT], start=True, stop=True), "gcol")
            e.on("beta_wide")
            for j in range(2):
                b = begin(f"beta{j}")
                for i in range(4):
                    ins = mm(b[:, i * P:(i + 1) * P], bb[:, 4 * j + i, :], ident, start=True, stop=True)
                end(ins, f"beta{j}")
            quarter("vd", 1)
            e.on("q_normed", 2)
            e.on("k_normed", 2)
            for name, src in (("kk", kn), ("qk", qn)):
                for j in range(2):
                    b = begin(f"{name}{j}")
                    for i in range(4):
                        h, t = (4 * j + i) // TT, i % TT
                        ins = mm(b[:, i * P:(i + 1) * P], kn[:, h, t * P:(t + 1) * P], src[:, h, t * P:(t + 1) * P],
                                 start=True, stop=True)
                    end(ins, f"{name}{j}")
            quarter("vd", 2)
            for name, src in (("vtr", vc), ("ktr", kn)):
                for j in range(2):
                    transposes(f"{name}{j}", [src[:, (4 * j + i) // TT, (i % TT) * P:(i % TT + 1) * P] for i in range(4)])
            quarter("vd", 3)
            e.on("pairs")
            for j in range(2):
                transposes(f"T0{j}", [Tt[:, 4 * j + i, :] for i in range(4)])
            for level in range(LEVELS):
                e.on("lower", level + 1)
                for j in range(2):
                    if level == 0:
                        e.after(f"T0{j}")
                    else:
                        e.after(f"Dt{level - 1}.{j}")
                        e.after(f"Dn{level - 1}.{j}")
                    b = begin(f"X{level}.{j}")
                    for i in range(4):
                        ins = mm(b[:, i * P:(i + 1) * P], Ct[:, 4 * j + i, :], Tn[:, 4 * j + i, :], start=True, stop=True)
                    end(ins, f"X{level}.{j}")
                for j in range(2):
                    e.after(f"X{level}.{j}")
                    for side in ("t", "n") if level < LEVELS - 1 else ("t",):
                        b = begin(f"D{side}{level}.{j}")
                        for i in range(4 * j, 4 * j + 4):
                            l, r = (X, Tt) if side == "t" else (Tt, X)
                            ins = mm(b[:, (i % 4) * P:(i % 4 + 1) * P], l[:, i, :], r[:, i, :], start=True, stop=True)
                        end(ins, f"D{side}{level}.{j}")
            e.after(f"Dt{LEVELS - 1}.0")
            e.after(f"Dt{LEVELS - 1}.1")
            e.on("k_scaled")
            for j in range(2):
                b = begin(f"u{j}")
                for i in range(4):
                    ins = mm(b[:, i * P:(i + 1) * P], Tt[:, 4 * j + i, :], vb[:, 4 * j + i, :], start=True, stop=True)
                end(ins, f"u{j}")
                b = begin(f"w{j}")
                for i in range(4):
                    ins = mm(b[:, i * P:(i + 1) * P], kbg[:, 4 * j + i, :], Tt[:, 4 * j + i, :], start=True, stop=True)
                end(ins, f"w{j}")
            e.after("w0")
            e.after("w1")
            e.on("q_scaled")
            e.on("state")
            qs = qn.rearrange("p h (t c) -> p (h t) c", t=TT)
            def unflip(n, src, heads):
                e.on("bias_in", 16 * n)
                for h in range(0, heads, 2):
                    b = begin(f"bias{n}.{h}")
                    end(mm(b[:, :], tile(K_FLIP), src[:, h:h + 2, :], start=True, stop=True), f"bias{n}.{h}")

            unflip(1, bias[:, 4:8, :], H)
            e.after("qd.0"); e.after("qd.1"); e.after("kd.0"); e.after("kd.1")
            scores("df", 8, False, (0,))
            for c in range(NCH):
                t, lo = c // 2, (c % 2) * CH
                if c:
                    e.after(f"dS{c - 1}")
                b = begin(f"wS{c}")
                for h in range(H):
                    ins = mm(b[:, h * P:(h + 1) * P], wT[:, h * TT + t, :], S[:, h, :], start=True, stop=True)
                end(ins, f"wS{c}")
                quarter("z", c)
                e.after(f"wS{c}")
                if c < NCH - 1:
                    b = begin(f"dS{c}")
                    for h in range(H):
                        ins = mm(b[:, h * P:(h + 1) * P], kr[lo:lo + CH, h * TT + t, :], vnew[lo:lo + CH, h * TT + t, :],
                                 start=True, stop=True)
                    end(ins, f"dS{c}")
                b = begin(f"o{c}")
                for h in range(H):
                    mm(b[:, h * P:(h + 1) * P], qs[:, h * TT + t, :], S[:, h, :], start=True, stop=False)
                    ins = mm(b[:, h * P:(h + 1) * P], aT[:, h * TT + t, :], vnew[:, h * TT + t, :], start=False, stop=True)
                end(ins, f"o{c}")
                if c == 0:
                    scores("df", 8, False, (1,))

            for i in range(4):
                e.after(f"vd.{i}")
            values("df", 8, False)

            def mixed(n, w_names, name):
                for j in range(4):
                    if j % 2 == 0:
                        e.on(f"mixed{n}", j // 2 + 1)
                    transposes(f"m{n}.{j}", [hn[:, t, k * P:(k + 1) * P] for k in (2 * j, 2 * j + 1) for t in range(TT)])
                for j in range(4):
                    e.after(f"m{n}.{j}")
                tokens_wide(name, w_names, lambda: unflip(2, flip, 8))

            mixed(0, "wo", "res0.")
            norm_transposed(G_FFN)
            normed(G_FFN)
            for j in range(FT // 2):
                n = L["gu", j]
                wait_load(eng, n)
                w = slot(n).rearrange("p (k g n) -> p k g n", k=KD, g=2)
                for g in range(2):
                    b = begin(f"gu{j}.{g}")
                    for f in range(2):
                        for k in range(KD):
                            ins = mm(b[:, f * T:(f + 1) * T], w[:, k, g, f * P:(f + 1) * P], hT[:, k, :], start=k == 0, stop=k == KD - 1)
                    end(ins, f"gu{j}.{g}")
                release(n, f"gu{j}.1")
            banks = [begin(f"dn{i}") for i in range(4)]
            for j0 in range(0, FT, 4):
                n = L["dn", j0]
                wait_load(eng, n)
                w = slot(n).rearrange("p (k n) -> p k n", k=4)
                for j in range(j0, min(j0 + 4, FT)):
                    if j % 2 == 0:
                        e.after(f"gu{j // 2}.1")
                for i in range(4):
                    t, half = i // 2, i % 2
                    for j in range(j0, min(j0 + 4, FT)):
                        ins = mm(banks[i][:, :], actT[:, j, t * P:(t + 1) * P], w[:, j - j0, half * 512:(half + 1) * 512],
                                 start=j == 0, stop=j == FT - 1)
                    if j0 + 4 >= FT:
                        end(ins, f"dn{i}")
                if j0 + 4 < FT:
                    ins.then_inc(sem("down_used"), 1)
                    released[n] = (sem("down_used"), j0 // 4 + 1)
                else:
                    release(n, "dn3")

            norm_transposed(G_MIX)
            normed(G_MIX)
            features("qkg", slot8(L["qkg"]), hT, L["qkg"])
            b = begin("al")
            for k in range(KD):
                ins = mm(b[0:16, 0:T], w_al[:, k, :], hT[:, k, :], start=k == 0, stop=k == KD - 1)
            end(ins, "al")
            tokens("vg", slot8(L["vg"]), hT, L["vg"])
            e.after("al")
            e.on("gla_zeroed", 3)
            b = begin("la")
            for t in range(TT):
                ins = mm(b[:, t * T:(t + 1) * T], alT[0:17, t * P:(t + 1) * P], w_up16[:, :], start=True, stop=True)
            end(ins, "la")
            tokens("rg", slot8(L["rg"]), hT, L["rg"])
            e.on("la_ready")
            b = begin("gb")
            for f in range(2):
                for t in range(TT):
                    ins = mm(b[:, f * T + t * P:f * T + (t + 1) * P], la[:, t, f * P:(f + 1) * P], tile(K_CAUSAL), start=True, stop=True)
            end(ins, "gb")
            for name in ("qm", "km"):
                features(name, slot8(L[name]), hT, L[name])
            for name in ("zg0", "zg1", "zm0", "zm1"):
                tokens(name, slot8(L[name]), hT, L[name])
            e.on("gla_q", 4)
            e.on("gla_k")
            for j in range(2):
                b = begin(f"ga{j}")
                for i in range(4):
                    h, t = (4 * j + i) // TT, i % TT
                    ins = mm(b[:, i * P:(i + 1) * P], e2[:, h // 2, t * P:(t + 1) * P], qez[:, h // 2, h % 2, t * P:(t + 1) * P],
                             start=True, stop=True)
                end(ins, f"ga{j}")
            e.on("gla_kl")
            transposes("klt", [kl[:, f, t * P:(t + 1) * P] for t in range(TT) for f in range(2)])
            e.after("klt")
            e.after("vg.0"); e.after("vg.1")
            e.after("ga0"); e.after("ga1")
            e.on("gla_qb")
            for c in range(NCH):
                t, lo = c // 2, (c % 2) * CH
                if c < NCH - 1:
                    b = begin(f"kv{c}")
                    for f in range(2):
                        ins = mm(b[:, f * T:(f + 1) * T], klt[lo:lo + CH, t, f, :], vt[lo:lo + CH, t, f * T:(f + 1) * T], start=True, stop=True)
                    end(ins, f"kv{c}")
            for c in range(NCH):
                t = c // 2
                if c:
                    e.after(f"kv{c - 1}")
                b = begin(f"go{c}")
                for f in range(2):
                    mm(b[:, f * T:(f + 1) * T], qb[:, f, t * P:(t + 1) * P], sts[:, c, f, :], start=True, stop=False)
                    for h in (2 * f, 2 * f + 1):
                        ins = mm(b[:, h * P:(h + 1) * P], atT[:, h * TT + t, :], vt[:, t, h * P:(h + 1) * P], start=False, stop=h % 2 == 1)
                end(ins, f"go{c}")
            e.after("qm.0"); e.after("qm.1"); e.after("km.0"); e.after("km.1")
            scores("mo", 8, False)
            tokens("vm", slot8(L["vm"]), hT, L["vm"])
            e.after("vm.0"); e.after("vm.1")
            values("mo", 8, False)

            def half_transposed(name, c0):
                for j in range(2):
                    transposes(f"{name}.{j}", [hn[:, t, c0 + k * P:c0 + (k + 1) * P] for k in (2 * j, 2 * j + 1) for t in range(TT)])
                for j in range(2):
                    e.after(f"{name}.{j}")

            def half_product(name, n, src, k0):
                wait_load(eng, n)
                w = slot(n).rearrange("p (k n) -> p k n", k=4)
                for t in range(TT):
                    for i in range(2):
                        b = begin(f"{name}{i}.{t}")
                        for k in range(4):
                            ins = mm(b[:, :], src[:, k0 + k, t * P:(t + 1) * P], w[:, k, i * 512:(i + 1) * 512], start=k == 0, stop=k == 3)
                        end(ins, f"{name}{i}.{t}")
                release(n, f"{name}1.1")

            e.after("moo0"); e.after("moo1")
            for c0, k0, name in ((512, 2, "pm"), (0, 0, "pg")):
                if name == "pg":
                    e.on("mixed1")
                for j in range(2):
                    transposes(f"m1.{k0 + j}", [hn[:, t, c0 + k * P:c0 + (k + 1) * P] for k in (2 * j, 2 * j + 1) for t in range(TT)])
                for j in range(2):
                    e.after(f"m1.{k0 + j}")
                half_product(name, L[name], hT, 2 * k0)
            e.on("merged", 4)
            for j in range(4):
                transposes(f"m2.{j}", [zg[:, t, k * P:(k + 1) * P] for k in (2 * j, 2 * j + 1) for t in range(TT)])
            for j in range(4):
                e.after(f"m2.{j}")
            tokens_wide("res1.", "wo2")

            norm_transposed(G_MEM, zm)
            normed(G_MEM)
            features("ck", slot8(L["ck"]), memT, L["ck"])
            tokens("cv", slot8(L["cv"]), memT, L["cv"], tiles=(0,))
            norm_transposed(G_CROSS)
            normed(G_CROSS)
            features("cq", slot8(L["cq"]), hT, L["cq"])
            e.after("cq.0"); e.after("cq.1"); e.after("ck.0"); e.after("ck.1")
            scores("me", H, True)
            tokens("cv", slot8(L["cv"]), memT, L["cv"], tiles=(1,))
            e.after("cv.0"); e.after("cv.1")
            values("me", H, True)
            e.after("meo0"); e.after("meo1")
            half_transposed("m3", 512)
            half_product("res2.", L["co"], hT, 0)

            norm_transposed(G_MOE)
            normed(G_MOE)
            order[0] += -order[0] % 8
            b = begin("rt")
            for t in range(TT):
                for k in range(KD):
                    ins = mm(b[:, t * (NG + NE):(t + 1) * (NG + NE)], hT[:, k, t * P:(t + 1) * P], w_rt[:, k, :], start=k == 0, stop=k == KD - 1)
            end(ins, "rt")
            for bk in B_ACC:
                eng.wait_ge(emptied[bk], used[bk])
            for k in range(KD):
                for t in range(TT):
                    ins = mm(bank[B_ACC[k // 2]][:, (k % 2) * T + t * P:(k % 2) * T + (t + 1) * P], x[:, t, k * P:(k + 1) * P], ident,
                             start=k % 2 == 0 and t == 0, stop=False, skip_group_check=True)
            e.on("masked")
            b = begin("rank")
            mm(b[:, 0:NE], tile(K_BEFORE), Mk[:, 0, :], start=True, stop=True)
            mm(b[:, NE:2 * NE], ones, Mk[:, 0, :], start=True, stop=False)
            mm(b[:, NE:2 * NE], tile(K_BEFORE), Mk[:, 1, :], start=False, stop=True)
            mm(b[:, 2 * NE:3 * NE], ones, Mk[:, 0, :], start=True, stop=False)
            end(mm(b[:, 2 * NE:3 * NE], ones, Mk[:, 1, :], start=False, stop=True), "rank")

            def places(r):
                eng.wait_ge(sem("hidden"), NP * r + 1)
                for g in range(4):
                    eng.wait_ge(sem("weighted"), 4 * r + (g + 1))
                    for t in range(TT):
                        bk = PLACE[t]
                        eng.wait_ge(sem(f"placed{t}"), 4 * r + (g + 1))
                        for i in range(4):
                            ins = tr(bank[bk][:, i * P:(i + 1) * P], pw[:, g % 2, t * 512 + i * P:t * 512 + (i + 1) * P], ident)
                        ins.then_inc(sem(f"place{t}"), 1)

            def gather(r, i):
                for k in range(KD):
                    for t in range(TT):
                        rhs = pick[:, t, bass.ds(2 * i, 2), :].rearrange("p o j -> p (o j)")
                        ins = mm(bank[B_X[k // 4]][:, (k % 4) * P:(k % 4 + 1) * P], hn[:, t, k * P:(k + 1) * P], rhs,
                                 start=t == 0, stop=t == TT - 1)
                    if k % 4 == 3:
                        ins.then_inc(sem("gathered"), 1)

            def column_pair(out, lhs, weights, kk, half=0):
                for k in range(kk):
                    for s in range(2):
                        ins = mm(out[SL * s:SL * s + SL, :], lhs[:, k, SL * s:SL * s + SL], weights[s][:, k, half * 512:(half + 1) * 512],
                                 start=k == 0, stop=k == kk - 1)
                return ins

            def gate_or_up(m, r, i):
                n = NP * r + i
                if m == 0:
                    eng.wait_ge(sem("gathered_out"), 2 * (NP + 1) * r + 2 * i + 2)
                    eng.wait_ge(sem("hidden"), n + 1)
                for s in range(2):
                    eng.wait_ge(sem(f"expert_in{2 * m + s}"), 16 * n + 16)
                w = [eslot(m, s).rearrange("p (k n) -> p k n", k=KD) for s in range(2)]
                column_pair(bank[(B_G, B_U)[m]], xg, w, KD).then_inc(sem(("gate_done", "up_done")[m]), 1)

            def turn_hidden(r, i):
                eng.wait_ge(sem("h_ready"), NP * r + i + 1)
                for f in range(DE // P):
                    ins = tr(bank[B_T][:, f * P:(f + 1) * P], es[:, f * P:(f + 1) * P], ident)
                ins.then_inc(sem("turned"), 1)

            def down(r, i):
                n = NP * r + i
                eng.wait_ge(sem("gathered_out"), 2 * (NP + 1) * r + 2 * i + 4)
                eng.wait_ge(sem("hidden"), n + 2)
                for s in range(2):
                    eng.wait_ge(sem(f"expert_in{4 + s}"), 16 * n + 16)
                w = [eslot(2, s).rearrange("p (k n) -> p k n", k=DE // P) for s in range(2)]
                for half in range(2):
                    column_pair(bank[B_Y[half]], eh, w, DE // P, half).then_inc(sem("y_done"), 1)

            def scatter(r, i):
                n = NP * r + i
                eng.wait_ge(sem("y_out_a"), n + 1)
                eng.wait_ge(sem("y_out_v"), n + 1)
                for k in range(KD):
                    rhs = put[:, i, :] if isinstance(i, int) else put[:, bass.ds(i, 1), :].rearrange("p o t -> p (o t)")
                    mm(bank[B_ACC[k // 2]][:, (k % 2) * T:(k % 2 + 1) * T], ys[:, k * P:(k + 1) * P], rhs,
                       start=False, stop=False, skip_group_check=True)

            def round_(r):
                places(r)
                for t in range(TT):
                    eng.wait_ge(sem(f"placed{t}"), 4 * r + 5)
                eng.wait_ge(sem("picked"), TT * r + TT)
                eng.wait_ge(sem("y_out_a"), NP * r + 1)
                eng.wait_ge(sem("y_out_v"), NP * r + 1)
                gather(r, 0)
                with eng.Fori(0, NP) as i:
                    gate_or_up(0, r, i)
                    scatter(r, i)
                    gather(r, i + 1)
                    gate_or_up(1, r, i)
                    turn_hidden(r, i)
                    down(r, i)
                scatter(r, NP)

            for bk in range(4):
                eng.wait_ge(emptied[bk], used[bk])
            e.on("moe_zeroed", 3)
            round_(0)
            e.on("over_known")
            flag = eng.value_load(over[0:1, 0:1], min_val=0, max_val=1)
            with eng.If(flag > 0):
                with eng.Fori(1, ROUNDS) as r:
                    round_(r)
            for k in range(KD // 2):
                ins = mm(bank[B_ACC[k]][:, 0:2], ones, put[:, 0, 0:2], start=False, stop=True, skip_group_check=True)
            ins.then_inc(sem("sum_done"), 1)
            e.on("sum_out_a", 2)
            e.on("sum_out_v", 2)
            for k in range(2):
                for t in range(TT):
                    bk = B_TAIL[2 * t + k]
                    for i in range(4):
                        ins = tr(bank[bk][:, i * P:(i + 1) * P], accT[:, 4 * k + i, t * P:(t + 1) * P], ident)
                    ins.then_inc(sem("sum_back"), 1)

        @block.sync
        def _(eng):
            def small_loads(eng):
                count = [0]

                def small(dst, src):
                    eng.dma_start(dst, src).then_inc(sem("small"), 16)
                    count[0] += 1

                def row(c0, n, v):
                    small(rowv[:, c0:c0 + n], v.rearrange("(o n) -> o n", o=1).broadcast_to([P, n]))

                small(cst[:, P:], const[:, P:])
                small(w_ba[:, :, :], w_in[:, :, C_BA:C_BA + 8])
                small(relb[0:32, 0:4], a["rel_bias"])
                small(relb[0:32, 4:12], a["rel_bias_2"])
                row(R_DT, 4, a["dt_bias"][0])
                row(R_A, 4, a["a_log"][0])
                row(R_LA, 128, a["la_norm_w"][0])
                row(R_DIFF, 128, a["diff_norm_w"][0])
                row(R_GLA, 512, a["g_gla_head_2"][0].rearrange("h d -> (h d)"))
                row(R_BG, NG, a["b_router_group_2"][0])
                row(R_BE, NE, a["b_router_expert_2"][0])
                for i, name in enumerate(("lambda_q1", "lambda_q2", "lambda_k1", "lambda_k2")):
                    row(R_LAM + 64 * i, 64, a[name][0])
                small(w_al[:, :, :], w_in2[:, :, C2_A:C2_A + 16])
                small(w_up16[0:16, :], a["w_alpha_up_2"][0])
                small(w_up16[16:17, :], a["b_alpha_2"])
                small(w_rt[:, :, 0:NG], kp(a["w_router_group_2"][0]))
                small(w_rt[:, :, NG:], kp(a["w_router_expert_2"][0]))
                assert count[0] == N_SMALL, count

            xs = a["x"][0].rearrange("(t p) d -> p t d", p=P)
            for t in range(TT):
                eng.dma_start(x[:, t, :], xs[:, t, :]).then_inc(sem(f"x_in{t}"), 16)
            eng.dma_start(cst[:, 0:P], const[:, 0:P]).then_inc(sem("consts"), 16)
            eng.dma_start(rows[48:96, :], a["conv_w"][0].rearrange("i (f p) -> (i f) p", p=P)).then_inc(sem("consts"), 16)
            for i, name in enumerate(("attn_norm_w", "ffn_norm_w", "g_mix_2", "g_cross_2", "g_mem_2", "g_moe_2")):
                v = a[name] if name == "g_mem_2" else a[name][0]
                eng.dma_start(rows[i * KD:(i + 1) * KD, :], v.rearrange("(k p) -> k p", p=P)).then_inc(sem("consts"), 16)
            for n, (name, src) in enumerate(loads):
                if n == 3:
                    small_loads(eng)
                if n >= RING_A:
                    s, v = released[n - RING_A]
                    eng.wait_ge(s, v)
                dst = slot(n)
                if name == "gu":
                    w = dst.rearrange("p (k g n) -> p k g n", k=KD, g=2)
                    for g in range(2):
                        eng.dma_start(w[:, :, g, :], src[:, :, g, :]).then_inc(loaded[n % RING_A], 16)
                    continue
                k, c = src.shape[1], src.shape[2]
                eng.dma_start(dst[:, 0:k * c].rearrange("p (k n) -> p k n", k=k), src).then_inc(loaded[n % RING_A], 16)
            wg, wu, wd = (a[f"w_exp_{m}_2"][0] for m in ("gate", "up", "down"))

            def expert(m, s, at_):
                w = (wg, wu, wd)[m]
                eng.dma_start(eslot(m, s).rearrange("p (k n) -> p k n", k=w.shape[1] // P),
                              w[at_].rearrange("o (k p) n -> p (o k) n", p=P)).then_inc(sem(f"expert_in{2 * m + s}"), 16)

            for m in range(3):
                for s in range(2):
                    j = expert_slots[2 * m + s]
                    if j == RING - 1:
                        eng.wait_ge(sem("mixed0"), 2)
                    elif j < RING_A:
                        sem_, value = released[max(n for n in range(NA) if n % RING_A == j)]
                        eng.wait_ge(sem_, value)
                    else:
                        bk, k = turns[f"hT{G_MEM}.3"]
                        eng.wait_ge(filled[bk], k)
                    expert(m, s, slice(s, s + 1))

            def refill(number, n):
                for m in range(3):
                    for s in range(2):
                        eng.wait_ge(sem(("gate_done", "up_done", "y_done")[m]), 2 * n if m == 2 else n)
                        expert(m, s, bass.ds(number + s, 1))

            with eng.Fori(0, NP - 1) as i:
                refill(2 * i + 2, i + 1)
            eng.wait_ge(sem("over_known"), 1)
            flag = eng.value_load(over[0:1, 0:1], min_val=0, max_val=1)
            with eng.If(flag > 0):
                with eng.Fori(1, ROUNDS) as r:
                    with eng.Fori(0, NP) as i:
                        refill(2 * i, NP * r + i)
            for t in range(TT):
                eng.wait_ge(sem("result"), t + 1)
                eng.dma_start(out[0, t * P:(t + 1) * P, :], x[:, t, :]).then_inc(sem("out"), 16)
            eng.wait_ge(sem("out"), 16 * TT)

        @block.gpsimd
        def _(eng):
            g = nc.gpsimd
            g.memset(qz[64:128, :, 0, :], 0.0).then_inc(sem("zeroed"), 1)
            eng.wait_ge(sem("zeroed"), 1)
            g.memset(qz[0:64, :, 1, :], 0.0).then_inc(sem("zeroed"), 1)
            eng.wait_ge(sem("zeroed"), 2)
            g.memset(cvi[:, :, 0:3], 0.0).then_inc(sem("zeroed"), 1)
            eng.wait_ge(sem("zeroed"), 3)
            g.memset(relb[32:33, :], 1.0).then_inc(sem("relb_one"), 1)
            eng.wait_ge(sem("relb_one"), 1)
            g.memset(S[:, :, :], 0.0).then_inc(sem("state"), 1)
            eng.wait_ge(sem("state"), 1)
            eng.wait_ge(emptied[turns["rel"][0]], turns["rel"][1])
            eng.dma_start(rel_dram[:, :], relr[:, :]).then_inc(sem("rel_stored"), 16)
            eng.wait_ge(sem("rel_stored"), 16)

            def biases(dst, h0, n):
                src = bass.AP(tensor=rel_dram.tensor, offset=rel_dram.offset + h0 * REL, ap=[[1, P], [REL, n], [1, T]])
                eng.dma_start(dst, src).then_inc(sem("bias_in"), 16)

            biases(bias[:, 4:8, :], 0, 4)
            gain = zt.rearrange("p t d -> p (t d)")
            eng.wait_ge(sem("mixed0"), 1)
            eng.dma_start(gain, a["final_norm_w"].rearrange("(o n) -> o n", o=1).broadcast_to([P, D])).then_inc(sem("gain_row"), 16)
            eng.wait_ge(sem("mixed0"), 2)
            biases(flip, 4, 8)
            eng.wait_ge(sem("block1"), 2)
            g.memset(alT[0:32, :], 1.0).then_inc(sem("gla_zeroed"), 1)
            eng.wait_ge(sem("gla_zeroed"), 1)
            g.memset(qez[:, :, :, :], 0.0).then_inc(sem("gla_zeroed"), 1)
            eng.wait_ge(sem("gla_zeroed"), 2)
            g.memset(sts[:, :, :, :], 0.0).then_inc(sem("gla_zeroed"), 1)
            eng.wait_ge(sem("gla_zeroed"), 3)
            eng.wait_ge(sem("merged"), 4)
            eng.dma_start(zm, a["mem_2"][0].rearrange("(t p) d -> p t d", p=P)).then_inc(sem("mem_in"), 16)
            eng.wait_ge(sem("mixed1"), 1)
            eng.dma_start(gain, a["g_final_2"].rearrange("(o n) -> o n", o=1).broadcast_to([P, D])).then_inc(sem("gain_row"), 16)
            bk, k = turns["rt"]
            eng.wait_ge(filled[bk], k)
            g.memset(put[:, 0, :], 0.0).then_inc(sem("moe_zeroed"), 1)
            eng.wait_ge(sem("moe_zeroed"), 1)
            g.memset(ys, 0.0).then_inc(sem("moe_zeroed"), 1)
            eng.wait_ge(sem("moe_zeroed"), 2)
            g.memset(pick[:, :, NE:NE + 2, :], 0.0).then_inc(sem("moe_zeroed"), 1)
            eng.wait_ge(sem("moe_zeroed"), 3)
            g.memset(st[:, 504:505], 0.0).then_inc(sem("y_out_v"), 1)

        @block.scalar
        def _(eng):
            e = Engine(eng, "act_step")

            def act(out, in_, func, name=None, turn=None, **kw):
                ins = nc.scalar.activation(out, in_, func, **kw)
                if turn:
                    e.empty(ins, turn)
                else:
                    e.step(ins, name)

            def norm(n, src, junk=hn, ready=None, residual=None):
                c = 128 + 8 * n
                for t in range(TT):
                    for turn in residual(t) if residual else ():
                        e.after(turn)
                    if ready:
                        e.on(*ready(t))
                    act(junk[:, t, :], src[:, t, :], ACT.Square, None, accum_out=st[:, c + t:c + t + 1])
                    act(st[:, c + 2 + t:c + 3 + t], st[:, c + t:c + t + 1], ACT.Sqrt, f"std{n}", scale=1.0 / D, bias=st[:, 510:511])

            def gained(n, hT=hT):
                for t in range(TT):
                    b = e.filled(f"hT{n}.{2 * t}")
                    for k in range(4):
                        act(hT[:, k, t * P:(t + 1) * P], b[:, k * P:(k + 1) * P], ACT.Copy, turn=f"hT{n}.{2 * t}" if k == 3 else None,
                            scale=cols[:, n * KD + k:n * KD + k + 1])

            def copy(dst, turn, view=None, func=ACT.Copy, **kw):
                b = e.filled(turn)
                act(dst, view(b) if view else b[:, :], func, turn=turn, **kw)

            def two(b):
                return b.rearrange("p (f t) -> p f t", f=2)

            def four(b):
                return b.rearrange("p (i c) -> p i c", i=4)

            def one(b):
                return b[:, 0:256]

            def quarter(m, i):
                return m[:, i // 2, (i % 2) * 256:(i % 2 + 1) * 256]

            def queries(turn, h0):
                b = e.filled(turn)
                act(qz[0:64, h0:h0 + 2, 0, :], two(b[0:64, :]), ACT.Copy)
                act(qz[64:128, h0:h0 + 2, 1, :], two(b[64:128, :]), ACT.Copy, turn=turn)

            def exponentials(kind, maps, full, tiles=range(TT)):
                for t in tiles:
                    w = T if full else (t + 1) * P
                    c, sct = sc_cols(kind, t), sc_tile(kind, t)
                    e.on(f"{kind}_max", t + 1)
                    for m in range(maps):
                        last = m == maps - 1
                        act(sct[:, m, 0:w], sct[:, m, 0:w], ACT.Exp,
                            (f"{kind}_e" if kind == "df" else f"{kind}_p") if last else None,
                            bias=st[:, c + m:c + m + 1], accum_out=st[:, c + 16 + m:c + 17 + m])

            def turned(kind, maps, full, tiles=range(TT)):
                for t in tiles:
                    w = T if full else (t + 1) * P
                    pm = 4 if kind == "df" else maps
                    for kt in range(w // P):
                        for m0 in range(0, pm, 4):
                            if kind == "df" or (kt + m0 // 4) % 2 == 0:
                                copy(pt_of(kind)[:, kt, m0:m0 + 4, :], f"{kind}t{t}.{kt}.{m0}", four)
                    if kind == "df":
                        copy(hn[:, t, 512:1024], f"dfo{t}")

            def head_squares(o, junk, cols_):
                for h in range(H):
                    act(junk[:, h * P:(h + 1) * P], o[:, h * P:(h + 1) * P], ACT.Square, accum_out=cols_[:, h:h + 1])

            def head_std(name, c, eps=0, tiles=range(TT)):
                for t in tiles:
                    s = st[:, c + 4 * t:c + 4 * t + 4]
                    if name == "gl":
                        e.on("gl_ss", t + 1)
                    act(s, s, ACT.Sqrt, f"{name}_std", scale=1.0 / P, bias=st[:, 510 + eps:511 + eps])

            def halves(name):
                return lambda t: (f"{name}0.{t}", f"{name}1.{t}")

            e.on("eps_col", 2)
            norm(G_ATTN, x, ready=lambda t: (f"x_in{t}", 16))
            e.after("cols")
            gained(G_ATTN)
            for g, name in enumerate(("q", "k", "v")):
                for half in range(2):
                    f = 4 * g + 2 * half
                    copy(cvi[:, f:f + 2, 3:3 + T], f"{name}.{half}", two)
                e.on("conv", g + 1)
                act(cv[:, 4 * g:4 * g + 4, :], cv[:, 4 * g:4 * g + 4, :], ACT.Silu, "silu")
                if g < 2:
                    act(sqk[g][:, :, :], cv[:, 4 * g:4 * g + 4, :].rearrange("p h (t c) -> p (h t) c", t=TT), ACT.Square, "squares")
            raw = st[:, 64:80].rearrange("p (t c) -> p c t", t=TT)
            ht = lambda c: st[:, c:c + HT].rearrange("p (h t) -> p h t", t=TT)
            e.after("ba")
            act(ht(56), raw[:, 0:H, :], ACT.Exp, "exp_b", scale=-1.0)
            e.on("abs_a")
            act(st[:, 96:104], st[:, 88:96], ACT.Exp, scale=-1.0)
            act(st[:, 104:112], st[:, 96:104], ACT.Ln, "softplus", bias=1.0)
            act(st[:, 120:124], rowv[:, R_A:R_A + H], ACT.Exp, "exp_a_log")
            e.on("lam_dots")
            act(st[:, 422:424], st[:, 420:422], ACT.Exp, "lam_exp")
            for half in range(2):
                queries(f"qd.{half}", 2 * half)
            for half in range(2):
                copy(kf[:, 2 * half:2 * half + 2, :], f"kd.{half}", two)
            for i in range(4):
                v = sqk[i // 2][:, (i % 2) * 4:(i % 2) * 4 + 4, :]
                copy(v, f"ss{i}", four, ACT.Ln, bias=st[:, 510:511])
            for i in range(4):
                v = sqk[i // 2][:, (i % 2) * 4:(i % 2) * 4 + 4, :]
                act(v, v, ACT.Exp, "inv_norm", scale=-0.5)
            e.after("gcol")
            act(st[:, 32:48], st[:, 16:32], ACT.Exp, "exp_g")
            e.on("k_normed", 2)
            for j in range(2):
                b = e.filled(f"B{j}")
                act(eB[:, 4 * j:4 * j + 4, :], four(b), ACT.Exp, "exp_B")
            e.on("gdiff")
            act(dT[:, :, :], dT[:, :, :], ACT.Exp, "decay")
            for i in range(4):
                copy(quarter(vt, i), f"vd.{i}", one)
            for j in range(2):
                copy(Tn[:, 4 * j:4 * j + 4, :], f"T0{j}", four)
            for level in range(LEVELS):
                for j in range(2):
                    copy(X[:, 4 * j:4 * j + 4, :], f"X{level}.{j}", four)
            for j in range(2):
                copy(u[:, 4 * j:4 * j + 4, :], f"u{j}", four)
                copy(wT[:, 4 * j:4 * j + 4, :], f"w{j}", four)
            for c in range(NCH):
                lo = (c % 2) * CH
                if c == 0:
                    exponentials("df", 8, False, (0,))
                copy(hn[lo:lo + CH, c // 2, 0:512], f"o{c}", lambda b: b[lo:lo + CH, :])
                if c == 1:
                    exponentials("df", 8, False, (1,))
                head_squares(hn[lo:lo + CH, c // 2, 0:512], dT.rearrange("p i c -> p (i c)")[lo:lo + CH, 0:512],
                             st[lo:lo + CH, 200 + 4 * (c // 2):204 + 4 * (c // 2)])
                copy(quarter(zt, c), f"z.{c}", one, func=ACT.Silu)
            for t in range(TT):
                turned("df", 8, False, (t,))
                if t == 0:
                    head_std("la", 200)
                head_squares(hn[:, t, 512:1024], df_squares.rearrange("p i c -> p (i c)")[:, 0:512], st[:, 216 + 4 * t:220 + 4 * t])
                head_std("dh", 216, 1, (t,))
            for j in (0, 2):
                copy(hT[:, 2 * j:2 * j + 2, :], f"m0.{j}", two)
            norm(G_FFN, x, residual=halves("res0."))
            gained(G_FFN)
            for j in range(FT // 2):
                if j >= 2:
                    e.after(f"gu{j - 2}.1")
                copy(sil[:, j % 2, :, :], f"gu{j}.0", two, ACT.Silu)
            norm(6, x, residual=lambda t: (f"dn{2 * t}", f"dn{2 * t + 1}"))
            norm(G_MIX, x, ready=lambda t: ("block1", t + 1))
            gained(G_MIX)
            copy(qg, "qkg.0", two)
            copy(kg, "qkg.1", two)
            e.on("gla_zeroed", 3)
            copy(alT[0:16, :], "al", lambda b: b[0:16, 0:T])
            for t in range(TT):
                copy(vt[:, t, :], f"vg.{t}")
            flat = lambda m: m.rearrange("p a b -> p (a b)")
            e.on("abs_la")
            act(flat(e2), flat(e1), ACT.Exp, scale=-1.0)
            act(flat(e2), flat(e2), ACT.Ln, "softplus_la", bias=1.0)
            for t in range(TT):
                copy(zt[:, t, :], f"rg.{t}", func=ACT.Silu)
            copy(flat(bc), "gb")
            for half in range(2):
                queries(f"qm.{half}", 2 * half)
            for half in range(2):
                copy(kf[:, 2 * half:2 * half + 2, :], f"km.{half}", two)
            e.on("gla_diff", 2)
            act(flat(e2), flat(e1), ACT.Exp, scale=-1.0)
            act(flat(e1), flat(e1), ACT.Exp)
            act(flat(kl), flat(kl), ACT.Exp)
            act(flat(qb), flat(bc), ACT.Exp, "gla_exp")
            for z, m in (("zg", zg), ("zm", zm)):
                for i in range(2):
                    for t in range(TT):
                        copy(m[:, t, i * 512:(i + 1) * 512], f"{z}{i}.{t}", func=ACT.Sigmoid)
            copy(klt.rearrange("p t f c -> p (t f) c"), "klt", four)
            for c in range(NCH):
                lo = (c % 2) * CH
                copy(hn[lo:lo + CH, c // 2, 0:512], f"go{c}", lambda b: b[lo:lo + CH, :])
            exponentials("mo", 8, False)
            for t in range(TT):
                copy(vt[:, t, :], f"vm.{t}")
            turned("mo", 8, False)
            copy(hT[:, 4:6, :], "m1.2", two)
            head_std("gl", 232)
            copy(hT[:, 0:2, :], "m1.0", two)
            for j in (0, 2):
                copy(hT[:, 2 * j:2 * j + 2, :], f"m2.{j}", two)
            norm(G_MEM, zm, ready=lambda t: ("mem_in", 16))
            gained(G_MEM, memT)
            for half in range(2):
                copy(kf[:, 2 * half:2 * half + 2, :], f"ck.{half}", two)
            copy(vt[:, 0, :], "cv.0")
            norm(G_CROSS, x, residual=halves("res1."))
            gained(G_CROSS)
            for half in range(2):
                copy(qz[:, 2 * half:2 * half + 2, 0, :], f"cq.{half}", two)
            exponentials("me", H, True)
            copy(vt[:, 1, :], "cv.1")
            turned("me", H, True)
            copy(hT[:, 0:2, :], "m3.0", two)
            norm(G_MOE, x, residual=halves("res2."))
            gained(G_MOE)
            e.on("router_max")
            act(ro[:, 16:24], ro[:, 16:24], ACT.Exp)
            e.on("router_top")
            act(ro[:, 200:202], ro[:, 200:202], ACT.Exp, "router_exp")
            def places(r):
                for g in range(4):
                    for t in range(TT):
                        eng.wait_ge(sem(f"place{t}"), 4 * r + (g + 1))
                        nc.scalar.activation(put[:, 4 * g + 1:4 * g + 5, t * P:(t + 1) * P], four(bank[PLACE[t]]), ACT.Copy)\
                            .then_inc(sem(f"placed{t}"), 1)

            def pair(r, i):
                n = NP * r + i
                eng.wait_ge(sem("gate_done"), n + 1)
                eng.wait_ge(sem("hidden"), n + 1)
                nc.scalar.activation(es, bank[B_G][:, :], ACT.Silu).then_inc(sem("silu_done"), 1)
                eng.wait_ge(sem("turned"), n + 1)
                nc.scalar.activation(eh.rearrange("p k j -> p (k j)"), bank[B_T][:, :], ACT.Copy).then_inc(sem("hidden"), 1)
                eng.wait_ge(sem("y_done"), 2 * n + 1)
                nc.scalar.activation(ys[:, 0:512], bank[B_Y[0]][:, :], ACT.Copy).then_inc(sem("y_out_a"), 1)

            def round_(r):
                places(r)
                with eng.Fori(0, NP) as i:
                    pair(r, i)

            e.on("moe_zeroed", 3)
            for t in range(TT):
                act(st[:, 500 + t:501 + t], st[:, 510:511], ACT.Copy, f"placed{t}")
            act(st[:, 502:503], st[:, 510:511], ACT.Copy, "y_out_a")
            act(st[:, 505:506], st[:, 510:511], ACT.Copy, "hidden")
            round_(0)
            e.on("over_known")
            flag = eng.value_load(over[0:1, 0:1], min_val=0, max_val=1)
            with eng.If(flag > 0):
                with eng.Fori(1, ROUNDS) as r:
                    round_(r)
            e.on("sum_done")
            for k in (0, 2):
                act(accT[:, 2 * k:2 * k + 2, :], two(bank[B_ACC[k]]), ACT.Copy, "sum_out_a")
            for m in (0, 2):
                e.on("sum_back", m // 2 + 1)
                act(x[:, m // 2, 0:512], bank[B_TAIL[m]][:, :], ACT.Copy, "x_back_a")
            e.on("x_back_v", 2)
            norm(7, x)

        @block.vector
        def _(eng):
            e = Engine(eng, "dve_step")
            v = nc.vector

            def tt(out, in0, in1, op, name=None, turn=None):
                ins = v.tensor_tensor(out, in0, in1, op)
                e.empty(ins, turn) if turn else e.step(ins, name)

            def ts(out, in0, s1, s2, op0, op1=None, name=None, turn=None):
                ins = v.tensor_scalar(out, in0, s1, s2, op0, op1) if op1 is not None else v.tensor_scalar(out, in0, s1, None, op0)
                e.empty(ins, turn) if turn else e.step(ins, name)

            def stt(out, in0, scalar, in1, op0, op1, name=None, turn=None):
                ins = v.scalar_tensor_tensor(out=out, in0=in0, scalar=scalar, in1=in1, op0=op0, op1=op1)
                e.empty(ins, turn) if turn else e.step(ins, name)

            def copy(dst, turn, view=None):
                b = e.filled(turn)
                e.empty(v.tensor_copy(dst, view(b) if view else b[:, :]), turn)

            def two(b):
                return b.rearrange("p (f t) -> p f t", f=2)

            def four(b):
                return b.rearrange("p (i c) -> p i c", i=4)

            def wide(c, n, w):
                return st[:, c:c + n].unsqueeze(2).broadcast_to([P, n, w])

            def rep(m, n):
                return m.unsqueeze(1).broadcast_to([P, n, P])

            def wide_gain(n):
                return cols[:, n * KD + 4:n * KD + 8].unsqueeze(2).broadcast_to([P, 4, P])

            def norm_scale(n, t):
                c = 128 + 8 * n + t
                e.on(f"std{n}", t + 1)
                e.step(v.reciprocal(st[:, c + 4:c + 5], st[:, c + 2:c + 3]))
                return st[:, c + 4:c + 5]

            def norm(n, src, dst=hn, turns_=None, between=None):
                for t in range(TT):
                    if t and between:
                        between()
                    if turns_:
                        residual(turns_(t), t)
                    ts(dst[:, t, :], src[:, t, :], norm_scale(n, t), None, ALU.mult, name=f"normed{n}")

            def gained(n, hT=hT):
                for t in range(TT):
                    turn = f"hT{n}.{2 * t + 1}"
                    tt(hT[:, 4:8, t * P:(t + 1) * P], four(e.filled(turn)), wide_gain(n), ALU.mult, turn=turn)

            def logits(kind, maps, full, scale, tiles=range(TT)):
                for t in tiles:
                    nk = TT if full else t + 1
                    w = nk * P
                    c, sct = sc_cols(kind, t), sc_tile(kind, t)
                    per = 512 // w
                    for m0 in range(0, maps, per):
                        turn = f"{kind}s{t}.{m0}"
                        b = e.filled(turn).rearrange("p (m k) -> p m k", m=per)
                        if kind == "df":
                            for i in range(2):
                                stt(sct[:, m0 + i:m0 + per:2, 0:w], b[:, i::2, :], scale, bias[:, m0 // 2:(m0 + per) // 2, T - w:],
                                    ALU.mult, ALU.add, turn=turn if i else None)
                        elif kind == "mo":
                            stt(sct[:, m0:m0 + per, 0:w], b, scale, bias[:, m0:m0 + per, T - w:], ALU.mult, ALU.add, turn=turn)
                        else:
                            ts(sct[:, m0:m0 + per, :], b, scale, None, ALU.mult, turn=turn)
                    e.step(v.tensor_reduce(st[:, c:c + maps], sct[:, 0:maps, 0:w], AX_X, ALU.max))
                    ts(st[:, c:c + maps], st[:, c:c + maps], -1.0, None, ALU.mult, name=f"{kind}_max")

            def combined(t):
                c, sct = sc_cols("df", t), sc_tile("df", t)
                w, r = (t + 1) * P, c + 24
                e.on("df_e", t + 1)
                e.step(v.reciprocal(st[:, r:r + 8], st[:, c + 16:c + 24]))
                ts(st[:, r + 1:r + 8:2], st[:, r + 1:r + 8:2], st[:, 425:426], None, ALU.mult)
                for h in range(H):
                    ts(sct[:, 2 * h, 0:w], sct[:, 2 * h, 0:w], st[:, r + 2 * h:r + 2 * h + 1], None, ALU.mult)
                    stt(sct[:, 2 * h, 0:w], sct[:, 2 * h + 1, 0:w], st[:, r + 2 * h + 1:r + 2 * h + 2], sct[:, 2 * h, 0:w],
                        ALU.mult, ALU.add, name="df_p" if h == H - 1 else None)

            def attended(kind, maps, full):
                for t in range(TT):
                    nk = TT if full else t + 1
                    w = nk * P
                    c = sc_cols(kind, t)
                    e.on(f"{kind}_p", t + 1)
                    r = c + 24
                    e.step(v.reciprocal(st[:, r:r + maps], st[:, c + 16:c + 16 + maps]))
                    for kt in range(nk):
                        for m0 in range(0, maps, 4):
                            if (kt + m0 // 4) % 2:
                                copy(pT[:, kt, m0:m0 + 4, :], f"{kind}t{t}.{kt}.{m0}", four)
                    b = e.filled(f"{kind}o{t}")
                    dv = 512 // maps
                    tt(hn[:, t, 512:1024].rearrange("p (m d) -> p m d", d=dv), b.rearrange("p (m d) -> p m d", d=dv),
                       wide(r, maps, dv), ALU.mult, turn=f"{kind}o{t}")

            def head_norm(name, o, c, gain, tmp, turns_, tiles=range(TT), factor=1.0, done=None):
                for t in tiles:
                    for turn in turns_(t):
                        e.after(turn)
                    s, d = slice(c + 4 * t, c + 4 * t + 4), slice(c + 8 + 4 * t, c + 12 + 4 * t)
                    if tmp is not None:
                        sq = tmp.rearrange("p (t h) d -> p t h d", t=TT)[:, t]
                        tt(sq, o[:, t], o[:, t], ALU.mult)
                        e.step(v.tensor_reduce(st[:, s], sq, AX_X, ALU.add), f"{name}_ss")
                    e.on(f"{name}_std", t + 1)
                    e.step(v.reciprocal(st[:, d], st[:, s]))
                    if factor != 1.0:
                        ts(st[:, d], st[:, d], factor, None, ALU.mult)
                    tt(o[:, t], o[:, t], wide(c + 8 + 4 * t, 4, P), ALU.mult)
                    tt(o[:, t], o[:, t], gain, ALU.mult, name=done if t else None)

            def residual(turns_, t):
                for half, turn in enumerate(turns_):
                    b = e.filled(turn)
                    sl = x[:, t, half * 512:(half + 1) * 512]
                    tt(sl, sl, b[:, :], ALU.add, turn=turn)

            e.step(v.memset(st[:, 510:511], EPS), "eps_col")
            e.step(v.memset(st[:, 511:512], 1e-5), "eps_col")
            e.on("zeroed", 3)
            b = e.filled("cols")
            e.empty(v.tensor_copy(cols[:, :], b[:, 0:96]), "cols")
            e.on("x_in0", 16)
            e.on("x_in1", 16)
            norm(G_ATTN, x)
            gained(G_ATTN)
            for g in range(3):
                name = "qkv"[g]
                for f in range(4):
                    if f % 2 == 0:
                        e.after(f"{name}.{f // 2}")
                    F = 4 * g + f
                    tap = lambda i: cols[:, 48 + 12 * i + F:49 + 12 * i + F]
                    ts(cv[:, F, :], cvi[:, F, 0:T], tap(0), None, ALU.mult)
                    for i in range(1, 4):
                        stt(cv[:, F, :], cvi[:, F, i:i + T], tap(i), cv[:, F, :], ALU.mult, ALU.add,
                            name="conv" if i == 3 and f == 3 else None)
            b = e.filled("rel")
            e.empty(v.tensor_copy(relr[:, :], b[0:12, 0:REL]), "rel")
            b = e.filled("ba")
            e.empty(v.tensor_copy(st[:, 64:80], b[:, 0:16]), "ba")
            raw = st[:, 64:80].rearrange("p (t c) -> p c t", t=TT)
            ht = lambda c: st[:, c:c + HT].rearrange("p (h t) -> p h t", t=TT)
            per_head = lambda v_: v_.unsqueeze(2).broadcast_to([P, H, TT])
            tt(ht(80), raw[:, H:2 * H, :], per_head(rowv[:, R_DT:R_DT + H]), ALU.add)
            stt(st[:, 88:96], st[:, 80:88], -1.0, st[:, 80:88], ALU.mult, ALU.max, name="abs_a")
            tt(work[:, 13348 - 1024:13348 - 1024 + 128], rowv[:, R_LAM:R_LAM + 128], rowv[:, R_LAM + 128:R_LAM + 256], ALU.mult)
            e.step(v.tensor_reduce(st[:, 420:422], work[:, 13348 - 1024:13348 - 1024 + 128].rearrange("p (i d) -> p i d", i=2), AX_X, ALU.add), "lam_dots")
            e.on("exp_b")
            ts(st[:, 56:64], st[:, 56:64], 1.0, None, ALU.add)
            e.step(v.reciprocal(st[:, 8:16], st[:, 56:64]))
            e.on("softplus")
            stt(st[:, 112:120], st[:, 80:88], 0.0, st[:, 104:112], ALU.max, ALU.add)
            e.on("exp_a_log")
            stt(ht(0), ht(112), -1.0, per_head(st[:, 120:124]), ALU.mult, ALU.mult)
            e.step(v.tensor_copy(gb[:, :, :], wide(0, HT, P)), "g_wide")
            e.step(v.tensor_copy(bb[:, :, :], wide(8, HT, P)), "beta_wide")
            e.on("lam_exp")
            tt(st[:, 424:425], st[:, 423:424], st[:, 422:423], ALU.subtract)
            ts(st[:, 425:426], st[:, 424:425], -LAM_INIT, None, ALU.add)
            for i in range(4):
                r = sqk[i // 2][:, (i % 2) * 4:(i % 2) * 4 + 4, :]
                e.on("inv_norm", i + 1)
                q = (qn, kn)[i // 2][:, 2 * (i % 2):2 * (i % 2) + 2, :].rearrange("p h (t c) -> p (h t) c", t=TT)
                stt(q, q, P ** -0.5 if i < 2 else 1.0, r, ALU.mult, ALU.mult, name="q_normed" if i < 2 else "k_normed")
            b = e.filled("gcol")
            e.empty(v.tensor_copy(st[:, 16:32], b[:, 0:16]), "gcol")
            for j in range(2):
                e.on("exp_B", j + 1)
                b = e.filled(f"B{j}")
                tt(dT[:, 4 * j:4 * j + 4, :], four(b), wide(16 + 4 * j, 4, P), ALU.subtract, turn=f"B{j}")
            tt(dT[:, :, :], dT[:, :, :], rep(tile(K_CAUSAL), HT), ALU.mult, name="gdiff")
            e.on("decay")
            tt(dT[:, :, :], dT[:, :, :], rep(tile(K_CAUSAL), HT), ALU.mult)
            for j in range(2):
                s = slice(4 * j, 4 * j + 4)
                b = e.filled(f"beta{j}")
                tt(LT[:, s, :], four(b), dT[:, s, :], ALU.mult, turn=f"beta{j}")
            tt(LT[:, :, :], LT[:, :, :], rep(tile(K_STRICT), HT), ALU.mult)
            for j in range(2):
                s = slice(4 * j, 4 * j + 4)
                b = e.filled(f"kk{j}")
                tt(LT[:, s, :], four(b), LT[:, s, :], ALU.mult, turn=f"kk{j}")
            tt(Tt[:, :, :], LT[:, :, :], rep(tile(K_PAIR), HT), ALU.mult)
            tt(Tt[:, :, :], rep(ident, HT), Tt[:, :, :], ALU.subtract, name="pairs")
            tt(Ct[:, :, :], LT[:, :, :], rep(tile(K_LEVEL), HT), ALU.mult, name="lower")
            for j in range(2):
                s = slice(4 * j, 4 * j + 4)
                b = e.filled(f"qk{j}")
                tt(aT[:, s, :], four(b), dT[:, s, :], ALU.mult, turn=f"qk{j}")
            e.on("exp_g")
            tt(st[:, 48:56], st[:, 8:16], st[:, 32:40], ALU.mult)
            for j in range(2):
                s = slice(4 * j, 4 * j + 4)
                b = e.filled(f"vtr{j}")
                tt(vb[:, s, :], four(b), wide(8 + 4 * j, 4, P), ALU.mult, turn=f"vtr{j}")
            for j in range(2):
                s = slice(4 * j, 4 * j + 4)
                b = e.filled(f"ktr{j}")
                tt(kbg[:, s, :], four(b), wide(48 + 4 * j, 4, P), ALU.mult)
                tt(kr[:, s, :], four(b), wide(40 + 4 * j, 4, P), ALU.mult, turn=f"ktr{j}")
            q = qn.rearrange("p h (t c) -> p (h t) c", t=TT)
            tt(q, q, eB[:, :, :], ALU.mult, name="q_scaled")
            e.step(v.memset(vnew[:, :, :], 0.0), "k_scaled")
            for level in range(LEVELS):
                for j in range(2):
                    e.filled(f"X{level}.{j}")
                if level < LEVELS - 1:
                    tt(Ct[:, :, :], LT[:, :, :], rep(tile(K_LEVEL + level + 1), HT), ALU.mult, name="lower")
                for j in range(2):
                    s = slice(4 * j, 4 * j + 4)
                    sides = ("t", "n") if level < LEVELS - 1 else ("t",)
                    for side in sides:
                        e.filled(f"D{side}{level}.{j}")
                    for side in sides:
                        m = Tt if side == "t" else Tn
                        turn = f"D{side}{level}.{j}"
                        tt(m[:, s, :], m[:, s, :], four(e.filled(turn)), ALU.subtract, turn=turn)
            by_t = lambda m, t: m.rearrange("p (h t) c -> p h t c", t=TT)[:, :, t, :]
            for h in (0, 2):
                copy(bias[:, h:h + 2, :], f"bias1.{h}", two)
            logits("df", 8, False, 0.125, (0,))
            for c in range(NCH):
                if c == 1:
                    logits("df", 8, False, 0.125, (1,))
                if c == 3:
                    combined(0)
                t, lo = c // 2, (c % 2) * CH
                hi = lo + CH
                if c == 0:
                    e.after("u0")
                    e.after("u1")
                b = e.filled(f"wS{c}")
                tt(by_t(vnew, t)[lo:hi], by_t(u, t)[lo:hi], four(b)[lo:hi], ALU.subtract, turn=f"wS{c}")
                if c < NCH - 1:
                    e.filled(f"o{c}")
                    b = e.filled(f"dS{c}")
                    for h in range(H):
                        stt(S[:, h, :], S[:, h, :], eB[:, h * TT + t, hi - 1:hi], b[:, h * P:(h + 1) * P], ALU.mult, ALU.add,
                            turn=f"dS{c}" if h == H - 1 else None)
            combined(1)
            heads = lambda c0: hn[:, :, c0:c0 + 512].rearrange("p t (h d) -> p t h d", h=H)
            for t in range(TT):
                head_norm("la", heads(0), 200, rep(rowv[:, R_LA:R_LA + P], 4), None, lambda t: (f"o{2 * t}", f"o{2 * t + 1}"), (t,))
                e.after(f"z.{2 * t}")
                e.after(f"z.{2 * t + 1}")
                tt(hn[:, t, 0:512], hn[:, t, 0:512], zt[:, t, :], ALU.mult, name="mixed0" if t else None)
            head_norm("dh", heads(512), 216, rep(rowv[:, R_DIFF:R_DIFF + P], 4), None, lambda t: (f"dfo{t}",),
                      factor=1.0 - LAM_INIT, done="mixed0")
            for j in (1, 3):
                copy(hT[:, 2 * j:2 * j + 2, :], f"m0.{j}", two)
            halves = lambda name: lambda t: (f"{name}0.{t}", f"{name}1.{t}")
            norm(G_FFN, x, turns_=halves("res0."), between=lambda: [copy(bias[:, h:h + 2, :], f"bias2.{h}", two) for h in (0, 2, 4, 6)])
            gained(G_FFN)
            for j in range(FT // 2):
                e.after(f"gu{j}.0")
                b = e.filled(f"gu{j}.1")
                tt(actT[:, 2 * j:2 * j + 2, :], two(b), sil[:, j % 2, :, :], ALU.mult, turn=f"gu{j}.1")
            gain = zt.rearrange("p t d -> p (t d)")
            e.on("gain_row", 16)
            for t in range(TT):
                residual((f"dn{2 * t}", f"dn{2 * t + 1}"), t)
                stt(x[:, t, :], x[:, t, :], norm_scale(6, t), gain, ALU.mult, ALU.mult, name="block1")
            norm(G_MIX, x)
            gained(G_MIX)
            flat = lambda m: m.rearrange("p a b -> p (a b)")
            b = e.filled("la")
            e.step(v.tensor_copy(flat(la), b[:, :]))
            stt(flat(e1), flat(la), -1.0, flat(la), ALU.mult, ALU.max, name="abs_la")
            e.on("softplus_la")
            stt(flat(la), b[:, :], 0.0, flat(e2), ALU.min, ALU.subtract, turn="la")
            ts(flat(la), flat(la), 1.0 / 16.0, None, ALU.mult, name="la_ready")
            e.after("gb")
            chunks = lambda m: m.rearrange("p f (i c) -> p (f i) c", c=CH)
            col = lambda m, c: chunks(m)[:, :, c:c + 1].broadcast_to([P, 2 * NCH, CH])
            tt(chunks(e1), chunks(bc), col(bc, CH // 2 - 1), ALU.subtract, name="gla_diff")
            tt(chunks(kl), col(bc, CH - 1), chunks(bc), ALU.subtract, name="gla_diff")
            e.on("gla_exp")
            e.on("gla_zeroed", 3)
            e.step(v.tensor_copy(st[:, 432:440].unsqueeze(2), chunks(qb)[:, :, CH - 1:CH]))
            e.after("qkg.0")
            e.after("qkg.1")
            for f in range(2):
                for m in range(2):
                    r = slice(64 * m, 64 * m + 64)
                    stt(qez[r, f, m, :], qg[r, f, :], 0.125, e1[r, f, :], ALU.mult, ALU.mult, name="gla_q")
            tt(flat(e2), flat(e2), flat(kg), ALU.mult, name="gla_k")
            tt(flat(kl), flat(kl), flat(kg), ALU.mult, name="gla_kl")
            stt(flat(qb), flat(qg), 0.125, flat(qb), ALU.mult, ALU.mult, name="gla_qb")
            for j in range(2):
                b = e.filled(f"ga{j}")
                tt(atT[:, 4 * j:4 * j + 4, :], four(b), rep(tile(K_CAUSAL), 4), ALU.mult, turn=f"ga{j}")
            for c in range(NCH - 1):
                b = e.filled(f"kv{c}")
                for f in range(2):
                    for m in range(2):
                        r = slice(64 * m, 64 * m + 64)
                        sl = slice(m * P, (m + 1) * P)
                        d = 432 + f * NCH + c
                        stt(sts[r, c + 1, f, sl], sts[r, c, f, sl], st[r, d:d + 1], b[r, f * T + m * P:f * T + (m + 1) * P],
                            ALU.mult, ALU.add, turn=f"kv{c}" if f and m else None)
            logits("mo", 8, False, 0.125)
            attended("mo", 8, False)
            copy(hT[:, 6:8, :], "m1.3", two)
            for t in range(TT):
                head_norm("gl", heads(0), 232, rowv[:, R_GLA:R_GLA + 512].rearrange("p (h d) -> p h d", h=H), gnt,
                          lambda t: (f"go{2 * t}", f"go{2 * t + 1}"), (t,))
                e.after(f"rg.{t}")
                tt(hn[:, t, 0:512], hn[:, t, 0:512], zt[:, t, :], ALU.mult, name="mixed1" if t else None)
            for name, z in (("pm", zm), ("pg", zg)):
                if name == "pg":
                    copy(hT[:, 2:4, :], "m1.1", two)
                for t in range(TT):
                    for i in range(2):
                        sl = z[:, t, i * 512:(i + 1) * 512]
                        e.after(f"{name[:0]}z{name[1]}{i}.{t}")
                        tt(sl, e.filled(f"{name}{i}.{t}")[:, :], sl, ALU.mult, turn=f"{name}{i}.{t}")
                        if name == "pg":
                            tt(sl, sl, zm[:, t, i * 512:(i + 1) * 512], ALU.add, name="merged")
            for j in (1, 3):
                copy(hT[:, 2 * j:2 * j + 2, :], f"m2.{j}", two)
            norm(G_MEM, zm, zm)
            gained(G_MEM, memT)
            for t in range(TT):
                residual(halves("res1.")(t), t)
            norm(G_CROSS, x)
            gained(G_CROSS)
            logits("me", H, True, P ** -0.5)
            attended("me", H, True)
            copy(hT[:, 2:4, :], "m3.1", two)
            norm(G_MOE, x, turns_=halves("res2."))
            gained(G_MOE)
            b = e.filled("rt")
            tt(rl[:, :, :], b[:, 0:TT * (NG + NE)].rearrange("p (t n) -> p t n", t=TT),
               rowv[:, R_BG:R_BG + NG + NE].unsqueeze(1).broadcast_to([P, TT, NG + NE]), ALU.add, turn="rt")
            r3 = lambda c, n: ro[:, c:c + TT * n].rearrange("p (t n) -> p t n", t=TT)
            bcast = lambda m, n: m.unsqueeze(2).broadcast_to([P, TT, n])
            rank = lambda n: ro[:, 0:n].unsqueeze(1).broadcast_to([P, TT, n])
            ts(ro[:, 0:8], index[:, 0:8], -1.0, 100.0, ALU.mult, ALU.add)

            def first_best(values, n, top, onehot_):
                e.step(v.tensor_reduce(top, values, AX_X, ALU.max))
                tt(onehot_, values, bcast(top, n), ALU.is_ge)
                tt(onehot_, onehot_, rank(n), ALU.mult)
                e.step(v.tensor_reduce(ro[:, 8:10], onehot_, AX_X, ALU.max))
                tt(onehot_, onehot_, bcast(ro[:, 8:10], n), ALU.is_equal)

            gmax, ohg = ro[:, 10:12], r3(32, NG)
            first_best(rl[:, :, 0:NG], NG, gmax, ohg)
            tt(r3(16, NG), rl[:, :, 0:NG], bcast(gmax, NG), ALU.subtract, name="router_max")
            prod = ro[:, 512:512 + TT * NE].rearrange("p (t g n) -> p t g n", t=TT, g=NG)
            tt(prod, rl[:, :, NG:].rearrange("p t (g n) -> p t g n", g=NG), ohg.unsqueeze(3).broadcast_to([P, TT, NG, EG]), ALU.mult)
            ein = r3(64, EG)
            for t in range(TT):
                e.step(v.tensor_reduce(ein[:, t], prod[:, t].rearrange("p g n -> p n g"), AX_X, ALU.add))
            oh1, oh2, rest = r3(96, EG), r3(128, EG), r3(160, EG)
            m1, m2 = ro[:, 12:14], ro[:, 14:16]
            first_best(ein, EG, m1, oh1)
            stt(rest, oh1, MASKED, ein, ALU.mult, ALU.add)
            first_best(rest, EG, m2, oh2)
            tt(ro[:, 200:202], m2, m1, ALU.subtract, name="router_top")
            by_group = lambda m, t: m[:, t, :].rearrange("p (g n) -> p g n", g=NG)
            group = lambda t: ohg[:, t].unsqueeze(2).broadcast_to([P, NG, EG])
            within = lambda m, t: m[:, t].unsqueeze(1).broadcast_to([P, NG, EG])
            tt(rest, oh1, oh2, ALU.add)
            for t in range(TT):
                tt(by_group(Mk, t), group(t), within(rest, t), ALU.mult, name="masked" if t else None)
            e.on("router_exp")
            e.step(v.tensor_reduce(ro[:, 204:206], r3(16, NG), AX_X, ALU.add))
            ts(ro[:, 206:208], ro[:, 200:202], 1.0, None, ALU.add)
            tt(ro[:, 206:208], ro[:, 206:208], ro[:, 204:206], ALU.mult)
            e.step(v.reciprocal(ro[:, 208:210], ro[:, 206:208]))
            tt(ro[:, 210:212], ro[:, 208:210], ro[:, 200:202], ALU.mult)
            tt(oh1, oh1, bcast(ro[:, 208:210], EG), ALU.mult)
            tt(oh2, oh2, bcast(ro[:, 210:212], EG), ALU.mult)
            tt(oh1, oh1, oh2, ALU.add)
            for t in range(TT):
                tt(by_group(Wt, t), group(t), within(oh1, t), ALU.mult)
            b = e.filled("rank")
            stt(rk, b[:, 0:2 * NE].rearrange("p (t n) -> p t n", t=TT), 1.0, Mk, ALU.add, ALU.mult)
            ts(rk, rk, -1.0, None, ALU.add)
            e.step(v.tensor_reduce(ro[:, 212:213], b[:, 2 * NE:3 * NE], AX_X, ALU.max))
            ts(over[:, :], ro[:, 212:213], float(SL), None, ALU.is_gt, turn="rank")
            e.step(v.memset(st[:, 503:504], 0.0), "over_known")

            def picks(r):
                if not isinstance(r, int):
                    v.tensor_scalar(rk, rk, -float(SL), None, ALU.add).then_inc(sem("rank_shifted"), 1)
                    eng.wait_ge(sem("rank_shifted"), r)
                for t in range(TT):
                    ins = v.tensor_tensor(pick[:, t, 0:NE, :], index[:, 0:SL].unsqueeze(1).broadcast_to([P, NE, SL]),
                                          rk[:, t, :].unsqueeze(2).broadcast_to([P, NE, SL]), ALU.is_equal)
                    ins.then_inc(sem("picked"), 1)
                eng.wait_ge(sem("picked"), TT * r + TT)
                for g in range(4):
                    if g >= 2:
                        for t in range(TT):
                            eng.wait_ge(sem(f"place{t}"), 4 * r + (g - 1))
                    src = pick[:, :, 8 * g:8 * g + 8, :]
                    dst = pw[:, g % 2, :].rearrange("p (t n j) -> p t n j", t=TT, n=8)
                    w = Wt[:, :, 8 * g:8 * g + 8].unsqueeze(3).broadcast_to([P, TT, 8, SL])
                    v.tensor_tensor(dst, src, w, ALU.mult).then_inc(sem("weighted"), 1)

            def gathered(n):
                for half in range(2):
                    eng.wait_ge(sem("gathered"), 2 * n + (half + 1))
                    c = G_MOE * KD + 4 * half
                    ins = v.tensor_tensor(xg[:, 4 * half:4 * half + 4, :], four(bank[B_X[half]]),
                                          cols[:, c:c + 4].unsqueeze(2).broadcast_to([P, 4, P]), ALU.mult)
                    ins.then_inc(sem("gathered_out"), 1)

            def pair(r, i):
                n = NP * r + i
                eng.wait_ge(sem("up_done"), n + 1)
                eng.wait_ge(sem("silu_done"), n + 1)
                v.tensor_tensor(es, bank[B_U][:, :], es, ALU.mult).then_inc(sem("h_ready"), 1)
                gathered((NP + 1) * r + (i + 1))
                eng.wait_ge(sem("y_done"), 2 * n + 2)
                v.tensor_copy(ys[:, 512:1024], bank[B_Y[1]][:, :]).then_inc(sem("y_out_v"), 1)

            def round_(r):
                picks(r)
                gathered((NP + 1) * r)
                with eng.Fori(0, NP) as i:
                    pair(r, i)

            round_(0)
            e.on("over_known")
            flag = eng.value_load(over[0:1, 0:1], min_val=0, max_val=1)
            with eng.If(flag > 0):
                with eng.Fori(1, ROUNDS) as r:
                    round_(r)
            e.on("sum_done")
            for k in (1, 3):
                e.step(v.tensor_copy(accT[:, 2 * k:2 * k + 2, :], two(bank[B_ACC[k]])), "sum_out_v")
            for m in (1, 3):
                e.on("sum_back", m // 2 + 3)
                e.step(v.tensor_copy(x[:, m // 2, 512:1024], bank[B_TAIL[m]][:, :]), "x_back_v")
            e.on("x_back_a", 2)
            e.on("gain_row", 32)
            for t in range(TT):
                stt(x[:, t, :], x[:, t, :], norm_scale(7, t), gain, ALU.mult, ALU.mult, name="result")


def kernel(**inputs):
    import concourse.bacc as bacc
    from concourse.bass_utils import run_bass_kernel_spmd

    nc = bacc.Bacc("TRN2", target_bir_lowering=False, num_devices=1)
    arrays, access = {}, {}
    for name, value in inputs.items():
        value = np.ascontiguousarray(value)
        arrays[f"in_{name}"] = value
        access[name] = nc.dram_tensor(f"in_{name}", value.shape, F32, kind="ExternalInput").ap()
    const = shape_constants()
    arrays["shape_const"] = const
    const_ap = nc.dram_tensor("shape_const", const.shape, F32, kind="ExternalInput").ap()
    result = nc.dram_tensor("out", (1, T, D), F32, kind="ExternalOutput").ap()
    two_blocks(nc, access, const_ap, result)
    ran = run_bass_kernel_spmd(nc, [arrays], core_ids=[0])
    return ran.results[0]["out"]
```
